# Optimizing a Trainium2 kernel written in Bass

```python
import math
import jax
import jax.numpy as jnp
from jax import lax
import numpy as np

D_MODEL = 1024
BATCH = 1
SEQ = 2048
DEPTH = 1

CTX_LEN = 256
GRID_W = 64
D_MIX = D_MODEL
HY_WIDTH = D_MIX // 4
HY_GROUPS = 4
HY_SHORT = 3
HY_POS_DIM = 33
HY_FFN = 64
HY_FAST_DECAY = 0.3
HY_SLOW_DECAY = 1.5
HY_TARGET = 1e-2
ML_WIDTH = D_MIX // 2
ML_HEADS = 4
ML_HEAD_DIM = ML_WIDTH // ML_HEADS
ML_CONV = 4
ML_CHUNK = 128
RG_WIDTH = D_MIX - HY_WIDTH - ML_WIDTH
RG_HEADS = 4
RG_BLOCK = RG_WIDTH // RG_HEADS
RG_CONV = 4
RG_C = 8.0
D_FF = 4 * D_MODEL
N_MOD = 6
EPS = 1e-6
HY_COLS = 3 * HY_WIDTH
ML_GATE_COLS = 4 * ML_HEADS
ML_COLS = 4 * ML_WIDTH + ML_GATE_COLS
RG_COLS = 2 * RG_WIDTH
P_IN = HY_COLS + ML_COLS + RG_COLS
OFF_ML = HY_COLS
OFF_RG = HY_COLS + ML_COLS

kernel_name = 'hybrid_hyena_mlstm_rglru_dit'

def rmsnorm(x, g):
    xf = x.astype(jnp.float32)
    y = xf * lax.rsqrt(jnp.mean(xf * xf, axis=-1, keepdims=True) + EPS)
    return (y * g.astype(jnp.float32)).astype(x.dtype)

def head_rmsnorm(y, n_heads, g):
    shp = y.shape
    yf = y.astype(jnp.float32).reshape(shp[:-1] + (n_heads, shp[-1] // n_heads))
    yf = yf * lax.rsqrt(jnp.mean(yf * yf, axis=-1, keepdims=True) + EPS)
    return yf.reshape(shp) * g.astype(jnp.float32)

def dwconv(x, w):
    K = w.shape[0]
    pl = (K - 1) // 2
    return lax.conv_general_dilated(
        x, w[:, None, :].astype(x.dtype), window_strides=(1,), padding=[(pl, K - 1 - pl)],
        dimension_numbers=('NWC', 'WIO', 'NWC'), feature_group_count=x.shape[-1])

def to_col_major(a, rows):
    B, T, C = a.shape
    return a.reshape(B, rows, GRID_W, C).transpose(0, 2, 1, 3).reshape(B, T, C)

def from_col_major(a, rows):
    B, T, C = a.shape
    return a.reshape(B, GRID_W, rows, C).transpose(0, 2, 1, 3).reshape(B, T, C)

def hyena_filters(L, w1, b1, w2, b2, w3, b3, freq):
    f32 = jnp.float32
    pos = jnp.arange(L, dtype=f32)[:, None]
    t = pos / max(L - 1, 1)
    bands = (HY_POS_DIM - 1) // 2
    fr = jnp.linspace(1e-4, bands - 1, bands, dtype=f32)[None]
    ang = (2.0 * math.pi / L) * fr * pos
    feats = jnp.concatenate([t, jnp.cos(ang), -jnp.sin(ang)], axis=-1)
    fq = freq.astype(f32)
    h = jnp.sin(fq[0] * (feats @ w1.astype(f32) + b1.astype(f32)))
    h = jnp.sin(fq[1] * (h @ w2.astype(f32) + b2.astype(f32)))
    h = (h @ w3.astype(f32) + b3.astype(f32)).reshape(L, 2, HY_WIDTH)
    max_decay = math.log(HY_TARGET) / HY_FAST_DECAY
    min_decay = math.log(HY_TARGET) / HY_SLOW_DECAY
    deltas = jnp.linspace(min_decay, max_decay, HY_WIDTH, dtype=f32)
    h = h * jnp.exp(-t * jnp.abs(deltas))[:, None, :]
    h_fwd, h_bwd = h[:, 0], h[:, 1]
    return jnp.concatenate([h_fwd, jnp.zeros((1, HY_WIDTH), f32), h_bwd[:0:-1]], axis=0)

def hyena_longconv(u, filt, bias):
    L = u.shape[1]
    uf = u.astype(jnp.float32)
    U = jnp.fft.rfft(uf, n=2 * L, axis=1)
    F = jnp.fft.rfft(filt, n=2 * L, axis=0)
    y = jnp.fft.irfft(U * F[None], n=2 * L, axis=1)[:, :L]
    return y + uf * bias.astype(jnp.float32)

def hyena_group(z, p):
    L = z.shape[1]
    z = dwconv(z, p['hy_conv'])
    x0, x1, v = jnp.split(z, 3, axis=-1)
    filt = hyena_filters(L, p['hy_w1'], p['hy_b1'], p['hy_w2'], p['hy_b2'],
                         p['hy_w3'], p['hy_b3'], p['hy_freq'])
    return x0.astype(jnp.float32) * hyena_longconv(x1 * v, filt, p['hy_bias'])

def mlstm_prep(z, p):
    B, T, _ = z.shape
    f32 = jnp.float32
    qk = jax.nn.silu(dwconv(z[..., :2 * ML_WIDTH], p['ml_conv']))
    heads = lambda a: a.astype(f32).reshape(B, T, ML_HEADS, ML_HEAD_DIM).transpose(0, 2, 1, 3)
    q = heads(qk[..., :ML_WIDTH])
    k = heads(qk[..., ML_WIDTH:]) * (ML_HEAD_DIM ** -0.5)
    v = heads(z[..., 2 * ML_WIDTH:3 * ML_WIDTH])
    gates = z[..., 4 * ML_WIDTH:].astype(f32) + p['ml_gate_b'].astype(f32)
    gates = gates.reshape(B, T, 4, ML_HEADS).transpose(2, 0, 3, 1)
    return q, k, v, gates[0::2], jax.nn.log_sigmoid(gates[1::2])

def mlstm_scan(q, k, v, log_i, log_f, state, need_out):
    B, H, T, DH = q.shape
    N = T // ML_CHUNK
    ch = lambda a: a.reshape(a.shape[:2] + (N, ML_CHUNK) + a.shape[3:])
    q, k, v, li, lf = ch(q), ch(k), ch(v), ch(log_i), ch(log_f)
    b = jnp.cumsum(lf, axis=-1)
    g = b[..., -1:] - b + li
    m_loc = jnp.max(g, axis=-1)
    w = jnp.exp(g - m_loc[..., None])
    C_loc = jnp.einsum('bhnl,bhnld,bhnle->bhnde', w, v, k)
    n_loc = jnp.einsum('bhnl,bhnle->bhne', w, k)

    def step(carry, inp):
        C, n, m = carry
        b_last, ml, Cl, nl = inp
        m_new = jnp.maximum(b_last + m, ml)
        a = jnp.exp(b_last + m - m_new)
        s = jnp.exp(ml - m_new)
        C_new = a[..., None, None] * C + s[..., None, None] * Cl
        n_new = a[..., None] * n + s[..., None] * nl
        return (C_new, n_new, m_new), (C, n, m)

    mv = lambda a: jnp.moveaxis(a, 2, 0)
    final, starts = lax.scan(step, state, (mv(b[..., -1]), mv(m_loc), mv(C_loc), mv(n_loc)))
    if not need_out:
        return None, final
    C0, n0, m0 = [jnp.moveaxis(a, 0, 2) for a in starts]
    causal = jnp.tril(jnp.ones((ML_CHUNK, ML_CHUNK), dtype=bool))
    D = jnp.where(causal, b[..., :, None] - b[..., None, :] + li[..., None, :], -jnp.inf)
    inter = b + m0[..., None]
    m = jnp.maximum(inter, jnp.max(D, axis=-1))
    S = jnp.einsum('bhntd,bhnsd->bhnts', q, k) * jnp.exp(D - m[..., None])
    wi = jnp.exp(inter - m)
    num = jnp.einsum('bhnts,bhnsd->bhntd', S, v) + wi[..., None] * jnp.einsum('bhnde,bhnte->bhntd', C0, q)
    den = jnp.sum(S, axis=-1) + wi * jnp.einsum('bhne,bhnte->bhnt', n0, q)
    h = num / jnp.maximum(jnp.abs(den), jnp.exp(-m))[..., None]
    return h.reshape(B, H, T, DH), final

def mlstm_dirs(q, k, v, log_i, log_f, states, need_out):
    rev = lambda a: jnp.flip(a, axis=2)
    h_f, s_f = mlstm_scan(q, k, v, log_i[0], log_f[0], states[0], need_out)
    h_b, s_b = mlstm_scan(rev(q), rev(k), rev(v), rev(log_i[1]), rev(log_f[1]), states[1], need_out)
    h = h_f + rev(h_b) if need_out else None
    return h, (s_f, s_b)

def heads_to_tokens(h):
    B, H, T, DH = h.shape
    return h.transpose(0, 2, 1, 3).reshape(B, T, H * DH)

def rglru_prep(zx, p):
    B, T, _ = zx.shape
    f32 = jnp.float32
    xr = dwconv(zx, p['rg_conv']).astype(f32)
    pre = jnp.einsum('bthi,dghij->dgbthj', xr.reshape(B, T, RG_HEADS, RG_BLOCK),
                     p['rg_gate_w'].astype(f32)).reshape(2, 2, B, T, RG_WIDTH)
    pre = pre + p['rg_gate_b'].astype(f32)[:, :, None, None, :]
    r = jax.nn.sigmoid(pre[:, 0])
    i = jax.nn.sigmoid(pre[:, 1])
    log_a = -RG_C * r * jax.nn.softplus(-p['rg_lambda'].astype(f32))[:, None, None, :]
    a = jnp.exp(log_a)
    b = jnp.sqrt(-jnp.expm1(2.0 * log_a)) * (i * xr[None])
    return a, b

def linear_scan(a, b, h0):
    def comb(l, r):
        return l[0] * r[0], r[0] * l[1] + r[1]
    A, Hs = lax.associative_scan(comb, (a, b), axis=1)
    return A * h0[:, None] + Hs

def rglru_dirs(a, b, h0s):
    h_f = linear_scan(a[0], b[0], h0s[0])
    h_b = jnp.flip(linear_scan(jnp.flip(a[1], 1), jnp.flip(b[1], 1), h0s[1]), 1)
    return h_f + h_b, (h_f[:, -1], h_b[:, 0])

def merge_groups(y_hy, h_ml, o_pre, h_rg, gate_pre, p, dt):
    g = p['mix_norm_g']
    y_hy = head_rmsnorm(y_hy, HY_GROUPS, g[:HY_WIDTH])
    y_ml = head_rmsnorm(h_ml, ML_HEADS, g[HY_WIDTH:HY_WIDTH + ML_WIDTH]) * jax.nn.sigmoid(o_pre.astype(jnp.float32))
    y_rg = head_rmsnorm(h_rg * jax.nn.gelu(gate_pre.astype(jnp.float32)), RG_HEADS, g[HY_WIDTH + ML_WIDTH:])
    y = jnp.concatenate([y_hy, y_ml, y_rg], axis=-1).astype(dt)
    return y @ p['w_out']

def token_mixer(h_ctx, h_lat, p, rows, need_ctx_out):
    B = h_lat.shape[0]
    f32 = jnp.float32
    z_ctx = h_ctx @ p['w_in']
    z_lat = h_lat @ p['w_in']
    ml_zero = (jnp.zeros((B, ML_HEADS, ML_HEAD_DIM, ML_HEAD_DIM), f32),
               jnp.zeros((B, ML_HEADS, ML_HEAD_DIM), f32), jnp.zeros((B, ML_HEADS), f32))
    rg_zero = jnp.zeros((B, RG_WIDTH), f32)
    cq, ck, cv, cli, clf = mlstm_prep(z_ctx[..., OFF_ML:OFF_RG], p)
    hm_c, ml_states = mlstm_dirs(cq, ck, cv, cli, clf, (ml_zero, ml_zero), need_ctx_out)
    ca, cb = rglru_prep(z_ctx[..., OFF_RG:OFF_RG + RG_WIDTH], p)
    hr_c, rg_states = rglru_dirs(ca, cb, (rg_zero, rg_zero))
    y_ctx = None
    if need_ctx_out:
        y_hy_c = hyena_group(z_ctx[..., :HY_COLS], p)
        y_ctx = merge_groups(y_hy_c, heads_to_tokens(hm_c),
                             z_ctx[..., OFF_ML + 3 * ML_WIDTH:OFF_ML + 4 * ML_WIDTH],
                             hr_c, z_ctx[..., OFF_RG + RG_WIDTH:], p, h_ctx.dtype)
    y_hy = hyena_group(z_lat[..., :HY_COLS], p)
    lq, lk, lv, lli, llf = mlstm_prep(to_col_major(z_lat[..., OFF_ML:OFF_RG], rows), p)
    hm, _ = mlstm_dirs(lq, lk, lv, lli, llf, ml_states, True)
    hm = from_col_major(heads_to_tokens(hm), rows)
    la, lb = rglru_prep(z_lat[..., OFF_RG:OFF_RG + RG_WIDTH], p)
    hr, _ = rglru_dirs(la, lb, rg_states)
    y_lat = merge_groups(y_hy, hm, z_lat[..., OFF_ML + 3 * ML_WIDTH:OFF_ML + 4 * ML_WIDTH],
                         hr, z_lat[..., OFF_RG + RG_WIDTH:], p, h_lat.dtype)
    return y_ctx, y_lat

def sq_relu_mlp(h, w1, w2):
    return jnp.square(jax.nn.relu(h @ w1)) @ w2

def modulate(t, g, m, i):
    return rmsnorm(t, g) * (1.0 + m[:, :, i + 1]) + m[:, :, i]

def setup_inputs(seed: int = 0) -> dict:
    key = jax.random.key(seed)
    ks = jax.random.split(key, 32)

    def nrm(k, shape, scale):
        return jax.random.normal(k, shape, jnp.float32) * scale

    x = nrm(ks[0], (BATCH, SEQ, D_MODEL), 1.0)
    c = nrm(ks[1], (BATCH, D_MODEL), 1.0)
    ctx = nrm(ks[2], (BATCH, CTX_LEN, D_MODEL), 1.0)
    c_ctx = nrm(ks[3], (D_MODEL,), 1.0)
    ada_w = nrm(ks[4], (DEPTH, D_MODEL, N_MOD * D_MODEL), D_MODEL ** -0.5)
    ada_b = nrm(ks[5], (DEPTH, N_MOD * D_MODEL), 0.02)
    norm1_g = 1.0 + nrm(ks[6], (DEPTH, D_MODEL), 0.02)
    norm2_g = 1.0 + nrm(ks[7], (DEPTH, D_MODEL), 0.02)
    w_in = nrm(ks[8], (DEPTH, D_MODEL, P_IN), D_MODEL ** -0.5)
    hy_conv = nrm(ks[9], (DEPTH, HY_SHORT, HY_COLS), HY_SHORT ** -0.5)
    hy_w1 = nrm(ks[10], (DEPTH, HY_POS_DIM, HY_FFN), HY_POS_DIM ** -0.5)
    hy_b1 = nrm(ks[11], (DEPTH, HY_FFN), 0.02)
    hy_w2 = nrm(ks[12], (DEPTH, HY_FFN, HY_FFN), HY_FFN ** -0.5)
    hy_b2 = nrm(ks[13], (DEPTH, HY_FFN), 0.02)
    hy_w3 = nrm(ks[14], (DEPTH, HY_FFN, 2 * HY_WIDTH), HY_FFN ** -0.5)
    hy_b3 = nrm(ks[15], (DEPTH, 2 * HY_WIDTH), 0.02)
    hy_freq = 1.0 + nrm(ks[16], (DEPTH, 2, HY_FFN), 0.02)
    hy_bias = nrm(ks[17], (DEPTH, HY_WIDTH), 1.0)
    ml_conv = nrm(ks[18], (DEPTH, ML_CONV, 2 * ML_WIDTH), ML_CONV ** -0.5)
    i_bias = nrm(ks[19], (DEPTH, 2, 1, ML_HEADS), 0.1)
    f_bias = jnp.linspace(3.0, 6.0, ML_HEADS, dtype=jnp.float32) + nrm(ks[20], (DEPTH, 2, 1, ML_HEADS), 0.1)
    ml_gate_b = jnp.concatenate([i_bias, f_bias], axis=2).reshape(DEPTH, ML_GATE_COLS)
    rg_conv = nrm(ks[21], (DEPTH, RG_CONV, RG_WIDTH), RG_CONV ** -0.5)
    rg_gate_w = nrm(ks[22], (DEPTH, 2, 2, RG_HEADS, RG_BLOCK, RG_BLOCK), RG_BLOCK ** -0.5)
    rg_gate_b = nrm(ks[23], (DEPTH, 2, 2, RG_WIDTH), 0.02)
    a_c = jax.random.uniform(ks[24], (DEPTH, 2, RG_WIDTH), jnp.float32, 0.9, 0.999)
    s = a_c ** (1.0 / RG_C)
    rg_lambda = jnp.log(s) - jnp.log1p(-s)
    mix_norm_g = 1.0 + nrm(ks[25], (DEPTH, D_MIX), 0.02)
    w_out = nrm(ks[26], (DEPTH, D_MIX, D_MODEL), D_MIX ** -0.5)
    mlp_w1 = nrm(ks[27], (DEPTH, D_MODEL, D_FF), D_MODEL ** -0.5)
    mlp_w2 = nrm(ks[28], (DEPTH, D_FF, D_MODEL), D_FF ** -0.5)
    final_g = 1.0 + nrm(ks[29], (D_MODEL,), 0.02)
    return {'x': x, 'c': c, 'ctx': ctx, 'c_ctx': c_ctx, 'ada_w': ada_w, 'ada_b': ada_b,
            'norm1_g': norm1_g, 'norm2_g': norm2_g, 'w_in': w_in, 'hy_conv': hy_conv,
            'hy_w1': hy_w1, 'hy_b1': hy_b1, 'hy_w2': hy_w2, 'hy_b2': hy_b2, 'hy_w3': hy_w3,
            'hy_b3': hy_b3, 'hy_freq': hy_freq, 'hy_bias': hy_bias, 'ml_conv': ml_conv,
            'ml_gate_b': ml_gate_b, 'rg_conv': rg_conv, 'rg_gate_w': rg_gate_w,
            'rg_gate_b': rg_gate_b, 'rg_lambda': rg_lambda, 'mix_norm_g': mix_norm_g,
            'w_out': w_out, 'mlp_w1': mlp_w1, 'mlp_w2': mlp_w2, 'final_g': final_g}

def reference(x, c, ctx, c_ctx, ada_w, ada_b, norm1_g, norm2_g, w_in, hy_conv,
              hy_w1, hy_b1, hy_w2, hy_b2, hy_w3, hy_b3, hy_freq, hy_bias, ml_conv,
              ml_gate_b, rg_conv, rg_gate_w, rg_gate_b, rg_lambda, mix_norm_g,
              w_out, mlp_w1, mlp_w2, final_g):
    B, T, D = x.shape
    rows = T // GRID_W
    ctx_s = ctx
    for l in range(DEPTH):
        need_ctx = l < DEPTH - 1
        p = {'w_in': w_in[l], 'w_out': w_out[l], 'hy_conv': hy_conv[l], 'hy_w1': hy_w1[l],
             'hy_b1': hy_b1[l], 'hy_w2': hy_w2[l], 'hy_b2': hy_b2[l], 'hy_w3': hy_w3[l],
             'hy_b3': hy_b3[l], 'hy_freq': hy_freq[l], 'hy_bias': hy_bias[l],
             'ml_conv': ml_conv[l], 'ml_gate_b': ml_gate_b[l], 'rg_conv': rg_conv[l],
             'rg_gate_w': rg_gate_w[l], 'rg_gate_b': rg_gate_b[l], 'rg_lambda': rg_lambda[l],
             'mix_norm_g': mix_norm_g[l]}
        mod = (jax.nn.silu(c) @ ada_w[l] + ada_b[l]).reshape(B, 1, N_MOD, D)
        mod_c = (jax.nn.silu(c_ctx) @ ada_w[l] + ada_b[l]).reshape(1, 1, N_MOD, D)
        hx = modulate(x, norm1_g[l], mod, 0)
        hc = modulate(ctx_s, norm1_g[l], mod_c, 0)
        y_ctx, y_lat = token_mixer(hc, hx, p, rows, need_ctx)
        x = x + mod[:, :, 2] * y_lat
        x = x + mod[:, :, 5] * sq_relu_mlp(modulate(x, norm2_g[l], mod, 3), mlp_w1[l], mlp_w2[l])
        if need_ctx:
            ctx_s = ctx_s + mod_c[:, :, 2] * y_ctx
            ctx_s = ctx_s + mod_c[:, :, 5] * sq_relu_mlp(modulate(ctx_s, norm2_g[l], mod_c, 3), mlp_w1[l], mlp_w2[l])
    return rmsnorm(x, final_g)


_drawn_inputs = setup_inputs


def setup_inputs(seed=0):
    import zlib

    import numpy as np

    out = dict(_drawn_inputs(seed))
    spreads = {}
    factors = {'ctx': 5.044,
     'norm1_g': 5.871,
     'norm2_g': 3.507,
     'hy_b1': 3.945,
     'hy_freq': 8.0,
     'rg_gate_b': 27.292,
     'mix_norm_g': 6.121,
     'final_g': 8.249}
    for name, (base, spread) in spreads.items():
        noise = np.random.default_rng([zlib.crc32(name.encode()), seed]).standard_normal(out[name].shape)
        drawn = base * np.exp(spread * noise) if base else spread * noise
        out[name] = jnp.asarray(drawn.astype(out[name].dtype))
    for name, factor in factors.items():
        out[name] = (out[name] * factor).astype(out[name].dtype)
    return out
```

```python
from contextlib import ExitStack
import math

import concourse.bass as bass
from concourse import mybir
import numpy as np

F32 = mybir.dt.float32
F16 = mybir.dt.float16
BF16 = mybir.dt.bfloat16
ALU = mybir.AluOpType
ACT = mybir.ActivationFunctionType

P = 128
D = 1024
L = 2048
TC = 256
LT = L + TC
KT = D // P
NT = L // P
NTC = LT // P
BLK = 512
NB = L // BLK
GW = 64
GR = L // GW
EPS = 1e-6
HYW, MLW, RGW = 256, 512, 256
NH = 4
DH = 128
OFF_ML = 3 * HYW
OFF_RG = OFF_ML + 4 * MLW + 16
P_IN = OFF_RG + 2 * RGW
DFF = 4 * D
FFT1, FFT2 = 128, 32
WS = 1024.0
FC = 256
NFC = DFF // FC
MAGIC = 12582912.0
NEG = -1e30

COLS = {}


def _cols():
    at = 0
    for name, n in (("cc", 16), ("n1g", 8), ("n2g", 8), ("adab", 32), ("hyc", 18), ("hyb", 2), ("mlc", 32),
                    ("rgc", 8), ("rgb", 8), ("rgl", 4), ("gcm", 4), ("ffn", 4), ("gb", 1), ("negt", 32)):
        COLS[name] = (at, n)
        at += n
    return at


NCOL = _cols()


def program(nc, dr):
    ctx = ExitStack()
    with ctx:
        def sb(name, shape, dt=F32):
            return ctx.enter_context(nc.sbuf_tensor(name, shape, dt))

        def sem(name):
            return ctx.enter_context(nc.semaphore(name))

        AW = 51200
        arena = sb("arena", [P, AW])
        pb = ctx.enter_context(nc.psum_tensor("pb", [P, 8, 512], F32))
        KB = 256

        def view(kb, shape, dt=F32, off=0):
            n = 1
            for s in shape:
                n *= s
            words = n * (2 if dt in (F16, BF16) else 4) // 4
            at = int(kb * KB) + off
            assert at + words <= AW, (kb, shape)
            v = arena[:, at:at + words]
            if dt != F32:
                v = v.bitcast(dt)
            if len(shape) == 2:
                v = v.rearrange("p (a b) -> p a b", a=shape[0])
            elif len(shape) == 3:
                v = v.rearrange("p (a b c) -> p a b c", a=shape[0], b=shape[1])
            return v

        cols = sb("cols", [P, NCOL])
        ident = sb("ident", [P, P])
        identb = sb("identb", [P, P], BF16)
        maskneg = sb("maskneg", [P, 2, P], BF16)
        conv_consts = sb("conv_consts", [P, 4, P])
        dft = conv_consts[:, 0:3, :]
        gones = conv_consts[:, 3, :]
        modT = sb("modT", [P, 32, 2])
        affA = sb("affA", [P, 3, KT])
        affB = sb("affB", [P, 3, KT])
        small = sb("small", [P, 64])

        def col(name, i=0, n=1):
            return cols[:, COLS[name][0] + i:COLS[name][0] + i + n]

        hT = view(0, [KT, 2, LT], F16)
        yT = view(72, [KT, 2, L], F16)
        wst = view(188, [KT, P])
        whl = view(192, [2, 2 * KT, P], F16)
        Fsp = view(88, [2, 64, 64])

        s = {}

        def S(name):
            if name not in s:
                s[name] = sem(name)
            return s[name]

        class Chain:

            def __init__(self, eng, name):
                self.eng, self.sem, self.n = eng, S(name), 0

            def __call__(self, ins):
                self.n = self.n + 1
                ins.then_inc(self.sem, 1)
                self.eng.wait_ge(self.sem, self.n)

        ada_ring = [view(0, [KT, BLK]), view(16, [KT, BLK])]
        featsT = view(32, [L])
        h1 = view(40, [L])
        h2 = view(48, [L])
        arow = view(56, [6 * D])
        filt = view(120, [HYW, FFT2])
        X1f = view(152, [HYW, FFT2])
        X1Tf = view(120, [2, 64, 64])
        w1bd = view(80, [P])
        w2bd = view(80.5, [P])
        w3s = view(81, [HYW])
        b3bc = view(82, [HYW])
        dbc = view(83, [HYW])
        dec = [view(84, [HYW]), view(85, [HYW])]
        ftmp = [view(86, [HYW]), view(87, [HYW])]
        red = [view(184, [BLK]), view(186, [BLK]), view(188, [BLK])]
        mask_in = view(194, [2, P])
        scs = small[:, 0:16]
        sct = small[:, 16:32]
        Fring = [view(190, [4, P]), view(192, [4, P])]

        xring = [view(120 + 4 * i, [D]) for i in range(4)]
        xnrm = [view(136, [D]), view(140, [D])]
        hf = [view(144, [KT, P]), view(148, [KT, P])]
        junk = view(152, [D])
        ssq = small[:, 32:32 + NTC]
        rst = sb("rst", [P, NTC])
        mhalf = sb("mhalf", [P, 1])
        adab_row = view(40, [2, D])

        JOBS = []

        def job(name, kind, parts, lat, with_ctx):
            JOBS.append(dict(name=name, kind=kind, parts=parts, n=NT if kind == "chunk" else NB + (1 if with_ctx else 0),
                             p0=(JOBS[-1]["p0"] + JOBS[-1]["n"]) if JOBS else 0, i=len(JOBS)))

        for j in range(2):
            for i, nm in ((1, "x1"), (2, "v"), (0, "x0")):
                job(f"hy{nm}{j}", "cm", [(0, HYW * i + P * j, P)], True, False)
        for j in range(2):
            job(f"rgx{j}", "cm", [(0, OFF_RG + P * j, P)], True, True)
            job(f"rgg{j}", "cm", [(0, OFF_RG + RGW + P * j, P)], True, False)
        GO = OFF_ML + 4 * MLW
        job("gates", "cm", [(0, GO, 4), (32, GO + 8, 4), (64, GO + 4, 4), (96, GO + 12, 4)], True, True)
        for h in range(NH):
            job(f"q{h}", "cm", [(0, OFF_ML + P * h, P)], True, False)
            job(f"k{h}", "cm", [(0, OFF_ML + MLW + P * h, P)], True, True)
            job(f"v{h}", "tm", [(0, OFF_ML + 2 * MLW + P * h, P)], True, True)
            job(f"o{h}", "chunk", [(0, OFF_ML + 3 * MLW + P * h, P)], True, False)
        J = {x["name"]: x for x in JOBS}
        w_src = dr["w_in"].rearrange("(k p) n -> p k n", p=P)

        def x_tokens(t):
            return dr["x"].rearrange("(r c) d -> c r d", c=GW)[4 * t:4 * t + 4]

        def to_rows(dst, b):
            return dst.rearrange("p (r c) -> p c r", c=GW)[:, 16 * b:16 * b + 16, :]

        def cr(a):
            return a.rearrange("p (c r) -> p c r", r=GR)

        def load_w(sp, jb):
            i = jb["i"]
            if i >= 1:
                sp.wait_ge(S("w_split"), i)
            if jb["name"] == "gates":
                sp.wait_ge(S("w_clear"), 1)
            for at, c0, n in jb["parts"]:
                sp.dma_start(wst[:, :, at:at + n], w_src[:, :, c0:c0 + n]).then_inc(S("w_in"), 16)

        def w_need(i):
            return 16 * sum(len(x["parts"]) for x in JOBS[:i + 1])

        def split_hi(act, i):
            if i >= len(JOBS):
                return
            act.wait_ge(S("w_in"), w_need(i))
            if i >= 2:
                act.wait_ge(S("p_mm"), JOBS[i - 2]["p0"] + JOBS[i - 2]["n"])
            act.activation(whl[:, (i + 1) % 2, 0:KT, :], wst, ACT.Copy, scale=WS).then_inc(S("w_hi"), 1)

        def split_lo(dve, i):
            if i >= len(JOBS):
                return
            dve.wait_ge(S("w_hi"), i + 1)
            dve.scalar_tensor_tensor(whl[:, (i + 1) % 2, KT:2 * KT, :], wst, WS, whl[:, (i + 1) % 2, 0:KT, :],
                                     ALU.mult, ALU.subtract).then_inc(S("w_split"), 1)
            if i + 1 < len(JOBS) and JOBS[i + 1]["name"] == "gates":
                dve.wait_ge(S("w_split"), i + 1)
                dve.memset(wst, 0.0).then_inc(S("w_clear"), 1)

        def project(pe, jb, blocks=None):
            i = jb["i"]
            pe.wait_ge(S("w_split"), i + 1)
            after_chunks = i >= 1 and JOBS[i - 1]["kind"] == "chunk"
            for b in (range(jb["n"]) if blocks is None else blocks):
                u = jb["p0"] + b
                if jb["kind"] == "chunk" or (after_chunks and b < 2):
                    pe.wait_ge(S("p_ev"), u if jb["kind"] == "chunk" else jb["p0"])
                    if after_chunks and u % 2 == 1:
                        pe.wait_ge(S("m_ylo"), NT * (int(jb["name"][1:])))
                elif u >= 2:
                    pe.wait_ge(S("p_ev"), u - 1)
                if jb["kind"] == "cm":
                    t0, n = (BLK * b, BLK) if b < NB else (L, TC)
                    for k in range(KT):
                        for m, (ws, hs) in enumerate(((0, 0), (0, 1), (1, 0))):
                            mm = pe.matmul(pb[:, u % 2, 0:n], whl[:, (i + 1) % 2, KT * ws + k, :], hT[:, k, hs, t0:t0 + n],
                                           start=(k == 0 and m == 0), stop=(k == KT - 1 and m == 2))
                else:
                    chunk = jb["kind"] == "chunk"
                    for q in range(1 if chunk else 4 if b < NB else 2):
                        for k in range(KT):
                            for m, (ws, hs) in enumerate(((0, 0), (1, 0), (0, 1))):
                                c0 = P * b if chunk else BLK * b + P * q
                                lhs = hT[:, k, hs, c0:c0 + P]
                                mm = pe.matmul(pb[:, 0 if chunk else u % 2, P * q:P * q + P], lhs, whl[:, (i + 1) % 2, KT * ws + k, :],
                                               start=(k == 0 and m == 0), stop=(k == KT - 1 and m == 2))
                mm.then_inc(S("p_mm"), 1)

        ZPW = L + 8
        ZP = [view(120, [ZPW]), view(128.0625, [ZPW])]
        U = view(136.25, [L])
        X0 = view(144.25, [L])
        uT = view(152.25, [FFT2, P])
        X1T = view(152.25, [2, 32, 64])
        X1 = view(120, [P, FFT2])
        US = view(120, [2, 32, 64])
        Y3 = view(152.25, [32, 3, 64])
        Z = view(120, [P, FFT2])
        yt = view(152.25, [FFT2, P])
        Fr2 = [view(176.25, [4, P]), view(178.25, [4, P])]
        Gr = [view(180.25, [4, 64]), view(181.25, [4, 64])]
        tP, tQ = view(176.25, [BLK]), view(178.25, [BLK])
        CV = view(120, [L])
        SQ = view(128, [L])
        RS = view(152.25, [L])
        YF = view(160.25, [L])


        XR = view(88, [LT])
        GG = view(97, [L])
        RA = view(105, [LT])
        rgw = view(114, [2, 4, P])
        OM = view(136.25, [LT])
        TI = view(145.25, [LT])
        HS = [view(154.25, [LT]), view(163.25, [LT])]
        RT = view(172.25, [2, BLK])
        TH = view(174.25 + 2, [2, BLK])
        A2 = view(180.25, [BLK])
        ZC = view(182.25, [TC + 8])
        ZR = view(163.25, [LT])
        RORD = [[4, 0, 1, 2, 3], [4, 3, 2, 1, 0]]

        def rcols(b):
            return slice(BLK * b, BLK * b + (BLK if b < NB else TC))
        spl = sb("spl", [P, 4])
        nspl = sb("nspl", [P, 4])
        rbh = sb("rbh", [P, 8])
        sp_t = sb("sp_t", [P, 16])

        GT = view(88, [LT])
        LN = view(97, [LT])
        RR = view(106, [LT])
        LF = view(136.25, [LT])
        MM = view(145.25, [LT])
        BB = view(154.25, [LT])
        CW = view(163.25, [LT])
        R1 = view(175, [LT])
        CC = sb("CC", [P, NTC, 16])
        EM = sb("EM", [P, NTC, 8])
        M0 = sb("M0", [P, NTC])
        NL = sb("NL", [P, NTC])
        AB = sb("AB", [P, 2, NH, NTC])
        QT = view(136, [L])
        KX = view(144, [LT])
        V1 = view(153, [NTC, DH + 1])
        CB = view(162.125, [NT, DH + 1])
        ZM = view(162.125, [LT])
        ZMC = view(171.15625, [TC + 8])
        E2 = [view(171.5, [P], off=P * i) for i in range(2)]
        S2 = [[view(171.5, [P], off=P * (2 + i)) for i in range(2)], [conv_consts[:, i, :] for i in range(2)]]
        QW = [[view(171.5, [P], off=P * (4 + i)) for i in range(2)], [conv_consts[:, 2 + i, :] for i in range(2)]]
        KW = [view(171.5, [P], off=P * 6), view(170.25, [P])]
        CF = [view(184, [DH + 1], off=(DH + 1) * i) for i in range(2)]
        HM = [view(184, [P], off=258), view(170.75, [P])]
        OT = view(184, [P], off=386)
        YO = view(184, [P], off=514)
        OS = view(188, [NT, P])
        JK = view(184, [P], off=642)
        GB = view(184, [P], off=770)
        DN = sb("DN", [P, 4])
        MS = sb("MS", [P, 2, 4])
        QF = 0.25 * DH ** -0.5
        FWD = [16, 17] + list(range(NT))
        BWD = [17, 16] + list(range(NT - 1, -1, -1))
        AR = sb("AR", [P, NTC])

        def kbank(it):
            return 2 + (it % ITS) % 4 if it % ITS < 17 else 2

        ITS = 34

        x1a, x1b = view(32, [NT // 2, D]), view(136, [NT // 2, D])

        def x1(t):
            return x1a[:, t, :] if t < NT // 2 else x1b[:, t - NT // 2, :]
        hT2 = yT
        wop = view(0, [KT, 2, D], F16)
        wos = view(64, [2, D])
        m2bc = view(60, [D])
        hf2 = [view(64, [KT, P]), view(68, [KT, P])]
        xn2 = [view(184, [D]), view(188, [D])]
        junk2 = view(192, [D])
        N5, N7 = NTC, NTC + NT
        ssq2 = sb("ssq2", [P, NT])
        rst2 = sb("rst2", [P, NT])

        FT = FC // P
        AS = 1.0 / 64
        w1s, w2s = view(168, [KT, FC]), view(176, [FT, D])
        w1p = [view(8 * i, [KT, 2, FC], F16) for i in range(2)]
        w2p = [view(16 + 8 * i, [FT, 2, D], F16) for i in range(2)]
        m5bc = view(196, [D])
        act_p = [view(64 + 4 * i, [FT, 2, BLK], F16) for i in range(2)]
        act_r, act_a = view(184, [FT, BLK]), view(188, [FT, BLK])
        fgbc = view(192, [D])
        outb = [view(168 + 4 * i, [D]) for i in range(4)]
        junk_f = [view(0, [D]), view(4, [D])]
        tiny = sb("tiny", [P, 1])
        NPEEL = 2

        def norm_act(act, y, sq, rs, q):
            act.activation(sq, y, ACT.Square).then_inc(S("nm_sq"), 1)
            for b in range(NB):
                act.wait_ge(S("nm_mm"), NB * q + b + 1)
                act.activation(rs[:, BLK * b:BLK * b + BLK], pb[:, 4 + b, :], ACT.Ln, scale=1.0 / 64, bias=eps_c[:]
                               ).then_inc(S("nm_ln"), 1)
            act.wait_ge(S("nm_ln"), NB * q + NB)
            act.activation(rs, rs, ACT.Exp, scale=-0.5).then_inc(S("nm_rs"), 1)

        def norm_pe(pe, sq, q):
            pe.wait_ge(S("nm_sq"), q + 1)
            for b in range(NB):
                pe.matmul(pb[:, 4 + b, :], gones, sq[:, BLK * b:BLK * b + BLK], start=True, stop=True
                          ).then_inc(S("nm_mm"), 1)

        def norm_dve(dve, ch, y, rs, yf, q, gi):
            t = q if q < 2 else q + 4
            dve.wait_ge(S("nm_rs"), q + 1)
            ch(dve.scalar_tensor_tensor(yf, y, col("gcm", gi), rs, ALU.mult, ALU.mult))
            yc = yf.rearrange("p (r c) -> p c r", c=GW)
            ch(dve.tensor_copy(cr(yT[:, t, 0, :]), yc))
            return dve.tensor_tensor(cr(yT[:, t, 1, :]), yc, cr(yT[:, t, 0, :]), ALU.subtract)

        eps_c = sb("eps_c", [P, 1])
        block = ctx.enter_context(nc.Block())

        @block.sync
        def _(sp):
            sp.dma_start(cols[:], dr["cols"]).then_inc(S("params_in"), 16)
            sp.dma_start(ident[:], dr["ident"]).then_inc(S("params_in"), 16)
            sp.dma_start(featsT, dr["feats"]).then_inc(S("filter_in"), 16)
            sp.wait_ge(S("w_zeroed"), 1)
            for q in range(2):
                r = slice(64 * q, 64 * q + 64)
                sp.dma_start(w1bd[64 * q:64 * q + 33, 64 * q:64 * q + 64], dr["hy_w1"]).then_inc(S("filter_in"), 16)
                sp.dma_start(w2bd[r, 64 * q:64 * q + 64], dr["hy_w2"]).then_inc(S("filter_in"), 16)
                sp.dma_start(w3s[r, :], dr["hy_w3"][:, HYW * q:HYW * q + HYW]).then_inc(S("filter_in"), 16)
                sp.dma_start(b3bc[r, :], dr["hy_b3"][:, HYW * q:HYW * q + HYW].broadcast_to([64, HYW])
                             ).then_inc(S("filter_in"), 16)
            sp.dma_start(dbc[:], dr["absdelta"].broadcast_to([P, HYW])).then_inc(S("filter_in"), 16)
            sp.dma_start(dft, dr["dft"]).then_inc(S("params_in"), 16)
            sp.dma_start(gones, dr["gones"]).then_inc(S("params_in"), 16)
            sp.dma_start(mask_in, dr["maskneg"]).then_inc(S("params_in"), 16)
            for b in range(12):
                if b >= 2:
                    sp.wait_ge(S("ada_mm"), b - 1)
                sp.dma_start(ada_ring[b % 2], dr["ada_w"][:, b * BLK:(b + 1) * BLK].rearrange("(k p) n -> p k n", p=P)
                             ).then_inc(S(f"ada_in{b % 2}"), 16)
            for fj in range(FFT2 // 4):
                if fj >= 2:
                    sp.wait_ge(S("f_s1"), 4 * (fj - 1))
                sp.dma_start(Fring[fj % 2], dr["Fm"][:, 4 * fj:4 * fj + 4, :]).then_inc(S(f"F_in{fj % 2}"), 16)
            sp.wait_ge(S("f_sin"), 2 * NB)
            sp.wait_ge(S("f_mm"), 2 * NB)
            sp.dma_start(adab_row[0:1, :, :], dr["adab25"]).then_inc(S("adab_in"), 16)
            sp.wait_ge(S("ada_row"), 2)
            for i, r in enumerate((2, 5)):
                sp.dma_start(dr["mod25"][i:i + 1, :], arow[0:1, r * D:(r + 1) * D]).then_inc(S("mod25_st"), 16)
            sp.wait_ge(S("f_tr"), 16)
            sp.wait_ge(S("f_spec"), 16)
            for t in range(NTC):
                if t == 4:
                    load_w(sp, JOBS[0])
                if t >= 4:
                    sp.wait_ge(S("h_sq"), t - 3)
                    sp.wait_ge(S("h_xn"), t - 3)
                src = x_tokens(t) if t < NT else dr["ctx"][(t - NT) * P:(t - NT + 1) * P, :]
                sp.dma_start(xring[t % 4], src).then_inc(S(f"x_in{t % 4}"), 16)
            for j in range(2):
                for i in (range(1, 5) if j == 0 else range(5, 8)):
                    load_w(sp, JOBS[i])
                sp.wait_ge(S("hy_ut"), 8 * j + 1)
                if j == 1:
                    sp.wait_ge(S("hy_done"), 1)
                for q in range(8):
                    if q >= 2:
                        sp.wait_ge(S("hy_s1m"), 8 * j + q - 1)
                    sp.dma_start(Fr2[q % 2][0:64], dr["Fm"][0:64, 4 * q:4 * q + 4, :]).then_inc(S(f"Fh{q % 2}"), 16)
                for q in range(8):
                    if q >= 2:
                        sp.wait_ge(S("hy_invb"), 8 * j + q - 1)
                    sp.dma_start(Gr[q % 2], dr["Gm"][:, 4 * q:4 * q + 4, :]).then_inc(S(f"Gh{q % 2}"), 16)
            for i in range(8, 12):
                load_w(sp, JOBS[i])
                if i == 8:
                    sp.wait_ge(S("rgw_clear"), 1)
                    for j in range(2):
                        for q in range(2):
                            sp.dma_start(rgw[64 * q:64 * q + 64, j, :, 64 * q:64 * q + 64],
                                         dr["rgw"][:, 2 * j + q].rearrange("g i j -> i g j")).then_inc(S("rgw_in"), 16)
            load_w(sp, J["k0"])
            load_w(sp, J["v0"])
            for h in range(NH):
                if h == 0:
                    sp.wait_ge(S("m_one"), 1)
                else:
                    sp.wait_ge(S("m_yo"), NT * h)
                sp.dma_start(GB, dr["gml"][:, P * h:P * h + P].broadcast_to([P, P])).then_inc(S("gb_in"), 16)
                load_w(sp, J[f"o{h}"])
                if h < NH - 1:
                    for nm in "qkv":
                        load_w(sp, J[f"{nm}{h + 1}"])
            last = JOBS[-1]
            sp.wait_ge(S("p_mm"), last["p0"] + last["n"])
            sp.wait_ge(S("mod25_st"), 32)
            sp.dma_start(m2bc, dr["mod25"][0:1, :].broadcast_to([P, D])).then_inc(S("m2_in"), 16)
            for k in range(KT):
                if k >= 2:
                    sp.wait_ge(S("wo_lo"), k - 1)
                sp.dma_start(wos[:, k % 2, :], dr["w_out"][P * k:P * k + P, :]).then_inc(S(f"wo_in{k % 2}"), 16)
            for t in range(NT // 2 - 1):
                sp.dma_start(x1(t), x_tokens(t)).then_inc(S("x1_in"), 16)
            sp.wait_ge(S("wo_m"), KT)
            sp.wait_ge(S("m_ylo"), NT * NH)
            for t in range(NT // 2 - 1, NT):
                sp.dma_start(x1(t), x_tokens(t)).then_inc(S("x1_rest_in"), 16)
            w1v = dr["mlp_w1"].rearrange("(k p) f -> p k f", p=P)
            w2v = dr["mlp_w2"].rearrange("(f p) d -> p f d", p=P)
            sp.dma_start(w1s, w1v[:, :, 0:FC]).then_inc(S("g_in1"), 16)
            sp.dma_start(w2s, w2v[:, 0:FT, :]).then_inc(S("g_in2"), 16)
            sp.dma_start(m5bc, dr["mod25"][1:2, :].broadcast_to([P, D])).then_inc(S("m5_in"), 16)
            sp.wait_ge(S("h_sq"), N5 + NT)
            sp.dma_start(fgbc, dr["final_g"].broadcast_to([P, D])).then_inc(S("fg_in"), 16)
            with sp.Fori(1, NFC) as c:
                sp.wait_ge(S("g_lo"), 2 * c - 1)
                sp.dma_start(w1s, w1v[:, :, bass.ds(c * FC, FC)]).then_inc(S("g_in1"), 16)
                sp.wait_ge(S("g_lo"), 2 * c)
                sp.dma_start(w2s, w2v[:, bass.ds(c * FT, FT), :]).then_inc(S("g_in2"), 16)
            ov = dr["out"].rearrange("(r c) d -> c r d", c=GW)
            for t in range(NT):
                sp.wait_ge(S("z_out"), t + 1)
                sp.dma_start(ov[4 * t:4 * t + 4], outb[t % 4]).then_inc(S(f"out_st{t % 4}"), 16)
            for i in range(4):
                sp.wait_ge(S(f"out_st{i}"), 16 * NT // 4)

        @block.scalar
        def _(act):
            ch = Chain(act, "act_chain")
            act.wait_ge(S("params_in"), 80)
            act.wait_ge(S("eps"), 1)
            act.activation(sct, col("cc", 0, 16), ACT.Tanh, scale=0.5).then_inc(S("ada_th"), 1)
            for lay in range(2):
                for b in range(NB):
                    act.wait_ge(S("f_red"), NB * lay + b + 1)
                    dst = (h1 if lay == 0 else h2)[:, b * BLK:(b + 1) * BLK]
                    act.activation(dst, red[2], ACT.Sin).then_inc(S("f_sin"), 1)
            act.wait_ge(S("filter_in"), 16 * 10)
            for n2 in range(FFT2):
                if n2 >= 2:
                    act.wait_ge(S("f_filt"), n2 - 1)
                act.activation(dec[n2 % 2], dbc, ACT.Exp, scale=col("negt", n2)).then_inc(S("f_dec"), 1)
                if n2 % 2 == 1 and n2 // 2 < 12:
                    b = n2 // 2
                    act.wait_ge(S("ada_mm"), b + 1)
                    act.activation(arow[0:2, b * BLK:(b + 1) * BLK], pb[0:2, b % 2, :], ACT.Copy).then_inc(S("ada_ev"), 1)
            for n2 in range(FFT2):
                act.wait_ge(S("f_s1"), n2 + 1)
                act.activation(X1f[:, :, n2], pb[:, 4 + n2 % 2, 0:HYW], ACT.Copy).then_inc(S("f_x1"), 1)
            for q in range(16):
                act.wait_ge(S("f_tr"), q + 1)
                act.activation(X1Tf[:, :, 4 * q:4 * q + 4, :].rearrange("p r g k -> p g r k"),
                               pb[:, 6 + q % 2, :].rearrange("p (g r k) -> p g r k", g=4, r=2), ACT.Copy
                               ).then_inc(S("f_x1t"), 1)
            split_hi(act, 0)
            act.wait_ge(S("aff"), 1)
            for t in range(NTC + 1):
                if t < NTC:
                    act.wait_ge(S(f"x_in{t % 4}"), 16 * (t // 4 + 1))
                    if t >= 1:
                        act.wait_ge(S("h_sq"), t)
                    act.activation(junk, xring[t % 4], ACT.Square, accum_out=ssq[:, t:t + 1]).then_inc(S("h_sq"), 1)
                if t == 0:
                    continue
                u = t - 1
                act.wait_ge(S("h_tr"), u + 1)
                if u >= 2:
                    act.wait_ge(S("h_lo"), u - 1)
                w = 0 if u < NT else 1
                for k in range(KT):
                    last = act.activation(hf[u % 2][:, k, :], pb[:, 2 + 2 * (u % 2) + k // 4, P * (k % 4):P * (k % 4) + P],
                                          ACT.Identity, scale=affA[:, w, k:k + 1], bias=affB[:, w, k:k + 1])
                last.then_inc(S("h_aff"), 1)
            split_hi(act, 1)
            act.wait_ge(S("h_lo"), NTC)
            for j in range(2):
                for i in range(3):
                    zc, jb = 3 * j + i, JOBS[3 * j + i]
                    if j == 1:
                        act.wait_ge(S("hy_done"), 1)
                    if zc >= 2:
                        act.wait_ge(S("cv"), zc - 1)
                    for b in range(NB):
                        u = jb["p0"] + b
                        act.wait_ge(S("p_mm"), u + 1)
                        act.activation(to_rows(ZP[zc % 2][:, 1:1 + L], b), cr(pb[:, u % 2, :]), ACT.Copy,
                                       scale=1 / WS).then_inc(S("p_ev"), 1)
                    split_hi(act, jb["i"] + 2)
                act.wait_ge(S("cv"), 3 * j + 3)
                for q in range(9):
                    if q < 8:
                        act.wait_ge(S("hy_utm"), 8 * j + q + 1)
                        act.activation(uT[0:64, 4 * q:4 * q + 4, :], pb[0:64, 2 + q % 2, :].rearrange("p (n c) -> p n c", n=4),
                                       ACT.Copy).then_inc(S("hy_ut"), 1)
                    if q >= 1:
                        v = q - 1
                        act.wait_ge(S("hy_s1m"), 8 * j + v + 1)
                        act.activation(X1[:, :, 4 * v:4 * v + 4].rearrange("p c n -> p n c"),
                                       pb[:, 4 + v % 2, :].rearrange("p (n c) -> p n c", n=4), ACT.Copy).then_inc(S("hy_x1"), 1)
                for q in range(8):
                    act.wait_ge(S("hy_trm"), 8 * j + q + 1)
                    act.activation(X1T[:, :, 4 * q:4 * q + 4, :].rearrange("p r g k -> p g r k"),
                                   pb[:, 2 + q % 2, :].rearrange("p (g r k) -> p g r k", g=4, r=2), ACT.Copy
                                   ).then_inc(S("hy_tr"), 1)
                act.wait_ge(S("hy_y"), 4 * j + 4)
                for q in range(8):
                    act.wait_ge(S("hy_inva"), 8 * j + q + 1)
                    act.activation(Z[:, 16 * q:16 * q + 16, :].rearrange("p c n -> p (c n)"), pb[:, 2 + q % 2, :], ACT.Copy
                                   ).then_inc(S("hy_ze"), 1)
                for q in range(8):
                    act.wait_ge(S("hy_invb"), 8 * j + q + 1)
                    act.activation(yt[0:64, 4 * q:4 * q + 4, :], pb[0:64, 4 + q % 2, :].rearrange("p (n c) -> p n c", n=4),
                                   ACT.Copy).then_inc(S("hy_yt"), 1)
                act.wait_ge(S("hy_yc"), j + 1)
                norm_act(act, CV, SQ, RS, j)
            act.activation(sp_t[:, 0:4], col("rgl", 0, 4), ACT.Abs).then_inc(S("sp_a"), 1)
            act.wait_ge(S("sp_a"), 1)
            act.activation(sp_t[:, 4:8], sp_t[:, 0:4], ACT.Exp, scale=-1.0).then_inc(S("sp_a"), 1)
            for j in range(2):
                jx, jg = J[f"rgx{j}"], J[f"rgg{j}"]
                act.wait_ge(S("hy_done"), 2)
                if j == 1:
                    act.wait_ge(S("rg_done"), 1)
                for b in range(NB + 1):
                    u = jx["p0"] + b
                    act.wait_ge(S("p_mm"), u + 1)
                    dst, src = ((to_rows(ZR[:, 1:1 + L], b), cr(pb[:, u % 2, :])) if b < NB else
                                (ZC[:, 1:1 + TC], pb[:, u % 2, 0:TC]))
                    act.activation(dst, src, ACT.Copy, scale=1 / WS).then_inc(S("p_ev"), 1)
                split_hi(act, jx["i"] + 2)
                for b in range(NB):
                    u = jg["p0"] + b
                    act.wait_ge(S("p_mm"), u + 1)
                    act.activation(to_rows(GG, b), cr(pb[:, u % 2, :]), ACT.Copy, scale=1 / WS).then_inc(S("p_ev"), 1)
                split_hi(act, jg["i"] + 2)
                act.wait_ge(S("rg_cv"), 2 * j + 2)
                act.wait_ge(S("p_ev"), jg["p0"] + NB)
                act.activation(HS[1][:, 0:L], GG, ACT.Square).then_inc(S("rg_g1"), 1)
                act.wait_ge(S("rg_g2"), j + 1)
                act.activation(HS[1][:, 0:L], HS[1][:, 0:L], ACT.Tanh, scale=math.sqrt(2 / math.pi)).then_inc(S("rg_g3"), 1)
                act.wait_ge(S("rg_spl"), 1)
                for d in range(2):
                    if d or j:
                        act.wait_ge(S("rg_scan"), 2 * j + d)
                    for x in range(NB + 1):
                        v, b = 10 * j + 5 * d + x, RORD[d][x]
                        n, c = (BLK if b < NB else TC), rcols(b)
                        act.wait_ge(S("rg_mm"), v + 1)
                        if v >= 2:
                            act.wait_ge(S("rg_th"), v - 1)
                            act.wait_ge(S("rg_om"), v - 1)
                        g = 4 * j + 2 * d
                        ch(act.activation(RT[:, v % 2, 0:n], pb[:, 2 + v % 2, 0:n], ACT.Tanh, scale=0.5, bias=rbh[:, g:g + 1]))
                        act.activation(TI[:, c], pb[:, 4 + v % 2, 0:n], ACT.Tanh, scale=0.5, bias=rbh[:, g + 1:g + 2]
                                       ).then_inc(S("rg_ev"), 1)
                        e = 2 * j + d
                        act.activation(RA[:, c], RT[:, v % 2, 0:n], ACT.Exp, scale=spl[:, e:e + 1], bias=spl[:, e:e + 1]
                                       ).then_inc(S("rg_a"), 1)
                        act.activation(TH[:, v % 2, 0:n], RT[:, v % 2, 0:n], ACT.Tanh, scale=nspl[:, e:e + 1],
                                       bias=nspl[:, e:e + 1]).then_inc(S("rg_th"), 1)
                    act.wait_ge(S("rg_om"), 10 * j + 5 * d + 5)
                    act.activation(OM, OM, ACT.Sqrt).then_inc(S("rg_sq"), 1)
                act.wait_ge(S("rg_y"), j + 1)
                norm_act(act, HS[0][:, 0:L], HS[1][:, 0:L], OM[:, 0:L], 2 + j)
            act.wait_ge(S("rg_done"), 2)
            jb = J["gates"]
            for b in range(NB + 1):
                u = jb["p0"] + b
                act.wait_ge(S("p_mm"), u + 1)
                dst, src = GT[:, rcols(b)], pb[:, u % 2, 0:BLK if b < NB else TC]
                act.activation(dst, src, ACT.Identity, scale=1 / WS, bias=col("gb")).then_inc(S("p_ev"), 1)
            split_hi(act, jb["i"] + 2)
            act.wait_ge(S("p_ev"), jb["p0"] + jb["n"])
            ch(act.activation(LN, GT, ACT.Abs))
            ch(act.activation(LN, LN, ACT.Exp, scale=-1.0))
            act.activation(LN, LN, ACT.Ln, bias=1.0).then_inc(S("r_ln"), 1)
            act.wait_ge(S("r_m"), 1)
            act.activation(AR[0:64, :], AR[0:64, :], ACT.Exp).then_inc(S("r_ar"), 1)
            act.activation(LF[0:64], MM[0:64], ACT.Exp, scale=-1.0)
            act.activation(R1[64:128], LN[0:64], ACT.Exp)
            act.activation(CW[64:128], RR[0:64], ACT.Exp).then_inc(S("r_rows"), 1)
            def wo_hi(k):
                act.wait_ge(S("wo_m"), k + 1)
                act.activation(wop[:, k, 0, :], wos[:, k % 2, :], ACT.Copy, scale=WS).then_inc(S("wo_hi"), 1)

            for h in range(NH):
                jq, jk, jv, jo = (J[f"{nm}{h}"] for nm in "qkvo")
                if h == 0:
                    act.wait_ge(S("m_one"), 1)
                for b in range(NB):
                    u = jq["p0"] + b
                    act.wait_ge(S("p_mm"), u + 1)
                    act.activation(ZM[:, 1 + BLK * b:1 + BLK * b + BLK], pb[:, u % 2, :], ACT.Copy, scale=1 / WS
                                   ).then_inc(S("p_ev"), 1)
                split_hi(act, jq["i"] + 2)
                act.wait_ge(S("m_cv"), 3 * h + 1)
                act.activation(ZM[:, 0:L], QT, ACT.Tanh, scale=0.5).then_inc(S("m_th"), 1)
                act.wait_ge(S("m_silu"), 2 * h + 1)
                for b in range(NB + 1):
                    u = jk["p0"] + b
                    act.wait_ge(S("p_mm"), u + 1)
                    if b < NB:
                        dst, src = ZM[:, 1 + BLK * b:1 + BLK * b + BLK], pb[:, u % 2, :]
                    else:
                        dst, src = ZMC[:, 1:1 + TC], pb[:, u % 2, 0:TC]
                    act.activation(dst, src, ACT.Copy, scale=1 / WS).then_inc(S("p_ev"), 1)
                split_hi(act, jk["i"] + 2)
                for b in range(NB + 1):
                    u, nn = jv["p0"] + b, (4 if b < NB else 2)
                    act.wait_ge(S("p_mm"), u + 1)
                    act.activation(V1[:, 4 * b:4 * b + nn, 0:DH], pb[:, u % 2, 0:P * nn].rearrange("p (n c) -> p n c", n=nn),
                                   ACT.Copy, scale=1 / WS).then_inc(S("p_ev"), 1)
                    if b == 0:
                        act.wait_ge(S("m_cv"), 3 * h + 3)
                        act.activation(ZM, KX, ACT.Tanh, scale=0.5).then_inc(S("m_th"), 1)
                split_hi(act, jv["i"] + 2)

                def kw(it, n, g):
                    act.wait_ge(S("m_kt"), it + 1)
                    if it >= 2:
                        act.wait_ge(S("m_cl"), it - 1)
                    act.activation(KW[it % 2], pb[:, kbank(it), 0:P], ACT.Identity, scale=CC[:, n, g + h:g + h + 1]
                                   ).then_inc(S("m_kw"), 1)

                def gate(m, dst):
                    act.wait_ge(S("p_mm"), jo["p0"] + m + 1)
                    act.activation(dst, pb[:, 0, 0:P], ACT.Tanh, scale=0.5 / WS).then_inc(S("p_ev"), 1)

                for x in range(17):
                    kw(ITS * h + x, BWD[x], 12)
                    if h == NH - 1 and x < NT:
                        gate(x, OS[:, x, :])
                for y in range(2):
                    kw(ITS * h + 17 + y, FWD[y], 8)
                for n in range(NT + 3):
                    cn = NT * h + n
                    if n < NT:
                        act.wait_ge(S("m_A"), cn + 1)
                        if cn >= 1:
                            act.wait_ge(S("m_S"), cn)
                        for d in range(2):
                            ins = act.activation(E2[d], pb[:, 6 + cn % 2, P * d:P * d + P], ACT.Exp,
                                                 bias=CC[:, n, 4 * d + h:4 * d + h + 1])
                        ins.then_inc(S("m_E"), 1)
                        if n < NT - 1:
                            kw(ITS * h + 19 + n, n, 8)
                    if n >= 3:
                        m, cm = n - 3, cn - 3
                        act.wait_ge(S("m_yt"), cm + 1)
                        act.activation(yT[:, 2 + h, 0, P * m:P * m + P], pb[:, 1, 0:P], ACT.Copy
                                       ).then_inc(S("m_yhi"), 1)
                    if 2 <= n < NT + 2 and h < NH - 1:
                        if cn >= 3:
                            act.wait_ge(S("m_yo"), cn - 2)
                        gate(n - 2, OT)
                    if 1 <= n <= NT:
                        cm = cn - 1
                        act.wait_ge(S("m_hs"), cm + 1)
                        if cm >= 1:
                            act.wait_ge(S("m_sq"), cm)
                        if cm >= 2:
                            act.wait_ge(S("m_rs"), cm - 1)
                        act.activation(JK, HM[cm % 2], ACT.Square, accum_out=MS[:, cm % 2, 0:1]).then_inc(S("m_sq"), 1)
                    if h == NH - 1 and 8 <= n < 8 + KT:
                        wo_hi(n - 8)
                split_hi(act, jo["i"] + 2)
            for t in range(NT + 2):
                if t < NT:
                    act.wait_ge(S("o_x1"), t + 1)
                    if t >= 1:
                        act.wait_ge(S("h_sq"), N5 + t)
                    act.activation(junk2, x1(t), ACT.Square, accum_out=ssq2[:, t:t + 1]).then_inc(S("h_sq"), 1)
                if t >= 2:
                    u = t - 2
                    act.wait_ge(S("h_tr"), N5 + u + 1)
                    if u >= 2:
                        act.wait_ge(S("h_lo"), N5 + u - 1)
                    for k in range(KT):
                        ins = act.activation(hf2[u % 2][:, k, :], pb[:, 4 + 2 * (u % 2) + k // 4, P * (k % 4):P * (k % 4) + P],
                                             ACT.Identity, scale=affA[:, 2, k:k + 1], bias=affB[:, 2, k:k + 1])
                    ins.then_inc(S("h_aff"), 1)

            def mlp_hi(c, sl):
                act.wait_ge(S("g_in1"), 16 * c + 16)
                act.activation(w1p[sl][:, :, 0, :], w1s, ACT.Copy, scale=WS).then_inc(S("g_hi"), 1)
                act.wait_ge(S("g_m5"), c + 1)
                act.activation(w2p[sl][:, :, 0, :], w2s, ACT.Copy, scale=WS).then_inc(S("g_hi"), 1)

            act.wait_ge(S("o_mm"), NT)
            mlp_hi(0, 0)
            act.wait_ge(S("h_lo"), N5 + NT)

            def act_units(it, last=False):
                for i in range(8):
                    c, tb = 2 * it + i // 4, i % 4
                    for f in range(FT):
                        n = (c * 4 + tb) * FT + f
                        act.wait_ge(S("g_mm1"), n + 1)
                        act.wait_ge(S("a_lo"), n + 1)
                        act.activation(act_r[:, f, :], pb[:, 2 * (tb % 2) + f, :], ACT.Relu, scale=math.sqrt(AS) / WS
                                       ).then_inc(S("a_r"), 1)
                        act.wait_ge(S("a_r"), n + 1)
                        act.activation(act_p[tb % 2][:, f, 0, :], act_r[:, f, :], ACT.Square).then_inc(S("a_hi"), 1)
                    if tb == 1 and not (last and i // 4 == 1):
                        mlp_hi(c + 1, (i // 4 + 1) % 2)
                    if last and i >= 6:
                        final_sq(tb - 2)

            def final_sq(tb):
                act.wait_ge(S("acc"), 4 + 8 * (4 * (NFC - 1) + tb + 1))
                for t in range(4 * tb, 4 * tb + 4):
                    if t >= 1:
                        act.wait_ge(S("h_sq"), N7 + t)
                    act.activation(junk_f[t % 2], x1(t), ACT.Square, accum_out=ssq2[:, t:t + 1]).then_inc(S("h_sq"), 1)

            with act.Fori(0, (NFC - NPEEL) // 2) as it:
                act_units(it)
            act_units((NFC - NPEEL) // 2, last=True)
            final_sq(2)
            final_sq(3)

        @block.gpsimd
        def _(pool):
            pool.memset(view(80, [256 + 256]), 0.0).then_inc(S("w_zeroed"), 1)
            pool.memset(eps_c[:], EPS).then_inc(S("eps"), 1)
            for n2 in range(FFT2):
                pool.wait_ge(S("f_raw"), n2 + 1)
                pool.wait_ge(S("f_dec"), n2 + 1)
                pool.tensor_tensor(filt[:, :, n2], ftmp[n2 % 2], dec[n2 % 2], ALU.mult).then_inc(S("f_filt"), 1)
            pool.memset(mhalf[:], -0.5).then_inc(S("mhalf"), 1)
            pool.wait_ge(S("mhalf"), 1)
            for t in range(NTC):
                pool.wait_ge(S("h_ms"), t + 1)
                pool.tensor_tensor(rst[:, t:t + 1], ssq[:, t:t + 1], mhalf[:], ALU.pow).then_inc(S("h_rs"), 1)
            pool.wait_ge(S("hy_y"), 8)
            pool.memset(view(114, [4 * KB]), 0.0).then_inc(S("rgw_clear"), 1)
            for cn in range(NT * NH):
                pool.wait_ge(S("m_ms"), cn + 1)
                if cn >= 2:
                    pool.wait_ge(S("m_yo"), cn - 1)
                pool.tensor_tensor(MS[:, cn % 2, 2:3], MS[:, cn % 2, 1:2], mhalf[:], ALU.pow).then_inc(S("m_rs"), 1)
                k = cn - NT * (NH - 1) - 4
                if 0 <= k < KT:
                    if k == 0:
                        pool.wait_ge(S("m2_in"), 16)
                    pool.wait_ge(S(f"wo_in{k % 2}"), 16 * (k // 2 + 1))
                    pool.tensor_tensor(wos[:, k % 2, :], wos[:, k % 2, :], m2bc, ALU.mult).then_inc(S("wo_m"), 1)
            for t in range(NT):
                pool.wait_ge(S("h_ms"), N5 + t + 1)
                pool.tensor_tensor(rst2[:, t:t + 1], ssq2[:, t:t + 1], mhalf[:], ALU.pow).then_inc(S("h_rs"), 1)

            def mlp_gate(c):
                pool.wait_ge(S("g_in2"), 16 * c + 16)
                for f in range(FT):
                    ins = pool.tensor_tensor(w2s[:, f, :], w2s[:, f, :], m5bc, ALU.mult)
                ins.then_inc(S("g_m5"), 1)

            pool.wait_ge(S("m5_in"), 16)
            mlp_gate(0)

            def pool_units(it, last=False):
                for i in range(8):
                    c, tb = 2 * it + i // 4, i % 4
                    for f in range(FT):
                        n = (c * 4 + tb) * FT + f
                        pool.wait_ge(S("a_r"), n + 1)
                        pool.tensor_tensor(act_a[:, f, :], act_r[:, f, :], act_r[:, f, :], ALU.mult).then_inc(S("a_sq"), 1)
                    if tb == 0 and not (last and i // 4 == 1):
                        mlp_gate(c + 1)
                    if last and i >= 7:
                        final_rs(tb - 3)

            def final_rs(tb):
                pool.wait_ge(S("h_ms"), N7 + tb + 1)
                pool.tensor_tensor(rst2[:, 4 * tb:4 * tb + 4], ssq2[:, 4 * tb:4 * tb + 4],
                                   mhalf[:].broadcast_to([P, 4]), ALU.pow).then_inc(S("h_rs"), 1)

            with pool.Fori(0, (NFC - NPEEL) // 2) as it:
                pool_units(it)
            pool_units((NFC - NPEEL) // 2, last=True)
            for tb in range(1, NB):
                final_rs(tb)

        @block.vector
        def _(dve):
            ch = Chain(dve, "dve_chain")
            dve.wait_ge(S("params_in"), 80)
            ch(dve.tensor_copy(identb[:], ident[:]))
            ch(dve.tensor_copy(maskneg[:], mask_in))
            dve.wait_ge(S("ada_th"), 1)
            ch(dve.scalar_tensor_tensor(scs, sct, 1.0, col("cc", 0, 16), ALU.add, ALU.mult))
            dve.tensor_scalar(scs, scs, 0.5, None, ALU.mult).then_inc(S("ada_c"), 1)
            for lay in range(2):
                for b in range(NB):
                    dve.wait_ge(S("f_mm"), NB * lay + b + 1)
                    arg, kk = red[0], red[1]
                    if NB * lay + b >= 1:
                        dve.wait_ge(S("f_red"), NB * lay + b)
                    ch(dve.tensor_scalar(arg, pb[:, 4 + b % 2, :], col("ffn", 2 * lay), col("ffn", 2 * lay + 1),
                                         ALU.add, ALU.mult))
                    ch(dve.tensor_scalar(kk, arg, 1.0 / (2 * math.pi), MAGIC, ALU.mult, ALU.add))
                    ch(dve.tensor_scalar(kk, kk, MAGIC, None, ALU.subtract))
                    for part in (6.28125, 0.0019350051879882812, 3.0199159819567e-07):
                        ch(dve.scalar_tensor_tensor(arg, kk, -part, arg, ALU.mult, ALU.add))
                    if NB * lay + b >= 1:
                        dve.wait_ge(S("f_sin"), NB * lay + b)
                    dve.tensor_scalar(red[2], arg, 3.1415925, -3.1415925, ALU.min, ALU.max).then_inc(S("f_red"), 1)
            for n2 in range(FFT2):
                dve.wait_ge(S("f_h3"), n2 + 1)
                if n2 >= 2:
                    dve.wait_ge(S("f_filt"), n2 - 1)
                dve.tensor_tensor(ftmp[n2 % 2], pb[:, 6 + n2 % 2, 0:HYW], b3bc, ALU.add).then_inc(S("f_raw"), 1)
            for q in range(16):
                dve.wait_ge(S("f_s2"), q + 1)
                dve.tensor_copy(Fsp[:, q % 2, 8 * (q // 2):8 * (q // 2) + 8, :],
                                pb[:, 2 + q % 2, :].rearrange("p (g k) -> p g k", g=8)).then_inc(S("f_spec"), 1)
            dve.wait_ge(S("ada_tr"), 1)
            ch(dve.tensor_copy(modT[:], pb[:, 7, 0:64].rearrange("p (a b) -> p a b", b=2)))
            mb = cols[:, COLS["adab"][0]:COLS["adab"][0] + 32].rearrange("p (a b) -> p a b", b=1)
            dve.tensor_tensor(modT[:], modT[:], mb.broadcast_to([P, 32, 2]), ALU.add).then_inc(S("adaT"), 1)
            dve.wait_ge(S("adaT"), 1)
            for w, (g, sc, sh, r) in enumerate((("n1g", 8, 0, 0), ("n1g", 8, 0, 1), ("n2g", 24, 16, 0))):
                ch(dve.scalar_tensor_tensor(affA[:, w, :], modT[:, sc:sc + KT, r], 1.0, col(g, 0, KT), ALU.add, ALU.mult))
                ch(dve.tensor_copy(affB[:, w, :], modT[:, sh:sh + KT, r]))
            dve.memset(rst[:], 0.0).then_inc(S("aff"), 1)
            dve.wait_ge(S("adab_in"), 16)
            for i, r in enumerate((2, 5)):
                a = arow[0:1, r * D:(r + 1) * D]
                dve.tensor_tensor(a, a, adab_row[0:1, i, :], ALU.add).then_inc(S("ada_row"), 1)
            dve.wait_ge(S("mod25_st"), 32)
            for t in range(NTC + 2):
                if t < NTC:
                    dve.wait_ge(S("h_sq"), t + 1)
                    dve.tensor_scalar(ssq[:, t:t + 1], ssq[:, t:t + 1], 1.0 / D, EPS, ALU.mult, ALU.add).then_inc(S("h_ms"), 1)
                if 1 <= t <= NTC:
                    u = t - 1
                    dve.wait_ge(S("h_rs"), u + 1)
                    if u >= 2:
                        dve.wait_ge(S("h_tr"), u - 1)
                    dve.tensor_scalar(xnrm[u % 2], xring[u % 4], rst[:, u:u + 1], None, ALU.mult).then_inc(S("h_xn"), 1)
                if t >= 2:
                    u = t - 2
                    dve.wait_ge(S("h_aff"), u + 1)
                    c = slice(P * u, P * u + P)
                    ch(dve.tensor_copy(hT[:, :, 0, c], hf[u % 2]))
                    dve.tensor_tensor(hT[:, :, 1, c], hf[u % 2], hT[:, :, 0, c], ALU.subtract).then_inc(S("h_lo"), 1)
                if t == 8:
                    split_lo(dve, 0)
            dve.wait_ge(S("h_lo"), NTC)
            split_lo(dve, 1)

            def conv(zc, jb, dst, taps, wc, n=L, z=None):
                zz = ZP[zc % 2] if z is None else z
                ch(dve.memset(zz[:, 0:1], 0.0))
                ch(dve.memset(zz[:, 1 + n:3 + n], 0.0))
                ch(dve.tensor_scalar(dst, zz[:, 0:n], wc[:, 0:1], None, ALU.mult))
                for k in range(1, taps):
                    ins = dve.scalar_tensor_tensor(dst, zz[:, k:k + n], wc[:, k:k + 1], dst, ALU.mult, ALU.add)
                    if k < taps - 1:
                        ch(ins)
                return ins

            for j in range(2):
                for i, (dst, wt) in enumerate(((U, 2 + j), (X0, 4 + j), (X0, j))):
                    zc, jb = 3 * j + i, JOBS[3 * j + i]
                    dve.wait_ge(S("p_ev"), jb["p0"] + jb["n"])
                    conv(zc, jb, dst, 3, col("hyc", 3 * wt, 3)).then_inc(S("cv"), 1)
                    dve.wait_ge(S("cv"), zc + 1)
                    if i == 1:
                        dve.tensor_tensor(U, U, X0, ALU.mult).then_inc(S("u_ready"), 1)
                        dve.wait_ge(S("u_ready"), j + 1)
                    split_lo(dve, jb["i"] + 2)
                for q in range(8):
                    dve.wait_ge(S("hy_s2m"), 8 * j + q + 1)
                    dve.tensor_copy(US[:, q % 2, 8 * (q // 2):8 * (q // 2) + 8, :],
                                    pb[:, 4 + q % 2, :].rearrange("p (g k) -> p g k", g=8)).then_inc(S("hy_s2e"), 1)
                dve.wait_ge(S("hy_s2e"), 8 * j + 8)
                v3 = lambda a: a.rearrange("p (g k) -> p g k", g=8)
                for gb in range(4):
                    g, gf = slice(8 * gb, 8 * gb + 8), slice(32 * j + 8 * gb, 32 * j + 8 * gb + 8)
                    ur, ui, fr, fi = US[:, 0, g, :], US[:, 1, g, :], Fsp[:, 0, gf, :], Fsp[:, 1, gf, :]
                    if gb:
                        dve.wait_ge(S("hy_y"), 4 * j + gb)
                    else:
                        dve.wait_ge(S("hy_s1m"), 8 * j + 8)
                    ch(dve.tensor_tensor(v3(tP), ur, fr, ALU.mult))
                    ch(dve.tensor_tensor(v3(tQ), ui, fi, ALU.mult))
                    ch(dve.tensor_tensor(Y3[:, g, 1, :], v3(tP), v3(tQ), ALU.subtract))
                    ch(dve.tensor_tensor(v3(tP), ur, fi, ALU.mult))
                    ch(dve.tensor_tensor(v3(tQ), ui, fr, ALU.mult))
                    ch(dve.tensor_tensor(Y3[:, g, 2, :], v3(tP), v3(tQ), ALU.add))
                    dve.scalar_tensor_tensor(Y3[:, g, 0, :], v3(tP), -1.0, v3(tQ), ALU.mult, ALU.subtract
                                             ).then_inc(S("hy_y"), 1)
                for q in range(4):
                    dve.wait_ge(S("hy_trb"), 4 * j + q + 1)
                    pv = lambda a: a.rearrange("p (a b) -> p b a", b=FFT2)[:, 8 * q:8 * q + 8, :]
                    dve.scalar_tensor_tensor(pv(CV), pv(U), col("hyb", j), pb[:, 2 + q % 2, :].rearrange("p (n a) -> p n a", n=8),
                                             ALU.mult, ALU.add).then_inc(S("hy_cv"), 1)
                dve.wait_ge(S("hy_cv"), 4 * j + 4)
                dve.tensor_tensor(CV, CV, X0, ALU.mult).then_inc(S("hy_yc"), 1)
                dve.wait_ge(S("hy_yc"), j + 1)
                norm_dve(dve, ch, CV, RS, YF, j, j).then_inc(S("hy_done"), 1)
                dve.wait_ge(S("hy_done"), j + 1)
            dve.wait_ge(S("sp_a"), 2)
            e, z, z2, pp = sp_t[:, 4:8], sp_t[:, 8:12], sp_t[:, 12:16], sp_t[:, 0:4]
            ch(dve.tensor_scalar(z, e, 2.0, None, ALU.add))
            ch(dve.reciprocal(z, z))
            ch(dve.tensor_tensor(z, z, e, ALU.mult))
            ch(dve.tensor_tensor(z2, z, z, ALU.mult))
            ch(dve.tensor_scalar(pp, z2, 1.0 / 17, None, ALU.mult))
            for k in (15, 13, 11, 9, 7, 5, 3):
                ch(dve.scalar_tensor_tensor(pp, pp, 1.0 / k, z2, ALU.add, ALU.mult))
            ch(dve.scalar_tensor_tensor(pp, pp, 1.0, z, ALU.add, ALU.mult))
            ch(dve.tensor_scalar(z, col("rgl", 0, 4), -1.0, 0.0, ALU.mult, ALU.max))
            ch(dve.scalar_tensor_tensor(z, pp, 2.0, z, ALU.mult, ALU.add))
            ch(dve.tensor_scalar(spl[:], z, -4.0, None, ALU.mult))
            ch(dve.tensor_scalar(nspl[:], z, 4.0, None, ALU.mult))
            dve.tensor_scalar(rbh[:], col("rgb", 0, 8), 0.5, None, ALU.mult).then_inc(S("rg_spl"), 1)
            for j in range(2):
                jx, jg = J[f"rgx{j}"], J[f"rgg{j}"]
                dve.wait_ge(S("p_ev"), jx["p0"] + jx["n"])
                wc = col("rgc", 4 * j, 4)
                conv(0, jx, XR[:, 0:L], 4, wc, z=ZR).then_inc(S("rg_cv"), 1)
                conv(0, jx, XR[:, L:LT], 4, wc, n=TC, z=ZC).then_inc(S("rg_cv"), 1)
                split_lo(dve, jx["i"] + 2)
                split_lo(dve, jg["i"] + 2)
                g2 = HS[1][:, 0:L]
                dve.wait_ge(S("rg_g1"), j + 1)
                ch(dve.tensor_scalar(g2, g2, 0.044715, 1.0, ALU.mult, ALU.add))
                dve.tensor_tensor(g2, g2, GG, ALU.mult).then_inc(S("rg_g2"), 1)
                dve.wait_ge(S("rg_g3"), j + 1)
                ch(dve.scalar_tensor_tensor(GG, g2, 1.0, GG, ALU.add, ALU.mult))
                for d in range(2):
                    for x in range(NB + 1):
                        v, b = 10 * j + 5 * d + x, RORD[d][x]
                        n, c = (BLK if b < NB else TC), rcols(b)
                        dve.wait_ge(S("rg_a"), v + 1)
                        ch(dve.tensor_tensor(A2[:, 0:n], RA[:, c], RA[:, c], ALU.mult))
                        dve.wait_ge(S("rg_th"), v + 1)
                        dve.scalar_tensor_tensor(OM[:, c], A2[:, 0:n], 1.0, TH[:, v % 2, 0:n], ALU.add, ALU.mult
                                                 ).then_inc(S("rg_om"), 1)
                        dve.wait_ge(S("rg_om"), v + 1)
                        ch(dve.scalar_tensor_tensor(TI[:, c], TI[:, c], 1.0, XR[:, c], ALU.add, ALU.mult))
                    dve.wait_ge(S("rg_sq"), 2 * j + d + 1)
                    ch(dve.scalar_tensor_tensor(OM, OM, 0.5, TI, ALU.mult, ALU.mult))
                    hs, rv = HS[d], (lambda a: a) if d == 0 else (lambda a: a[:, ::-1])
                    ch(dve.tensor_tensor_scan(rv(hs[:, L:LT]), rv(RA[:, L:LT]), rv(OM[:, L:LT]), 0.0, ALU.mult, ALU.add))
                    at = LT - 1 if d == 0 else L
                    dve.tensor_tensor_scan(rv(hs[:, 0:L]), rv(RA[:, 0:L]), rv(OM[:, 0:L]), hs[:, at:at + 1],
                                           ALU.mult, ALU.add).then_inc(S("rg_scan"), 1)
                    dve.wait_ge(S("rg_scan"), 2 * j + d + 1)
                h0 = HS[0][:, 0:L]
                ch(dve.tensor_tensor(h0, h0, HS[1][:, 0:L], ALU.add))
                dve.scalar_tensor_tensor(h0, h0, 0.5, GG, ALU.mult, ALU.mult).then_inc(S("rg_y"), 1)
                dve.wait_ge(S("rg_y"), j + 1)
                norm_dve(dve, ch, h0, OM[:, 0:L], TI[:, 0:L], 2 + j, 2 + j).then_inc(S("rg_done"), 1)
                dve.wait_ge(S("rg_done"), j + 1)
            split_lo(dve, J["gates"]["i"] + 2)
            ch(dve.memset(RR[0:64], 1.0))
            ch(dve.memset(RR[0:32, 0:LT:P], 0.0))
            ch(dve.memset(RR[32:64, P - 1:LT:P], 0.0))
            dve.wait_ge(S("r_ln"), 1)
            ch(dve.scalar_tensor_tensor(LF[0:64], GT[64:128], 0.0, LN[64:128], ALU.min, ALU.subtract))
            for d in range(2):
                r = slice(32 * d, 32 * d + 32)
                rv = (lambda a: a) if d == 0 else (lambda a: a[:, ::-1])
                ch(dve.tensor_tensor_scan(rv(MM[r, L:LT]), rv(LF[r, L:LT]), rv(GT[r, L:LT]), 0.0, ALU.add, ALU.max))
                at = LT - 1 if d == 0 else L
                ch(dve.tensor_tensor_scan(rv(MM[r, 0:L]), rv(LF[r, 0:L]), rv(GT[r, 0:L]), MM[r, at:at + 1],
                                          ALU.add, ALU.max))
                ch(dve.tensor_tensor_scan(rv(BB[r]), rv(RR[r]), rv(LF[r]), 0.0, ALU.mult, ALU.add))
            ch(dve.tensor_tensor(CW[0:64], GT[0:64], BB[0:64], ALU.subtract))
            ch(dve.tensor_tensor(R1[0:64], BB[0:64], MM[0:64], ALU.subtract))
            f, b = slice(0, 32), slice(32, 64)
            ch(dve.memset(M0[0:64, :], 0.0))
            ch(dve.tensor_copy(M0[f, 1:NT], MM[f, P - 1:P * (NT - 1):P]))
            ch(dve.tensor_copy(M0[f, 0:1], MM[f, LT - 1:LT]))
            ch(dve.tensor_copy(M0[f, 17:18], MM[f, L + P - 1:L + P]))
            ch(dve.tensor_copy(M0[b, 0:NT - 1], MM[b, P:L:P]))
            ch(dve.tensor_copy(M0[b, NT - 1:NT], MM[b, L:L + 1]))
            ch(dve.tensor_copy(M0[b, 16:17], MM[b, L + P:L + P + 1]))
            ch(dve.tensor_copy(NL[f, :], R1[f, P - 1:LT:P]))
            ch(dve.tensor_copy(NL[b, :], R1[b, 0:LT:P]))
            ch(dve.tensor_tensor(AR[0:64, :], M0[0:64, :], NL[0:64, :], ALU.add))
            v = lambda a: a.rearrange("p (n t) -> p n t", t=P)
            bc = lambda a: a[0:64, :].rearrange("p (n t) -> p n t", t=1).broadcast_to([64, NTC, P])
            ch(dve.tensor_tensor(v(LN[0:64]), v(R1[0:64]), bc(M0), ALU.add))
            dve.tensor_tensor(v(RR[0:64]), v(CW[0:64]), bc(NL), ALU.add).then_inc(S("r_m"), 1)
            dve.wait_ge(S("r_bc"), 1)
            dve.tensor_copy(AB[:].rearrange("p d h n -> p (d h n)"), pb[:, 6, 0:2 * NH * NTC]).then_inc(S("r_ab"), 1)
            for n in range(NTC):
                dve.wait_ge(S("r_tr"), n + 1)
                dve.tensor_copy(CC[:, n, :].rearrange("p (g h) -> p g h", g=4),
                                pb[:, 2 + n % 2, 0:P].rearrange("p (g h) -> p g h", g=4)[:, :, 0:NH])
                dve.tensor_copy(EM[:, n, :].rearrange("p (g h) -> p g h", g=2),
                                pb[:, 2 + n % 2, P:P + 64].rearrange("p (g h) -> p g h", g=2)[:, :, 0:NH]
                                ).then_inc(S("r_cc"), 1)
            dve.memset(V1[:, :, DH:DH + 1], 1.0).then_inc(S("m_one"), 1)
            def wo_lo(k):
                dve.wait_ge(S("wo_hi"), k + 1)
                dve.scalar_tensor_tensor(wop[:, k, 1, :], wos[:, k % 2, :], WS, wop[:, k, 0, :], ALU.mult, ALU.subtract
                                         ).then_inc(S("wo_lo"), 1)

            for h in range(NH):
                jq, jk, jv, jo = (J[f"{nm}{h}"] for nm in "qkvo")
                dve.wait_ge(S("p_ev"), jq["p0"] + NB)
                if h:
                    dve.wait_ge(S("m_ylo"), NT * h)
                conv(0, jq, QT, 4, col("mlc", 4 * h, 4), z=ZM).then_inc(S("m_cv"), 1)
                split_lo(dve, jq["i"] + 2)
                dve.wait_ge(S("m_th"), 2 * h + 1)
                dve.scalar_tensor_tensor(QT, ZM[:, 0:L], 1.0, QT, ALU.add, ALU.mult).then_inc(S("m_silu"), 1)
                dve.wait_ge(S("m_silu"), 2 * h + 1)
                dve.wait_ge(S("p_ev"), jk["p0"] + NB + 1)
                wc = col("mlc", 4 * (NH + h), 4)
                conv(0, jk, KX[:, 0:L], 4, wc, z=ZM).then_inc(S("m_cv"), 1)
                conv(0, jk, KX[:, L:LT], 4, wc, n=TC, z=ZMC).then_inc(S("m_cv"), 1)
                split_lo(dve, jk["i"] + 2)
                dve.wait_ge(S("m_th"), 2 * h + 2)
                dve.scalar_tensor_tensor(KX, ZM, 1.0, KX, ALU.add, ALU.mult).then_inc(S("m_silu"), 1)
                dve.wait_ge(S("m_silu"), 2 * h + 2)
                split_lo(dve, jv["i"] + 2)

                def cl(it):
                    dve.wait_ge(S("m_cl"), it + 1)
                    if it >= 1:
                        dve.wait_ge(S("m_st"), it)
                    return pb[:, kbank(it), P:P + DH + 1]

                def state(it, dst, src, d, n):
                    part = cl(it)
                    if src is None:
                        dve.tensor_copy(dst, part).then_inc(S("m_st"), 1)
                    else:
                        dve.scalar_tensor_tensor(dst, src, AB[:, d, h, n:n + 1], part, ALU.mult, ALU.add
                                                 ).then_inc(S("m_st"), 1)

                i0 = ITS * h
                for x in range(17):
                    if x == 0 and h:
                        dve.wait_ge(S("m_out"), NT * h)
                    n = BWD[x]
                    state(i0 + x, CF[0] if x == 0 else CB[:, 15 if x == 1 else n - 1, :],
                          None if x == 0 else CF[0] if x == 1 else CB[:, n, :], 1, n)
                for y in range(2):
                    state(i0 + 17 + y, CF[y], None if y == 0 else CF[0], 0, FWD[y])
                for n in range(NT + 3):
                    cn = NT * h + n
                    if n < NT:
                        c = slice(P * n, P * n + P)
                        dve.wait_ge(S("m_E"), cn + 1)
                        if cn >= 2:
                            dve.wait_ge(S("m_out"), cn - 1)
                        for d in range(2):
                            dve.scalar_tensor_tensor(S2[cn % 2][d], pb[:, 3, 0:P], QF, E2[d], ALU.mult, ALU.mult)
                        for d in range(2):
                            ins = dve.scalar_tensor_tensor(QW[cn % 2][d], pb[:, 6 + cn % 2, P * (2 + d):P * (3 + d)], QF,
                                                           QT[:, c], ALU.mult, ALU.mult)
                        ins.then_inc(S("m_S"), 1)
                    if 1 <= n <= NT:
                        m, cm = n - 1, cn - 1
                        bk, hm = 4 + cm % 2, HM[cm % 2]
                        dve.wait_ge(S("m_out"), cm + 1)
                        if cm >= 2:
                            dve.wait_ge(S("m_sq"), cm - 1)
                            dve.wait_ge(S("m_yo"), cm - 1)
                        den = pb[:, bk, 256:389:132]
                        ch(dve.tensor_tensor(DN[:, 0:2], den, EM[:, m, h:8:4], ALU.max))
                        ch(dve.scalar_tensor_tensor(DN[:, 0:2], den, -1.0, DN[:, 0:2], ALU.mult, ALU.max))
                        ch(dve.reciprocal(DN[:, 2:4], DN[:, 0:2]))
                        ch(dve.tensor_scalar(hm, pb[:, bk, P:2 * P], DN[:, 2:3], None, ALU.mult))
                        dve.scalar_tensor_tensor(hm, pb[:, bk, 260:260 + P], DN[:, 3:4], hm, ALU.mult, ALU.add
                                                 ).then_inc(S("m_hs"), 1)
                    if 2 <= n < NT + 2:
                        cm = cn - 2
                        ms = MS[:, cm % 2, :]
                        dve.wait_ge(S("m_sq"), cm + 1)
                        if cm >= 2:
                            dve.wait_ge(S("m_rs"), cm - 1)
                        dve.tensor_scalar(ms[:, 1:2], ms[:, 0:1], 4.0 / DH, 4.0 * EPS, ALU.mult, ALU.add).then_inc(S("m_ms"), 1)
                    if n >= 3:
                        m, cm = n - 3, cn - 3
                        dve.wait_ge(S("m_yhi"), cm + 1)
                        cs = slice(P * m, P * m + P)
                        dve.tensor_tensor(yT[:, 2 + h, 1, cs], pb[:, 1, 0:P], yT[:, 2 + h, 0, cs],
                                          ALU.subtract).then_inc(S("m_ylo"), 1)
                    if n < NT - 1:
                        if n >= 1:
                            dve.wait_ge(S("m_out"), cn)
                        state(i0 + 19 + n, CF[n % 2], CF[(n + 1) % 2], 0, n)
                    if 2 <= n < NT + 2:
                        m, cm = n - 2, cn - 2
                        dve.wait_ge(S("p_ev"), jo["p0"] + m + 1)
                        if m == 0:
                            dve.wait_ge(S("gb_in"), 16 * (h + 1))
                        ch(dve.scalar_tensor_tensor(OT, OT if h < NH - 1 else OS[:, m, :], 1.0, GB, ALU.add, ALU.mult))
                        dve.wait_ge(S("m_rs"), cm + 1)
                        if cm >= 1:
                            dve.wait_ge(S("m_yt"), cm)
                        dve.scalar_tensor_tensor(YO, HM[cm % 2], MS[:, cm % 2, 2:3], OT, ALU.mult, ALU.mult
                                                 ).then_inc(S("m_yo"), 1)
                    if h == NH - 1 and 8 <= n < 8 + KT:
                        wo_lo(n - 8)
                split_lo(dve, jo["i"] + 2)
            dve.wait_ge(S("x1_in"), 16 * (NT // 2 - 1))
            for t in range(NT + 3):
                if t < NT:
                    dve.wait_ge(S("o_mm"), t + 1)
                    if t == NT // 2 - 1:
                        dve.wait_ge(S("x1_rest_in"), 16 * (NT // 2 + 1))
                    xt = x1(t)
                    dve.scalar_tensor_tensor(xt, pb[:, 2 * (t % 2):2 * (t % 2) + 2, :].rearrange("p a b -> p (a b)"), 1 / WS,
                                             xt, ALU.mult, ALU.add).then_inc(S("o_x1"), 1)
                if 1 <= t <= NT:
                    u = t - 1
                    dve.wait_ge(S("h_sq"), N5 + u + 1)
                    dve.tensor_scalar(ssq2[:, u:u + 1], ssq2[:, u:u + 1], 1.0 / D, EPS, ALU.mult, ALU.add).then_inc(S("h_ms"), 1)
                    dve.wait_ge(S("h_rs"), N5 + u + 1)
                    if u >= 2:
                        dve.wait_ge(S("h_tr"), N5 + u - 1)
                    dve.tensor_scalar(xn2[u % 2], x1(u), rst2[:, u:u + 1], None, ALU.mult).then_inc(S("h_xn"), 1)
                if t >= 3:
                    u = t - 3
                    dve.wait_ge(S("h_aff"), N5 + u + 1)
                    c = slice(P * u, P * u + P)
                    ch(dve.tensor_copy(hT2[:, :, 0, c], hf2[u % 2]))
                    dve.tensor_tensor(hT2[:, :, 1, c], hf2[u % 2], hT2[:, :, 0, c], ALU.subtract).then_inc(S("h_lo"), 1)
            for i in range(4):
                dve.memset(tiny[:], 0.0).then_inc(S("acc"), 1)
                dve.wait_ge(S("acc"), i + 1)
            for i in range(FT):
                dve.memset(tiny[:], 0.0).then_inc(S("a_lo"), 1)
                dve.wait_ge(S("a_lo"), i + 1)

            def mlp_lo(c, sl):
                dve.wait_ge(S("g_hi"), 2 * c + 1)
                dve.scalar_tensor_tensor(w1p[sl][:, :, 1, :], w1s, WS, w1p[sl][:, :, 0, :], ALU.mult, ALU.subtract
                                         ).then_inc(S("g_lo"), 1)
                dve.wait_ge(S("g_hi"), 2 * c + 2)
                dve.scalar_tensor_tensor(w2p[sl][:, :, 1, :], w2s, WS, w2p[sl][:, :, 0, :], ALU.mult, ALU.subtract
                                         ).then_inc(S("g_lo"), 1)

            mlp_lo(0, 0)

            def add_out(c, tb):
                dve.wait_ge(S("acc"), (c * 4 + tb) * 8 + 4)
                for o in range(8):
                    dve.wait_ge(S("g_mm2"), (c * 4 + tb) * 8 + o + 1)
                    xs = x1(4 * tb + o // 2)[:, BLK * (o % 2):BLK * (o % 2) + BLK]
                    dve.scalar_tensor_tensor(xs, pb[:, 4 + o % 4, :], 1.0 / (WS * AS), xs, ALU.mult, ALU.add
                                             ).then_inc(S("acc"), 1)

            def final_ms(tb):
                dve.wait_ge(S("h_sq"), N7 + 4 * tb + 4)
                c = slice(4 * tb, 4 * tb + 4)
                dve.tensor_scalar(ssq2[:, c], ssq2[:, c], 1.0 / D, EPS, ALU.mult, ALU.add).then_inc(S("h_ms"), 1)

            def final_out(tb):
                dve.wait_ge(S("h_rs"), N7 + tb + 1)
                if tb == 0:
                    dve.wait_ge(S("fg_in"), 16)
                for t in range(4 * tb, 4 * tb + 4):
                    if t >= 4:
                        dve.wait_ge(S(f"out_st{t % 4}"), 16 * (t // 4))
                    dve.scalar_tensor_tensor(outb[t % 4], x1(t), rst2[:, t:t + 1], fgbc, ALU.mult, ALU.mult
                                             ).then_inc(S("z_out"), 1)

            def dve_units(it, last=False):
                for i in range(8):
                    c, tb = 2 * it + i // 4, i % 4
                    for f in range(FT):
                        n = (c * 4 + tb) * FT + f
                        dve.wait_ge(S("a_sq"), n + 1)
                        dve.wait_ge(S("a_hi"), n + 1)
                        dve.tensor_tensor(act_p[tb % 2][:, f, 1, :], act_a[:, f, :], act_p[tb % 2][:, f, 0, :], ALU.subtract
                                          ).then_inc(S("a_lo"), 1)
                    if i >= 1:
                        add_out(2 * it + (i - 1) // 4, (i - 1) % 4)
                    if tb == 1 and not (last and i // 4 == 1):
                        mlp_lo(c + 1, (i // 4 + 1) % 2)
                    if last and i == 7:
                        final_ms(0)
                        final_out(0)
                add_out(2 * it + 1, 3)

            with dve.Fori(0, (NFC - NPEEL) // 2) as it:
                dve_units(it)
            dve_units((NFC - NPEEL) // 2, last=True)
            for tb in range(1, NB):
                final_ms(tb)
                final_out(tb)

        @block.tensor
        def _(pe):
            def ada_block(b):
                pe.wait_ge(S(f"ada_in{b % 2}"), 16 * (b // 2 + 1))
                if b >= 2:
                    pe.wait_ge(S("ada_ev"), b - 1)
                for k in range(KT):
                    mm = pe.matmul(pb[0:2, b % 2, :], scs.rearrange("p (k r) -> p k r", r=2)[:, k, :], ada_ring[b % 2][:, k, :],
                                   start=(k == 0), stop=(k == KT - 1))
                mm.then_inc(S("ada_mm"), 1)
            pe.wait_ge(S("filter_in"), 16 * 10)
            for lay in range(2):
                for b in range(NB):
                    u = NB * lay + b
                    if u >= 2:
                        pe.wait_ge(S("f_red"), u - 1)
                    if lay == 1:
                        pe.wait_ge(S("f_sin"), b + 1)
                    pe.matmul(pb[:, 4 + b % 2, :], (w1bd if lay == 0 else w2bd),
                              (featsT if lay == 0 else h1)[:, b * BLK:(b + 1) * BLK], start=True, stop=True
                              ).then_inc(S("f_mm"), 1)
                if lay == 0:
                    pe.wait_ge(S("ada_c"), 1)
                    ada_block(0)
                    ada_block(1)
            pe.wait_ge(S("f_sin"), 2 * NB)
            for n2 in range(FFT2):
                if n2 >= 2:
                    pe.wait_ge(S("f_raw"), n2 - 1)
                for q in range(2):
                    r = slice(64 * q, 64 * q + 64)
                    mm = pe.matmul(pb[r, 6 + n2 % 2, 0:HYW],
                                   h2[r, :].rearrange("p (a b) -> p b a", b=FFT2)[:, n2, :] if q == 0 else
                                   h2[r, :].rearrange("p (a b) -> p b a", b=FFT2)[:, n2, :],
                                   w3s[r, :], start=True, stop=True)
                mm.then_inc(S("f_h3"), 1)
                if n2 % 2 == 1 and 1 + n2 // 2 < 12 and n2 >= 3:
                    ada_block(1 + n2 // 2)
            for n2 in range(FFT2):
                pe.wait_ge(S("f_filt"), n2 + 1)
                pe.wait_ge(S(f"F_in{(n2 // 4) % 2}"), 16 * (n2 // 8 + 1))
                if n2 >= 2:
                    pe.wait_ge(S("f_x1"), n2 - 1)
                pe.matmul(pb[:, 4 + n2 % 2, 0:HYW], Fring[(n2 // 4) % 2][:, n2 % 4, :], filt[:, :, n2],
                          start=True, stop=True).then_inc(S("f_s1"), 1)
            pe.wait_ge(S("f_x1"), FFT2)
            for q in range(16):
                if q >= 2:
                    pe.wait_ge(S("f_x1t"), q - 1)
                for i in range(4):
                    mm = pe.transpose(pb[:, 6 + q % 2, P * i:P * i + P],
                                      X1f[:, 4 * (4 * q + i):4 * (4 * q + i) + 4, :].rearrange("p c n -> p (c n)"), ident[:])
                mm.then_inc(S("f_tr"), 1)
            pe.wait_ge(S("f_x1t"), 16)
            for q in range(16):
                g8 = slice(8 * (q // 2), 8 * (q // 2) + 8)
                if q >= 2:
                    pe.wait_ge(S("f_spec"), q - 1)
                a, b = (0, 1) if q % 2 == 0 else (1, 0)
                pe.matmul(pb[:, 2 + q % 2, :], dft[:, 0, :], X1Tf[:, a, g8, :], start=True, stop=False)
                pe.matmul(pb[:, 2 + q % 2, :], dft[:, 1 + q % 2, :], X1Tf[:, b, g8, :], start=False, stop=True
                          ).then_inc(S("f_s2"), 1)
            pe.wait_ge(S("ada_ev"), 12)
            for i in range(32):
                row = [0, 1, 3, 4][i // 8]
                mm = pe.transpose(pb[:, 7, 2 * i:2 * i + 2], arow[0:2, row * D + P * (i % 8):row * D + P * (i % 8) + P],
                                  ident[0:2, 0:2])
            mm.then_inc(S("ada_tr"), 1)
            for t in range(NTC):
                pe.wait_ge(S("h_xn"), t + 1)
                if t >= 2:
                    pe.wait_ge(S("h_aff"), t - 1)
                for k in range(KT):
                    mm = pe.transpose(pb[:, 2 + 2 * (t % 2) + k // 4, P * (k % 4):P * (k % 4) + P],
                                      xnrm[t % 2][:, P * k:P * k + P], ident[:])
                mm.then_inc(S("h_tr"), 1)
            pe.wait_ge(S("h_lo"), NTC)
            for j in range(2):
                for i in range(3):
                    project(pe, JOBS[3 * j + i])
                pe.wait_ge(S("u_ready"), j + 1)
                un = U.rearrange("p (a b) -> p b a", b=FFT2)
                for q in range(9):
                    if q < 8:
                        if q >= 2:
                            pe.wait_ge(S("hy_ut"), 8 * j + q - 1)
                        for i in range(4):
                            mm = pe.transpose(pb[0:64, 2 + q % 2, P * i:P * i + P], un[:, 4 * q + i, :], ident[:])
                        mm.then_inc(S("hy_utm"), 1)
                    if q >= 1:
                        v = q - 1
                        pe.wait_ge(S("hy_ut"), 8 * j + v + 1)
                        pe.wait_ge(S(f"Fh{v % 2}"), 16 * (4 * j + v // 2 + 1))
                        if v >= 2:
                            pe.wait_ge(S("hy_x1"), 8 * j + v - 1)
                        for i in range(4):
                            mm = pe.matmul(pb[:, 4 + v % 2, P * i:P * i + P], Fr2[v % 2][0:64, i, :], uT[0:64, 4 * v + i, :],
                                           start=True, stop=True)
                        mm.then_inc(S("hy_s1m"), 1)
                pe.wait_ge(S("hy_x1"), 8 * j + 8)
                for q in range(8):
                    if q >= 2:
                        pe.wait_ge(S("hy_tr"), 8 * j + q - 1)
                    for i in range(4):
                        g = 4 * q + i
                        mm = pe.transpose(pb[:, 2 + q % 2, P * i:P * i + P],
                                          X1[:, 4 * g:4 * g + 4, :].rearrange("p c n -> p (c n)"), ident[:])
                    mm.then_inc(S("hy_trm"), 1)
                pe.wait_ge(S("hy_tr"), 8 * j + 8)
                for q in range(8):
                    g8 = slice(8 * (q // 2), 8 * (q // 2) + 8)
                    if q >= 2:
                        pe.wait_ge(S("hy_s2e"), 8 * j + q - 1)
                    a, b = (0, 1) if q % 2 == 0 else (1, 0)
                    pe.matmul(pb[:, 4 + q % 2, :], dft[:, 0, :], X1T[:, a, g8, :], start=True, stop=False)
                    pe.matmul(pb[:, 4 + q % 2, :], dft[:, 1 + q % 2, :], X1T[:, b, g8, :], start=False, stop=True
                              ).then_inc(S("hy_s2m"), 1)
                for q in range(8):
                    pe.wait_ge(S("hy_y"), 4 * j + q // 2 + 1)
                    if q >= 2:
                        pe.wait_ge(S("hy_ze"), 8 * j + q - 1)
                    for i in range(4):
                        g = 4 * q + i
                        pe.matmul(pb[:, 2 + q % 2, P * i:P * i + P], Y3[:, g, 1:3, :].rearrange("p a k -> p (a k)"),
                                  dft[:, 0, :], start=True, stop=False)
                        mm = pe.matmul(pb[:, 2 + q % 2, P * i:P * i + P], Y3[:, g, 0:2, :].rearrange("p a k -> p (a k)"),
                                       dft[:, 1, :], start=False, stop=True)
                    mm.then_inc(S("hy_inva"), 1)
                pe.wait_ge(S("hy_ze"), 8 * j + 8)
                for q in range(8):
                    pe.wait_ge(S(f"Gh{q % 2}"), 16 * (4 * j + q // 2 + 1))
                    if q >= 2:
                        pe.wait_ge(S("hy_yt"), 8 * j + q - 1)
                    for i in range(4):
                        mm = pe.matmul(pb[0:64, 4 + q % 2, P * i:P * i + P], Gr[q % 2][:, i, :], Z[:, :, 4 * q + i],
                                       start=True, stop=True)
                    mm.then_inc(S("hy_invb"), 1)
                for q in range(4):
                    pe.wait_ge(S("hy_yt"), 8 * j + 2 * q + 2)
                    if q >= 2:
                        pe.wait_ge(S("hy_cv"), 4 * j + q - 1)
                    for i in range(8):
                        mm = pe.transpose(pb[:, 2 + q % 2, 64 * i:64 * i + 64], yt[0:64, 8 * q + i, :], ident[0:64, 0:64])
                    mm.then_inc(S("hy_trb"), 1)
                norm_pe(pe, SQ, j)
            for j in range(2):
                project(pe, J[f"rgx{j}"])
                project(pe, J[f"rgg{j}"])
                pe.wait_ge(S("rgw_in"), 64)
                pe.wait_ge(S("rg_cv"), 2 * j + 2)
                for v in range(10 * j, 10 * j + 10):
                    d, x = (v // 5) % 2, v % 5
                    b = RORD[d][x]
                    n = BLK if b < NB else TC
                    if v >= 2:
                        pe.wait_ge(S("rg_ev"), v - 1)
                    for g in range(2):
                        mm = pe.matmul(pb[:, 2 + 2 * g + v % 2, 0:n], rgw[:, j, 2 * d + g, :], XR[:, rcols(b)],
                                       start=True, stop=True)
                    mm.then_inc(S("rg_mm"), 1)
                norm_pe(pe, HS[1][:, 0:L], 2 + j)
            project(pe, J["gates"])
            pe.wait_ge(S("r_ar"), 1)
            for d in range(2):
                for h in range(NH):
                    mm = pe.matmul(pb[:, 6, NTC * (NH * d + h):NTC * (NH * d + h) + NTC],
                                   ident[0:64, 32 * d + h:32 * d + h + 1].broadcast_to([64, P]), AR[0:64, :],
                                   start=True, stop=True)
            mm.then_inc(S("r_bc"), 1)
            pe.wait_ge(S("r_rows"), 1)
            for n in range(NTC):
                if n >= 2:
                    pe.wait_ge(S("r_cc"), n - 1)
                pe.transpose(pb[:, 2 + n % 2, 0:P], CW[:, P * n:P * n + P], ident[:])
                pe.transpose(pb[:, 2 + n % 2, P:P + 64], LF[0:64, P * n:P * n + P], ident[0:64, 0:64]).then_inc(S("r_tr"), 1)
            for h in range(NH):
                jq, jk, jv, jo = (J[f"{nm}{h}"] for nm in "qkvo")
                project(pe, jq)
                project(pe, jk)
                project(pe, jv)
                pe.wait_ge(S("m_silu"), 2 * h + 2)
                pe.wait_ge(S("r_cc"), NTC)
                i0 = ITS * h

                def ktr(it, n):
                    x = it - i0
                    if x == 0 and h:
                        pe.wait_ge(S("m_ylo"), NT * h)
                    if x >= 17 or (x == 0 and h):
                        pe.wait_ge(S("m_st"), it)
                    elif x >= 4:
                        pe.wait_ge(S("m_st"), it - 3)
                    pe.transpose(pb[:, kbank(it), 0:P], KX[:, P * n:P * n + P], ident[:]).then_inc(S("m_kt"), 1)

                def csum(it, n):
                    pe.wait_ge(S("m_kw"), it + 1)
                    pe.matmul(pb[:, kbank(it), P:P + DH + 1], KW[it % 2], V1[:, n, :], start=True, stop=True).then_inc(S("m_cl"), 1)

                seq = BWD[0:17] + FWD[0:17]
                ktr(i0, seq[0])
                for x in range(19):
                    if x + 1 < 17:
                        ktr(i0 + x + 1, seq[x + 1])
                    csum(i0 + x, seq[x])
                    if h == NH - 1 and x < NT:
                        project(pe, jo, [x])
                    if x + 1 >= 17:
                        ktr(i0 + x + 1, seq[x + 1])

                def heads(n):
                    cn = NT * h + n
                    c = slice(P * n, P * n + P)
                    if cn >= 1:
                        pe.wait_ge(S("m_S"), cn)
                    row = lambda r: ident[:, r:r + 1].broadcast_to([P, P])
                    for d in range(2):
                        pe.matmul(pb[:, 6 + cn % 2, P * d:P * d + P], row(32 * d + h), R1[:, c], start=True, stop=False)
                        pe.matmul(pb[:, 6 + cn % 2, P * d:P * d + P], identb[:], maskneg[:, d, :], start=False, stop=True)
                    for d in range(2):
                        pe.matmul(pb[:, 6 + cn % 2, P * (2 + d):P * (3 + d)], row(64 + 32 * d + h), R1[:, c],
                                  start=True, stop=True)
                    pe.matmul(pb[:, 3, 0:P], KX[:, c], QT[:, c], start=True, stop=True).then_inc(S("m_A"), 1)

                def ytr(m):
                    cm = NT * h + m
                    pe.wait_ge(S("m_yo"), cm + 1)
                    if cm >= 1:
                        pe.wait_ge(S("m_ylo"), cm)
                    pe.transpose(pb[:, 1, 0:P], YO, ident[:]).then_inc(S("m_yt"), 1)

                heads(0)
                for n in range(NT + 2):
                    cn = NT * h + n
                    if n < NT - 1:
                        heads(n + 1)
                        csum(i0 + 19 + n, n)
                    if n < NT:
                        pe.wait_ge(S("m_S"), cn + 1)
                        pe.wait_ge(S("m_st"), i0 + 19 + n)
                        if cn >= 2:
                            pe.wait_ge(S("m_hs"), cn - 1)
                        for d in range(2):
                            o = pb[:, 4 + cn % 2, P + 132 * d:P + 132 * d + DH + 1]
                            pe.matmul(o, S2[cn % 2][d], V1[:, n, :], start=True, stop=False)
                            mm = pe.matmul(o, QW[cn % 2][d], CF[(n + 1) % 2] if d == 0 else CB[:, n, :], start=False, stop=True)
                        mm.then_inc(S("m_out"), 1)
                    if 1 <= n <= NT and h < NH - 1:
                        project(pe, jo, [n - 1])
                    if n < NT - 2:
                        ktr(i0 + 20 + n, n + 1)
                    if n >= 2:
                        ytr(n - 2)
            pe.wait_ge(S("wo_lo"), KT)
            pe.wait_ge(S("m_ylo"), NT * NH)
            for t in range(NT + 2):
                if t < NT:
                    if t >= 2:
                        pe.wait_ge(S("o_x1"), t - 1)
                    for dh in range(2):
                        for k in range(KT):
                            for m, (ys, ws) in enumerate(((0, 0), (0, 1), (1, 0))):
                                mm = pe.matmul(pb[:, 2 * (t % 2) + dh, :], yT[:, k, ys, P * t:P * t + P],
                                               wop[:, k, ws, BLK * dh:BLK * dh + BLK],
                                               start=(k == 0 and m == 0), stop=(k == KT - 1 and m == 2))
                    mm.then_inc(S("o_mm"), 1)
                if t >= 2:
                    u = t - 2
                    pe.wait_ge(S("h_xn"), N5 + u + 1)
                    if u >= 2:
                        pe.wait_ge(S("h_aff"), N5 + u - 1)
                    for k in range(KT):
                        mm = pe.transpose(pb[:, 4 + 2 * (u % 2) + k // 4, P * (k % 4):P * (k % 4) + P],
                                          xn2[u % 2][:, P * k:P * k + P], ident[:])
                    mm.then_inc(S("h_tr"), 1)

            def up(c, tb, sl):
                if tb == 0:
                    pe.wait_ge(S("g_lo"), 2 * c + 1)
                pe.wait_ge(S("h_lo"), N5 + 4 * tb + 4)
                for f in range(FT):
                    for k in range(KT):
                        for m, (ws, hs) in enumerate(((0, 0), (0, 1), (1, 0))):
                            mm = pe.matmul(pb[:, 2 * (tb % 2) + f, :], w1p[sl][:, k, ws, P * f:P * f + P],
                                           hT2[:, k, hs, BLK * tb:BLK * tb + BLK],
                                           start=(k == 0 and m == 0), stop=(k == KT - 1 and m == 2))
                    mm.then_inc(S("g_mm1"), 1)

            def down(c, tb, sl):
                pe.wait_ge(S("a_lo"), ((c * 4 + tb) + 1) * FT + FT)
                if tb == 0:
                    pe.wait_ge(S("g_lo"), 2 * c + 2)
                for o in range(8):
                    tt, dh = o // 2, o % 2
                    pe.wait_ge(S("acc"), (c * 4 + tb) * 8 + o + 1)
                    for f in range(FT):
                        for m, (hs, ws) in enumerate(((0, 0), (0, 1), (1, 0))):
                            mm = pe.matmul(pb[:, 4 + o % 4, :], act_p[tb % 2][:, f, hs, P * tt:P * tt + P],
                                           w2p[sl][:, f, ws, BLK * dh:BLK * dh + BLK],
                                           start=(f == 0 and m == 0), stop=(f == FT - 1 and m == 2))
                    mm.then_inc(S("g_mm2"), 1)

            def pe_units(it):
                for i in range(8):
                    up(2 * it + i // 4, i % 4, i // 4)
                    if i >= 1:
                        down(2 * it + (i - 1) // 4, (i - 1) % 4, (i - 1) // 4)
                down(2 * it + 1, 3, 1)

            with pe.Fori(0, (NFC - NPEEL) // 2) as it:
                pe_units(it)
            pe_units((NFC - NPEEL) // 2)


def host_data(inp):
    f = lambda a: np.ascontiguousarray(np.asarray(a))
    z = lambda *sh: np.zeros(sh, np.float32)
    pk = z(P, NCOL)

    def put(name, a):
        at, n = COLS[name]
        pk[:, at:at + n] = a

    byp = lambda a: f(a).reshape(-1, P).T
    put("cc", np.stack([byp(inp["c"][0]), byp(inp["c_ctx"])], axis=2).reshape(P, 16))
    put("n1g", byp(inp["norm1_g"][0]))
    put("n2g", byp(inp["norm2_g"][0]))
    ab = f(inp["ada_b"][0]).reshape(6, D)
    put("adab", byp(ab[[0, 1, 3, 4]].reshape(-1)))
    hc = f(inp["hy_conv"][0])
    put("hyc", hc.reshape(3, 6, P).transpose(2, 1, 0).reshape(P, 18))
    put("hyb", byp(inp["hy_bias"][0]))
    put("mlc", f(inp["ml_conv"][0]).reshape(4, 8, P).transpose(2, 1, 0).reshape(P, 32))
    put("rgc", f(inp["rg_conv"][0]).reshape(4, 2, P).transpose(2, 1, 0).reshape(P, 8))
    put("rgb", f(inp["rg_gate_b"][0]).reshape(4, 2, P).transpose(2, 1, 0).reshape(P, 8))
    put("rgl", f(inp["rg_lambda"][0]).reshape(2, 2, P).transpose(2, 1, 0).reshape(P, 4))
    mg = f(inp["mix_norm_g"][0])
    put("gcm", byp(np.concatenate([mg[:HYW], mg[HYW + MLW:]])))
    two = lambda a: np.concatenate([f(a), f(a)])
    put("ffn", np.stack([two(inp["hy_b1"][0]), two(inp["hy_freq"][0, 0]), two(inp["hy_b2"][0]),
                         two(inp["hy_freq"][0, 1])], axis=1))
    gb = f(inp["ml_gate_b"][0]).reshape(4, NH)
    g2 = z(P, 1)
    g2[0:4, 0], g2[32:36, 0], g2[64:68, 0], g2[96:100, 0] = gb[0], gb[2], gb[1], gb[3]
    put("gb", g2)
    n1, n2 = np.arange(64)[:, None], np.arange(FFT2)[None]
    tf = FFT2 * n1 + n2
    tb = L - FFT2 * n1 - n2
    put("negt", -(np.concatenate([tf, tb], axis=0) / (L - 1)).astype(np.float32))
    out = {"cols": pk, "ident": np.eye(P, dtype=np.float32)}
    bands = 16
    pos = np.arange(L, dtype=np.float32)
    t = (pos / np.float32(L - 1)).astype(np.float32)
    fr = np.linspace(1e-4, bands - 1, bands, dtype=np.float32)
    ang = (np.float32(2.0 * math.pi / L) * fr[None] * pos[:, None]).astype(np.float32)
    feats = np.concatenate([t[:, None], np.cos(ang), -np.sin(ang)], axis=-1).astype(np.float32)
    ft = z(P, L)
    ft[0:33] = feats.T
    ft[64:97, 1:] = feats[:0:-1].T
    out["feats"] = ft
    mx, mn = math.log(1e-2) / 0.3, math.log(1e-2) / 1.5
    out["absdelta"] = np.abs(np.linspace(mn, mx, HYW, dtype=np.float32))[None]
    n1 = np.arange(FFT1)[:, None, None]
    n2 = np.arange(FFT2)[None, :, None]
    k1 = np.arange(64)[None, None, :]
    th = 2 * np.pi * (k1 + 0.5) * (FFT2 * n1 + n2) / (FFT1 * FFT2)
    Fm = np.concatenate([np.cos(th), -np.sin(th)], axis=2)
    Fm[64:] *= -1
    Fm[64, 0] = 0
    out["Fm"] = Fm.astype(np.float32)
    thi = th[:64].transpose(2, 1, 0)
    sc = 2.0 / (FFT1 * FFT2)
    out["Gm"] = (np.concatenate([np.cos(thi), -np.sin(thi)], axis=0) * sc).astype(np.float32)
    a = np.arange(FFT2)
    w = 2 * np.pi * a[:, None] * a[None] / FFT2
    bd = lambda m: np.kron(np.eye(4), m)
    out["dft"] = np.stack([bd(np.cos(w)), bd(np.sin(w)), bd(-np.sin(w))], axis=1).astype(np.float32)
    out["gones"] = np.kron(np.eye(2), np.ones((64, 64))).astype(np.float32)
    si, ti = np.arange(P)[:, None], np.arange(P)[None]
    out["maskneg"] = np.stack([np.where(si <= ti, 0, NEG), np.where(si >= ti, 0, NEG)], axis=1).astype(np.float32)
    for name in ("hy_w1", "hy_w2", "hy_w3", "ada_w", "w_in", "w_out", "mlp_w1", "mlp_w2"):
        out[name] = f(inp[name][0])
    out["hy_b3"] = f(inp["hy_b3"])
    out["x"] = f(inp["x"][0])
    out["rgw"] = f(inp["rg_gate_w"][0]).reshape(4, 4, 64, 64)
    out["gml"] = mg[None, HYW:HYW + MLW].copy()
    out["final_g"] = f(inp["final_g"])[None]
    out["adab25"] = ab[[2, 5]][None].copy()
    out["ctx"] = f(inp["ctx"][0])
    return out


def kernel(**inputs):
    import concourse.bacc as _bacc
    from concourse.bass_utils import run_bass_kernel_spmd as _run

    nc = _bacc.Bacc("TRN2", target_bir_lowering=False, num_devices=1)
    arrays = host_data(inputs)
    dr = {k: nc.dram_tensor("in_" + k, a.shape, mybir.dt.from_np(a.dtype), kind="ExternalInput").ap()
          for k, a in arrays.items()}
    dr["out"] = nc.dram_tensor("out_0", (L, D), F32, kind="ExternalOutput").ap()
    dr["mod25"] = nc.dram_tensor("mod25", (2, D), F32, kind="Internal").ap()
    program(nc, dr)
    r = _run(nc, [{"in_" + k: a for k, a in arrays.items()}], core_ids=[0])
    return r.results[0]["out_0"].reshape(1, L, D)
```

```python
from contextlib import ExitStack
import math

import concourse.bass as bass
from concourse import mybir
import numpy as np

F32 = mybir.dt.float32
F16 = mybir.dt.float16
BF16 = mybir.dt.bfloat16
ALU = mybir.AluOpType
ACT = mybir.ActivationFunctionType

P = 128
D = 1024
L = 2048
TC = 256
LT = L + TC
KT = D // P
NT = L // P
NTC = LT // P
BLK = 512
NB = L // BLK
GW = 64
GR = L // GW
EPS = 1e-6
HYW, MLW, RGW = 256, 512, 256
NH = 4
DH = 128
OFF_ML = 3 * HYW
OFF_RG = OFF_ML + 4 * MLW + 16
P_IN = OFF_RG + 2 * RGW
DFF = 4 * D
FFT1, FFT2 = 128, 32
WS = 1024.0
FC = 256
NFC = DFF // FC
MAGIC = 12582912.0
NEG = -1e30

COLS = {}


def _cols():
    at = 0
    for name, n in (("cc", 16), ("n1g", 8), ("n2g", 8), ("adab", 32), ("hyc", 18), ("hyb", 2), ("mlc", 32),
                    ("rgc", 8), ("rgb", 8), ("rgl", 4), ("gcm", 4), ("ffn", 4), ("gb", 1), ("negt", 32)):
        COLS[name] = (at, n)
        at += n
    return at


NCOL = _cols()


def program(nc, dr):
    ctx = ExitStack()
    with ctx:
        def sb(name, shape, dt=F32):
            return ctx.enter_context(nc.sbuf_tensor(name, shape, dt))

        def sem(name):
            return ctx.enter_context(nc.semaphore(name))

        AW = 51200
        arena = sb("arena", [P, AW])
        pb = ctx.enter_context(nc.psum_tensor("pb", [P, 8, 512], F32))
        KB = 256

        def view(kb, shape, dt=F32, off=0):
            n = 1
            for s in shape:
                n *= s
            words = n * (2 if dt in (F16, BF16) else 4) // 4
            at = int(kb * KB) + off
            assert at + words <= AW, (kb, shape)
            v = arena[:, at:at + words]
            if dt != F32:
                v = v.bitcast(dt)
            if len(shape) == 2:
                v = v.rearrange("p (a b) -> p a b", a=shape[0])
            elif len(shape) == 3:
                v = v.rearrange("p (a b c) -> p a b c", a=shape[0], b=shape[1])
            return v

        cols = sb("cols", [P, NCOL])
        ident = sb("ident", [P, P])
        identb = sb("identb", [P, P], BF16)
        maskneg = sb("maskneg", [P, 2, P], BF16)
        conv_consts = sb("conv_consts", [P, 4, P])
        dft = conv_consts[:, 0:3, :]
        gones = conv_consts[:, 3, :]
        modT = sb("modT", [P, 32, 2])
        affA = sb("affA", [P, 3, KT])
        affB = sb("affB", [P, 3, KT])
        small = sb("small", [P, 64])

        def col(name, i=0, n=1):
            return cols[:, COLS[name][0] + i:COLS[name][0] + i + n]

        hT = view(0, [KT, 2, LT], F16)
        yT = view(72, [KT, 2, L], F16)
        wst = view(188, [KT, P])
        whl = view(192, [2, 2 * KT, P], F16)
        Fsp = view(88, [2, 64, 64])

        s = {}

        def S(name):
            if name not in s:
                s[name] = sem(name)
            return s[name]

        class Chain:

            def __init__(self, eng, name):
                self.eng, self.sem, self.n = eng, S(name), 0

            def __call__(self, ins):
                self.n = self.n + 1
                ins.then_inc(self.sem, 1)
                self.eng.wait_ge(self.sem, self.n)

        ada_ring = [view(0, [KT, BLK]), view(16, [KT, BLK])]
        featsT = view(32, [L])
        h1 = view(40, [L])
        h2 = view(48, [L])
        arow = view(56, [6 * D])
        filt = view(120, [HYW, FFT2])
        X1f = view(152, [HYW, FFT2])
        X1Tf = view(120, [2, 64, 64])
        w1bd = view(80, [P])
        w2bd = view(80.5, [P])
        w3s = view(81, [HYW])
        b3bc = view(82, [HYW])
        dbc = view(83, [HYW])
        dec = [view(84, [HYW]), view(85, [HYW])]
        ftmp = [view(86, [HYW]), view(87, [HYW])]
        red = [view(184, [BLK]), view(186, [BLK]), view(188, [BLK])]
        mask_in = view(194, [2, P])
        scs = small[:, 0:16]
        sct = small[:, 16:32]
        Fring = [view(190, [4, P]), view(192, [4, P])]

        xring = [view(152 + 4 * i, [D]) for i in range(4)]
        hf = [view(168, [KT, P]), view(172, [KT, P])]
        xnrm = [view(176, [D]), view(180, [D])]
        junk = view(184, [D])
        ssq = small[:, 32:32 + NTC]
        rst = sb("rst", [P, NTC])
        mhalf = sb("mhalf", [P, 1])
        adab_row = view(40, [2, D])

        JOBS = []

        def job(name, kind, parts, lat, with_ctx):
            JOBS.append(dict(name=name, kind=kind, parts=parts, n=NT if kind == "chunk" else NB + (1 if with_ctx else 0),
                             p0=sum(x["n"] for x in JOBS), step=1, i=len(JOBS)))

        for j in range(2):
            for i, nm in ((1, "x1"), (2, "v"), (0, "x0")):
                job(f"hy{nm}{j}", "cm", [(0, HYW * i + P * j, P)], True, False)
        for j in range(2):
            job(f"rgg{j}", "cm", [(0, OFF_RG + RGW + P * j, P)], True, False)
            job(f"rgx{j}", "cm", [(0, OFF_RG + P * j, P)], True, True)
        GO = OFF_ML + 4 * MLW
        job("gates", "cm", [(0, GO, 4), (32, GO + 8, 4), (64, GO + 4, 4), (96, GO + 12, 4)], True, True)
        for h in range(NH):
            job(f"k{h}", "cm", [(0, OFF_ML + MLW + P * h, P)], True, True)
            job(f"q{h}", "cm", [(0, OFF_ML + P * h, P)], True, False)
            job(f"v{h}", "tm", [(0, OFF_ML + 2 * MLW + P * h, P)], True, True)
            job(f"o{h}", "chunk", [(0, OFF_ML + 3 * MLW + P * h, P)], True, False)
        J = {x["name"]: x for x in JOBS}
        JOBS[0]["step"] = JOBS[1]["step"] = 2
        JOBS[1]["p0"] = 1
        for h in range(NH):
            J[f"v{h}"]["p0"] += NB
            J[f"v{h}"]["step"] = -1

        def unit(jb, b):
            return jb["p0"] + jb["step"] * b

        def units_to_end(jb):
            return max(unit(jb, 0), unit(jb, jb["n"] - 1)) + 1
        w_src = dr["w_in"].rearrange("(k p) n -> p k n", p=P)

        def x_tokens(t):
            return dr["x"].rearrange("(r c) d -> c r d", c=GW)[4 * t:4 * t + 4]

        def to_rows(dst, b):
            return dst.rearrange("p (r c) -> p c r", c=GW)[:, 16 * b:16 * b + 16, :]

        def cr(a):
            return a.rearrange("p (c r) -> p c r", r=GR)

        def load_w(sp, jb):
            i = jb["i"]
            if i >= 1:
                sp.wait_ge(S("w_split"), i)
            if jb["name"] == "gates":
                sp.wait_ge(S("w_clear"), 1)
            for at, c0, n in jb["parts"]:
                sp.dma_start(wst[:, :, at:at + n], w_src[:, :, c0:c0 + n]).then_inc(S("w_in"), 16)

        def w_need(i):
            return 16 * sum(len(x["parts"]) for x in JOBS[:i + 1])

        def split_hi(act, i):
            if i >= len(JOBS):
                return
            act.wait_ge(S("w_in"), w_need(i))
            if i >= 2:
                act.wait_ge(S("p_mm"), units_to_end(JOBS[i - 2]))
            act.activation(whl[:, (i + 1) % 2, 0:KT, :], wst, ACT.Copy, scale=WS).then_inc(S("w_hi"), 1)

        def split_lo(dve, i):
            if i >= len(JOBS):
                return
            dve.wait_ge(S("w_hi"), i + 1)
            dve.scalar_tensor_tensor(whl[:, (i + 1) % 2, KT:2 * KT, :], wst, WS, whl[:, (i + 1) % 2, 0:KT, :],
                                     ALU.mult, ALU.subtract).then_inc(S("w_split"), 1)
            if i + 1 < len(JOBS) and JOBS[i + 1]["name"] == "gates":
                dve.wait_ge(S("w_split"), i + 1)
                dve.memset(wst, 0.0).then_inc(S("w_clear"), 1)

        def project(pe, jb, blocks=None):
            i = jb["i"]
            pe.wait_ge(S("w_split"), i + 1)
            after_chunks = i >= 1 and JOBS[i - 1]["kind"] == "chunk"
            for b in (range(jb["n"]) if blocks is None else blocks):
                u = unit(jb, b)
                if jb["kind"] == "chunk" or (after_chunks and b < 2):
                    pe.wait_ge(S("p_ev"), u if jb["kind"] == "chunk" else jb["p0"])
                    if after_chunks and u % 2 == 0:
                        pe.wait_ge(S("m_ylo"), NT * (int(jb["name"][1:])))
                elif u >= 2:
                    pe.wait_ge(S("p_ev"), u - 1)
                if jb["kind"] == "cm":
                    t0, n = (BLK * b, BLK) if b < NB else (L, TC)
                    for k in range(KT):
                        for m, (ws, hs) in enumerate(((0, 0), (0, 1), (1, 0))):
                            mm = pe.matmul(pb[:, u % 2, 0:n], whl[:, (i + 1) % 2, KT * ws + k, :], hT[:, k, hs, t0:t0 + n],
                                           start=(k == 0 and m == 0), stop=(k == KT - 1 and m == 2))
                else:
                    chunk = jb["kind"] == "chunk"
                    for q in range(1 if chunk else 4 if b < NB else 2):
                        for k in range(KT):
                            for m, (ws, hs) in enumerate(((0, 0), (1, 0), (0, 1))):
                                c0 = P * b if chunk else BLK * b + P * q
                                lhs = hT[:, k, hs, c0:c0 + P]
                                mm = pe.matmul(pb[:, 1 if chunk else u % 2, P * q:P * q + P], lhs, whl[:, (i + 1) % 2, KT * ws + k, :],
                                               start=(k == 0 and m == 0), stop=(k == KT - 1 and m == 2))
                mm.then_inc(S("p_mm"), 1)

        ZPW = L + 8
        ZP = [[view(120, [ZPW]), view(128.0625, [ZPW])],
              [view(168.25, [ZPW]), view(176.3125, [ZPW])]]
        ZX = view(80, [L])
        U = view(136.25, [L])
        X0 = view(144.25, [L])
        uT = view(152.25, [FFT2, P])
        X1T = view(152.25, [2, 32, 64])
        X1 = view(120, [P, FFT2])
        US = view(120, [2, 32, 64])
        Y3 = view(152.25, [32, 3, 64])
        Z = view(120, [P, FFT2])
        yt = view(152.25, [FFT2, P])
        Fr2 = [view(176.25, [4, P]), view(178.25, [4, P])]
        Gr = [view(180.25, [4, 64]), view(181.25, [4, 64])]
        tP, tQ = view(176.25, [BLK]), view(178.25, [BLK])
        CV = view(120, [L])
        SQ = view(128, [L])
        RS = view(152.25, [L])
        YF = view(160.25, [L])


        XR = view(88, [LT])
        GG = [view(97, [L]), view(128, [L])]
        RA = view(106, [LT])
        rgw = view(115, [2, 4, P])
        OM = view(136.25, [LT])
        TI = view(145.25, [LT])
        HS = [view(154.25, [LT]), view(163.25, [LT])]
        RT = view(172.25, [2, BLK])
        TH = view(174.25 + 2, [2, BLK])
        A2 = view(180.25, [BLK])
        ZC = view(182.25, [TC + 8])
        ZR = view(163.25, [LT])
        RORD = [[4, 0, 1, 2, 3], [4, 3, 2, 1, 0]]

        def rcols(b):
            return slice(BLK * b, BLK * b + (BLK if b < NB else TC))
        spl = sb("spl", [P, 4])
        nspl = sb("nspl", [P, 4])
        rbh = sb("rbh", [P, 8])
        sp_t = sb("sp_t", [P, 16])

        GT = view(97, [LT])
        LN = view(88, [LT])
        RR = view(106, [LT])
        LF = view(136.25, [LT])
        MM = view(145.25, [LT])
        BB = view(154.25, [LT])
        CW = GT
        R1 = view(175, [LT])
        CC = sb("CC", [P, NTC, 16])
        EM = sb("EM", [P, NTC, 8])
        M0 = sb("M0", [P, NTC])
        NL = sb("NL", [P, NTC])
        AB = sb("AB", [P, 2, NH, NTC])
        QT = view(136, [L])
        KX = view(144, [LT])
        V1 = view(153, [NTC, DH + 1])
        TK = view(153, [LT])
        CB = view(162.125, [NT, DH + 1])
        ZM = view(163.25, [LT])
        ZMC = view(172.3125, [TC + 8])
        E2 = [view(171.5, [P], off=P * i) for i in range(2)]
        S2 = [[view(171.5, [P], off=P * (2 + i)) for i in range(2)], [conv_consts[:, i, :] for i in range(2)]]
        QW = [[view(171.5, [P], off=P * (4 + i)) for i in range(2)], [conv_consts[:, 2 + i, :] for i in range(2)]]
        KW = [view(171.5, [P], off=P * 6), view(170.25, [P])]
        CF = [view(184, [DH + 1], off=(DH + 1) * i) for i in range(2)]
        HM = [view(184, [P], off=258), view(170.75, [P])]
        OT = view(184, [P], off=386)
        YO = view(184, [P], off=514)
        OS = view(188, [NT, P])
        JK = view(184, [P], off=642)
        GB = view(184, [P], off=770)
        DN = sb("DN", [P, 4])
        MS = sb("MS", [P, 2, 4])
        QF = 0.25 * DH ** -0.5
        FWD = [16, 17] + list(range(NT))
        BWD = [17, 16] + list(range(NT - 1, -1, -1))
        AR = sb("AR", [P, NTC])

        def kbank(it):
            return 2 + (it % ITS) % 4 if it % ITS < 17 else 2

        ITS = 34

        x1a, x1b = view(32, [NT // 2, D]), view(136, [NT // 2, D])

        def x1(t):
            return x1a[:, t, :] if t < NT // 2 else x1b[:, t - NT // 2, :]
        hT2 = yT
        wop = view(0, [KT, 2, D], F16)
        wos = [view(64, [D]), view(68, [D]), view(56, [D]), view(52, [D])]
        EARLY = 5

        def wo_half(i):
            return i // 2, slice(BLK * (i % 2), BLK * (i % 2) + BLK)

        m2bc = view(60, [D])
        hf2 = [view(64, [KT, P]), view(68, [KT, P])]
        xn2 = [view(184, [D]), view(188, [D])]
        junk2 = view(192, [D])
        N5, N7 = NTC, NTC + NT
        ssq2 = sb("ssq2", [P, NT])
        rst2 = sb("rst2", [P, NT])

        FT = FC // P
        AS = 1.0 / 64
        w1s, w2s = view(168, [KT, FC]), view(176, [FT, D])
        w1p = [view(8 * i, [KT, 2, FC], F16) for i in range(2)]
        w2p = [view(16 + 8 * i, [FT, 2, D], F16) for i in range(2)]
        m5bc = view(196, [D])
        act_p = [view(64 + 4 * i, [FT, 2, BLK], F16) for i in range(2)]
        act_r, act_a = view(184, [FT, BLK]), view(188, [FT, BLK])
        fgbc = view(192, [D])
        outb = [view(168 + 4 * i, [D]) for i in range(4)]
        junk_f = [view(0, [D]), view(4, [D])]
        tiny = sb("tiny", [P, 1])
        NPEEL = 2

        def norm_act(act, y, sq, rs, q, between=None):
            act.activation(sq, y, ACT.Square).then_inc(S("nm_sq"), 1)
            if between:
                between()
            for b in range(NB):
                act.wait_ge(S("nm_mm"), NB * q + b + 1)
                act.activation(rs[:, BLK * b:BLK * b + BLK], pb[:, 4 + b, :], ACT.Ln, scale=1.0 / 64, bias=eps_c[:]
                               ).then_inc(S("nm_ln"), 1)
            act.wait_ge(S("nm_ln"), NB * q + NB)
            act.activation(rs, rs, ACT.Exp, scale=-0.5).then_inc(S("nm_rs"), 1)

        def norm_pe(pe, sq, q):
            pe.wait_ge(S("nm_sq"), q + 1)
            for b in range(NB):
                pe.matmul(pb[:, 4 + b, :], gones, sq[:, BLK * b:BLK * b + BLK], start=True, stop=True
                          ).then_inc(S("nm_mm"), 1)

        def norm_dve(dve, ch, y, rs, yf, q, gi):
            t = q if q < 2 else q + 4
            dve.wait_ge(S("nm_rs"), q + 1)
            ch(dve.scalar_tensor_tensor(yf, y, col("gcm", gi), rs, ALU.mult, ALU.mult))
            yc = yf.rearrange("p (r c) -> p c r", c=GW)
            ch(dve.tensor_copy(cr(yT[:, t, 0, :]), yc))
            return dve.tensor_tensor(cr(yT[:, t, 1, :]), yc, cr(yT[:, t, 0, :]), ALU.subtract)

        eps_c = sb("eps_c", [P, 1])
        block = ctx.enter_context(nc.Block())

        @block.sync
        def _(sp):
            sp.dma_start(cols[:], dr["cols"]).then_inc(S("params_in"), 16)
            sp.dma_start(ident[:], dr["ident"]).then_inc(S("params_in"), 16)
            sp.dma_start(featsT, dr["feats"]).then_inc(S("filter_in"), 16)
            sp.wait_ge(S("w_zeroed"), 1)
            for q in range(2):
                r = slice(64 * q, 64 * q + 64)
                sp.dma_start(w1bd[64 * q:64 * q + 33, 64 * q:64 * q + 64], dr["hy_w1"]).then_inc(S("filter_in"), 16)
                sp.dma_start(w2bd[r, 64 * q:64 * q + 64], dr["hy_w2"]).then_inc(S("filter_in"), 16)
                sp.dma_start(w3s[r, :], dr["hy_w3"][:, HYW * q:HYW * q + HYW]).then_inc(S("filter_in"), 16)
                sp.dma_start(b3bc[r, :], dr["hy_b3"][:, HYW * q:HYW * q + HYW].broadcast_to([64, HYW])
                             ).then_inc(S("filter_in"), 16)
            sp.dma_start(dbc[:], dr["absdelta"].broadcast_to([P, HYW])).then_inc(S("filter_in"), 16)
            sp.dma_start(dft, dr["dft"]).then_inc(S("params_in"), 16)
            sp.dma_start(gones, dr["gones"]).then_inc(S("params_in"), 16)
            sp.dma_start(mask_in, dr["maskneg"]).then_inc(S("params_in"), 16)
            for b in range(12):
                if b >= 2:
                    sp.wait_ge(S("ada_mm"), b - 1)
                sp.dma_start(ada_ring[b % 2], dr["ada_w"][:, b * BLK:(b + 1) * BLK].rearrange("(k p) n -> p k n", p=P)
                             ).then_inc(S(f"ada_in{b % 2}"), 16)
            sp.wait_ge(S("f_sin"), 2 * NB)
            sp.wait_ge(S("f_mm"), 2 * NB)
            sp.dma_start(adab_row[0:1, :, :], dr["adab25"]).then_inc(S("adab_in"), 16)
            for fj in range(FFT2 // 4):
                if fj >= 2:
                    sp.wait_ge(S("f_s1"), 4 * (fj - 1))
                sp.dma_start(Fring[fj % 2], dr["Fm"][:, 4 * fj:4 * fj + 4, :]).then_inc(S(f"F_in{fj % 2}"), 16)
                if fj == 1:
                    sp.wait_ge(S("ada_row"), 2)
                    for i, r in enumerate((2, 5)):
                        sp.dma_start(dr["mod25"][i:i + 1, :], arow[0:1, r * D:(r + 1) * D]).then_inc(S("mod25_st"), 16)
            sp.wait_ge(S("f_tr"), 16)
            for t in range(NTC):
                if t in (2, 6):
                    load_w(sp, JOBS[t // 4])
                if t >= 4:
                    sp.wait_ge(S("h_sq"), t - 3)
                    sp.wait_ge(S("h_xn"), t - 3)
                src = x_tokens(t) if t < NT else dr["ctx"][(t - NT) * P:(t - NT + 1) * P, :]
                sp.dma_start(xring[t % 4], src).then_inc(S(f"x_in{t % 4}"), 16)
            for j in range(2):
                for i in (range(2, 5) if j == 0 else range(5, 8)):
                    load_w(sp, JOBS[i])
                sp.wait_ge(S("hy_ut"), 8 * j + 1)
                if j == 1:
                    sp.wait_ge(S("hy_done"), 1)
                for q in range(8):
                    if q >= 2:
                        sp.wait_ge(S("hy_s1m"), 8 * j + q - 1)
                    sp.dma_start(Fr2[q % 2][0:64], dr["Fm"][0:64, 4 * q:4 * q + 4, :]).then_inc(S(f"Fh{q % 2}"), 16)
                for q in range(8):
                    if q >= 2:
                        sp.wait_ge(S("hy_invb"), 8 * j + q - 1)
                    sp.dma_start(Gr[q % 2], dr["Gm"][:, 4 * q:4 * q + 4, :]).then_inc(S(f"Gh{q % 2}"), 16)
            for i in range(8, 12):
                load_w(sp, JOBS[i])
                if i == 8:
                    sp.wait_ge(S("rgw_clear"), 1)
                    for j in range(2):
                        for q in range(2):
                            sp.dma_start(rgw[64 * q:64 * q + 64, j, :, 64 * q:64 * q + 64],
                                         dr["rgw"][:, 2 * j + q].rearrange("g i j -> i g j")).then_inc(S("rgw_in"), 16)
            load_w(sp, J["q0"])
            load_w(sp, J["v0"])
            for h in range(NH):
                if h == 0:
                    sp.wait_ge(S("m_one"), 1)
                else:
                    sp.wait_ge(S("m_yo"), NT * h)
                sp.dma_start(GB, dr["gml"][:, P * h:P * h + P].broadcast_to([P, P])).then_inc(S("gb_in"), 16)
                load_w(sp, J[f"o{h}"])
                if h < NH - 1:
                    for nm in "kqv":
                        load_w(sp, J[f"{nm}{h + 1}"])
            last = JOBS[-1]
            sp.wait_ge(S("p_mm"), units_to_end(last))
            sp.wait_ge(S("mod25_st"), 32)
            sp.dma_start(m2bc, dr["mod25"][0:1, :].broadcast_to([P, D])).then_inc(S("m2_in"), 16)
            for k in range(KT):
                if k >= 4:
                    sp.wait_ge(S("wo_lo"), 2 * (k - 3))
                sp.dma_start(wos[k % 4], dr["w_out"][P * k:P * k + P, :]).then_inc(S(f"wo_in{k % 4}"), 16)
            for t in range(EARLY):
                sp.dma_start(x1(t), x_tokens(t)).then_inc(S("x1_in"), 16)
            sp.wait_ge(S("wo_lo"), 2 * KT)
            sp.wait_ge(S("m_ylo"), NT * NH)
            for t in range(EARLY, NT):
                sp.dma_start(x1(t), x_tokens(t)).then_inc(S("x1_rest_in"), 16)
            w1v = dr["mlp_w1"].rearrange("(k p) f -> p k f", p=P)
            w2v = dr["mlp_w2"].rearrange("(f p) d -> p f d", p=P)
            sp.dma_start(w1s, w1v[:, :, 0:FC]).then_inc(S("g_in1"), 16)
            sp.dma_start(w2s, w2v[:, 0:FT, :]).then_inc(S("g_in2"), 16)
            sp.dma_start(m5bc, dr["mod25"][1:2, :].broadcast_to([P, D])).then_inc(S("m5_in"), 16)
            sp.wait_ge(S("h_sq"), N5 + NT)
            sp.dma_start(fgbc, dr["final_g"].broadcast_to([P, D])).then_inc(S("fg_in"), 16)
            with sp.Fori(1, NFC) as c:
                sp.wait_ge(S("g_lo"), 2 * c - 1)
                sp.dma_start(w1s, w1v[:, :, bass.ds(c * FC, FC)]).then_inc(S("g_in1"), 16)
                sp.wait_ge(S("g_lo"), 2 * c)
                sp.dma_start(w2s, w2v[:, bass.ds(c * FT, FT), :]).then_inc(S("g_in2"), 16)
            ov = dr["out"].rearrange("(r c) d -> c r d", c=GW)
            for t in range(NT):
                sp.wait_ge(S("z_out"), t + 1)
                sp.dma_start(ov[4 * t:4 * t + 4], outb[t % 4]).then_inc(S(f"out_st{t % 4}"), 16)
            for i in range(4):
                sp.wait_ge(S(f"out_st{i}"), 16 * NT // 4)

        @block.scalar
        def _(act):
            ch = Chain(act, "act_chain")
            act.wait_ge(S("params_in"), 80)
            act.wait_ge(S("eps"), 1)
            act.activation(sct, col("cc", 0, 16), ACT.Tanh, scale=0.5).then_inc(S("ada_th"), 1)
            for lay in range(2):
                for b in range(NB):
                    act.wait_ge(S("f_red"), NB * lay + b + 1)
                    dst = (h1 if lay == 0 else h2)[:, b * BLK:(b + 1) * BLK]
                    act.activation(dst, red[2], ACT.Sin).then_inc(S("f_sin"), 1)
            act.wait_ge(S("filter_in"), 16 * 10)
            for n2 in range(FFT2):
                if n2 >= 2:
                    act.wait_ge(S("f_filt"), n2 - 1)
                act.activation(dec[n2 % 2], dbc, ACT.Exp, scale=col("negt", n2)).then_inc(S("f_dec"), 1)
                if n2 % 2 == 1 and n2 // 2 < 12:
                    b = n2 // 2
                    act.wait_ge(S("ada_mm"), b + 1)
                    act.activation(arow[0:2, b * BLK:(b + 1) * BLK], pb[0:2, b % 2, :], ACT.Copy).then_inc(S("ada_ev"), 1)
            for n2 in range(FFT2):
                act.wait_ge(S("f_s1"), n2 + 1)
                act.activation(X1f[:, :, n2], pb[:, 4 + n2 % 2, 0:HYW], ACT.Copy).then_inc(S("f_x1"), 1)
            for q in range(16):
                act.wait_ge(S("f_tr"), q + 1)
                act.activation(X1Tf[:, :, 4 * q:4 * q + 4, :].rearrange("p r g k -> p g r k"),
                               pb[:, 6 + q % 2, :].rearrange("p (g r k) -> p g r k", g=4, r=2), ACT.Copy
                               ).then_inc(S("f_x1t"), 1)
            def conv_in(k):
                act.wait_ge(S("p_mm"), k + 1)
                act.activation(to_rows(ZP[0][k % 2][:, 1:1 + L], k // 2), cr(pb[:, k % 2, :]), ACT.Copy,
                               scale=1 / WS).then_inc(S("p_ev"), 1)

            act.wait_ge(S("aff"), 1)
            for t in range(NTC + 2):
                if t < NTC:
                    act.wait_ge(S(f"x_in{t % 4}"), 16 * (t // 4 + 1))
                    if t >= 1:
                        act.wait_ge(S("h_sq"), t)
                    act.activation(junk, xring[t % 4], ACT.Square, accum_out=ssq[:, t:t + 1]).then_inc(S("h_sq"), 1)
                if t in (5, 9):
                    split_hi(act, t // 4 - 1)
                if t >= 10 and t % 2 == 0:
                    conv_in((t - 10) // 2)
                if t < 2:
                    continue
                u = t - 2
                act.wait_ge(S("h_tr"), u + 1)
                if u >= 2:
                    act.wait_ge(S("h_lo"), u - 1)
                w = 0 if u < NT else 1
                for k in range(KT // 2):
                    last = act.activation(hf[u % 2][:, k, :], pb[:, 2 + 2 * (u % 2), P * k:P * k + P],
                                          ACT.Identity, scale=affA[:, w, k:k + 1], bias=affB[:, w, k:k + 1])
                last.then_inc(S("h_aff"), 1)
            for k in range(5, 8):
                conv_in(k)
            split_hi(act, 2)
            split_hi(act, 3)
            def x1v_in(i, blocks):
                for b in blocks:
                    u = unit(JOBS[3 + i], b)
                    act.wait_ge(S("p_mm"), u + 1)
                    act.activation(to_rows(ZP[1][i][:, 1:1 + L], b), cr(pb[:, u % 2, :]), ACT.Copy,
                                   scale=1 / WS).then_inc(S("p_ev"), 1)

            def x0_in(j, blocks):
                for b in blocks:
                    u = unit(JOBS[3 * j + 2], b)
                    act.wait_ge(S("p_mm"), u + 1)
                    act.activation(to_rows(ZX, b), cr(pb[:, u % 2, :]), ACT.Copy, scale=1 / WS).then_inc(S("p_ev"), 1)

            def gate_in(jg, dst, blocks):
                for b in blocks:
                    u = unit(jg, b)
                    act.wait_ge(S("p_mm"), u + 1)
                    act.activation(to_rows(dst, b), cr(pb[:, u % 2, :]), ACT.Copy, scale=1 / WS).then_inc(S("p_ev"), 1)

            for j in range(2):
                x0_in(j, (0, 1))
                act.wait_ge(S("cv"), 3 * j + 2)
                for q in range(9):
                    if q < 8:
                        act.wait_ge(S("hy_utm"), 8 * j + q + 1)
                        act.activation(uT[0:64, 4 * q:4 * q + 4, :], pb[0:64, 2 + q % 2, :].rearrange("p (n c) -> p n c", n=4),
                                       ACT.Copy).then_inc(S("hy_ut"), 1)
                    if q >= 1:
                        v = q - 1
                        act.wait_ge(S("hy_s1m"), 8 * j + v + 1)
                        act.activation(X1[:, :, 4 * v:4 * v + 4].rearrange("p c n -> p n c"),
                                       pb[:, 4 + v % 2, :].rearrange("p (n c) -> p n c", n=4), ACT.Copy).then_inc(S("hy_x1"), 1)
                for q in range(8):
                    act.wait_ge(S("hy_trm"), 8 * j + q + 1)
                    act.activation(X1T[:, :, 4 * q:4 * q + 4, :].rearrange("p r g k -> p g r k"),
                                   pb[:, 2 + q % 2, :].rearrange("p (g r k) -> p g r k", g=4, r=2), ACT.Copy
                                   ).then_inc(S("hy_tr"), 1)
                x0_in(j, (2, 3))
                split_hi(act, 3 * j + 4)
                act.wait_ge(S("hy_y"), 4 * j + 4)
                for q in range(8):
                    act.wait_ge(S("hy_inva"), 8 * j + q + 1)
                    act.activation(Z[:, 16 * q:16 * q + 16, :].rearrange("p c n -> p (c n)"), pb[:, 2 + q % 2, :], ACT.Copy
                                   ).then_inc(S("hy_ze"), 1)
                for q in range(8):
                    act.wait_ge(S("hy_invb"), 8 * j + q + 1)
                    act.activation(yt[0:64, 4 * q:4 * q + 4, :], pb[0:64, 4 + q % 2, :].rearrange("p (n c) -> p n c", n=4),
                                   ACT.Copy).then_inc(S("hy_yt"), 1)
                following = x1v_in if j == 0 else lambda i, blocks: gate_in(J["rgg0"], GG[0], blocks)
                following(0, (0,))
                act.wait_ge(S("hy_yc"), j + 1)
                norm_act(act, CV, SQ, RS, j, lambda: following(0, (1,)))
                following(0, (2, 3))
                if j == 0:
                    split_hi(act, 5)
                    x1v_in(1, range(NB))
                    split_hi(act, 6)
            act.activation(sp_t[:, 0:4], col("rgl", 0, 4), ACT.Abs).then_inc(S("sp_a"), 1)
            act.wait_ge(S("sp_a"), 1)
            act.activation(sp_t[:, 4:8], sp_t[:, 0:4], ACT.Exp, scale=-1.0).then_inc(S("sp_a"), 1)

            def x_in(j, blocks):
                for b in blocks:
                    u = unit(J[f"rgx{j}"], b)
                    act.wait_ge(S("p_mm"), u + 1)
                    dst, src = ((to_rows(ZR[:, 1:1 + L], b), cr(pb[:, u % 2, :])) if b < NB else
                                (ZC[:, 1:1 + TC], pb[:, u % 2, 0:TC]))
                    act.activation(dst, src, ACT.Copy, scale=1 / WS).then_inc(S("p_ev"), 1)

            def keys(h, blocks):
                for b in blocks:
                    u = unit(J[f"k{h}"], b)
                    act.wait_ge(S("p_mm"), u + 1)
                    if b < NB:
                        dst, src = ZM[:, 1 + BLK * b:1 + BLK * b + BLK], pb[:, u % 2, :]
                    else:
                        dst, src = ZMC[:, 1:1 + TC], pb[:, u % 2, 0:TC]
                    act.activation(dst, src, ACT.Copy, scale=1 / WS).then_inc(S("p_ev"), 1)

            for j in range(2):
                jx, jg = J[f"rgx{j}"], J[f"rgg{j}"]
                if j == 0:
                    act.wait_ge(S("hy_done"), 2)
                    x_in(0, range(NB + 1))
                split_hi(act, jg["i"] + 2)
                split_hi(act, jx["i"] + 2)

                def fill(blocks):
                    if j == 0:
                        gate_in(J["rgg1"], GG[1], blocks)
                        return
                    for b in blocks:
                        u = unit(J["gates"], b)
                        act.wait_ge(S("p_mm"), u + 1)
                        dst, src = GT[:, rcols(b)], pb[:, u % 2, 0:BLK if b < NB else TC]
                        act.activation(dst, src, ACT.Identity, scale=1 / WS, bias=col("gb")).then_inc(S("p_ev"), 1)

                fill((0, 1))
                act.wait_ge(S("rg_cv"), 2 * j + 2)
                act.activation(HS[1][:, 0:L], GG[j], ACT.Square).then_inc(S("rg_g1"), 1)
                fill((2,))
                act.wait_ge(S("rg_g2"), j + 1)
                act.activation(HS[1][:, 0:L], HS[1][:, 0:L], ACT.Tanh, scale=math.sqrt(2 / math.pi)).then_inc(S("rg_g3"), 1)
                fill((3,) if j == 0 else (3, 4))
                act.wait_ge(S("rg_spl"), 1)
                if j:
                    act.wait_ge(S("rg_done"), 1)
                for d in range(2):
                    if d or j:
                        act.wait_ge(S("rg_scan"), 2 * j + d)
                    for x in range(NB + 1):
                        v, b = 10 * j + 5 * d + x, RORD[d][x]
                        n, c = (BLK if b < NB else TC), rcols(b)
                        act.wait_ge(S("rg_mm"), v + 1)
                        if v >= 2:
                            act.wait_ge(S("rg_th"), v - 1)
                            act.wait_ge(S("rg_om"), v - 1)
                        g = 4 * j + 2 * d
                        ch(act.activation(RT[:, v % 2, 0:n], pb[:, 2 + v % 2, 0:n], ACT.Tanh, scale=0.5, bias=rbh[:, g:g + 1]))
                        act.activation(TI[:, c], pb[:, 4 + v % 2, 0:n], ACT.Tanh, scale=0.5, bias=rbh[:, g + 1:g + 2]
                                       ).then_inc(S("rg_ev"), 1)
                        e = 2 * j + d
                        act.activation(RA[:, c], RT[:, v % 2, 0:n], ACT.Exp, scale=spl[:, e:e + 1], bias=spl[:, e:e + 1]
                                       ).then_inc(S("rg_a"), 1)
                        act.activation(TH[:, v % 2, 0:n], RT[:, v % 2, 0:n], ACT.Tanh, scale=nspl[:, e:e + 1],
                                       bias=nspl[:, e:e + 1]).then_inc(S("rg_th"), 1)
                    act.wait_ge(S("rg_om"), 10 * j + 5 * d + 5)
                    act.activation(OM, OM, ACT.Sqrt).then_inc(S("rg_sq"), 1)
                if j == 1:
                    split_hi(act, J["gates"]["i"] + 2)
                act.wait_ge(S("rg_y"), j + 1)
                following = (lambda b: x_in(1, b)) if j == 0 else (lambda b: keys(0, b))
                following((0,))
                norm_act(act, HS[0][:, 0:L], GG[j], OM[:, 0:L], 2 + j, lambda: following((1,)))
                if j == 0:
                    x_in(1, range(2, NB + 1))
            act.wait_ge(S("p_ev"), units_to_end(J["gates"]))
            ch(act.activation(LN, GT, ACT.Abs))
            ch(act.activation(LN, LN, ACT.Exp, scale=-1.0))
            act.activation(LN, LN, ACT.Ln, bias=1.0).then_inc(S("r_ln"), 1)

            keys(0, range(2, NB + 1))
            split_hi(act, J["k0"]["i"] + 2)
            act.wait_ge(S("r_m"), 1)
            act.activation(AR[0:64, :], AR[0:64, :], ACT.Exp).then_inc(S("r_ar"), 1)
            act.activation(LF[0:64], MM[0:64], ACT.Exp, scale=-1.0)
            act.activation(R1[64:128], LN[0:64], ACT.Exp)
            act.activation(CW[64:128], RR[0:64], ACT.Exp).then_inc(S("r_rows"), 1)
            def wo_hi(i):
                k, c = wo_half(i)
                act.wait_ge(S("wo_m"), i + 1)
                act.activation(wop[:, k, 0, c], wos[k % 4][:, c], ACT.Copy, scale=WS).then_inc(S("wo_hi"), 1)

            for h in range(NH):
                jq, jk, jv, jo = (J[f"{nm}{h}"] for nm in "qkvo")
                if h:
                    keys(h, range(NB + 1))
                    split_hi(act, jk["i"] + 2)
                act.wait_ge(S("m_cv"), 3 * h + 1)
                for b in range(NB):
                    u = unit(jq, b)
                    act.wait_ge(S("p_mm"), u + 1)
                    act.activation(ZM[:, 1 + BLK * b:1 + BLK * b + BLK], pb[:, u % 2, :], ACT.Copy, scale=1 / WS
                                   ).then_inc(S("p_ev"), 1)
                    if b == 0:
                        act.wait_ge(S("m_cv"), 3 * h + 2)
                        act.activation(TK, KX, ACT.Tanh, scale=0.5).then_inc(S("m_th"), 1)
                split_hi(act, jq["i"] + 2)

                def values(b):
                    u, nn = unit(jv, b), (4 if b < NB else 2)
                    act.wait_ge(S("p_mm"), u + 1)
                    act.activation(V1[:, 4 * b:4 * b + nn, 0:DH], pb[:, u % 2, 0:P * nn].rearrange("p (n c) -> p n c", n=nn),
                                   ACT.Copy, scale=1 / WS).then_inc(S("p_ev"), 1)

                act.wait_ge(S("m_ones"), h + 1)
                values(4)
                values(3)
                act.wait_ge(S("m_cv"), 3 * h + 3)
                act.activation(ZM[:, 0:L], QT, ACT.Tanh, scale=0.5).then_inc(S("m_th"), 1)
                values(2)
                act.wait_ge(S("m_silu"), 2 * h + 2)

                def kw(it, n, g):
                    act.wait_ge(S("m_kt"), it + 1)
                    if it >= 2:
                        act.wait_ge(S("m_cl"), it - 1)
                    act.activation(KW[it % 2], pb[:, kbank(it), 0:P], ACT.Identity, scale=CC[:, n, g + h:g + h + 1]
                                   ).then_inc(S("m_kw"), 1)

                def gate(m, dst):
                    act.wait_ge(S("p_mm"), jo["p0"] + m + 1)
                    act.activation(dst, pb[:, 1, 0:P], ACT.Tanh, scale=0.5 / WS).then_inc(S("p_ev"), 1)

                for x in range(17):
                    kw(ITS * h + x, BWD[x], 12)
                    if x in (6, 10):
                        values(1 if x == 6 else 0)
                    if x == 10:
                        split_hi(act, jv["i"] + 2)
                    if h == NH - 1 and x >= 11:
                        for m in range(2 * (x - 11), 2 * (x - 11) + 2 if x < 16 else NT):
                            gate(m, OS[:, m, :])

                def decays(n):
                    cn = NT * h + n
                    act.wait_ge(S("m_A"), cn + 1)
                    if cn >= 1:
                        act.wait_ge(S("m_S"), cn)
                    for d in range(2):
                        ins = act.activation(E2[d], pb[:, 6 + cn % 2, P * d:P * d + P], ACT.Exp,
                                             bias=CC[:, n, 4 * d + h:4 * d + h + 1])
                    ins.then_inc(S("m_E"), 1)

                decays(0)
                for y in range(2):
                    kw(ITS * h + 17 + y, FWD[y], 8)
                for n in range(NT + 3):
                    cn = NT * h + n
                    if 1 <= n < NT:
                        decays(n)
                    if n < NT - 1:
                        kw(ITS * h + 19 + n, n, 8)
                    if n >= 3:
                        m, cm = n - 3, cn - 3
                        act.wait_ge(S("m_yt"), cm + 1)
                        act.activation(yT[:, 2 + h, 0, P * m:P * m + P], pb[:, 0, 0:P], ACT.Copy
                                       ).then_inc(S("m_yhi"), 1)
                    if 2 <= n < NT + 2 and h < NH - 1:
                        if cn >= 3:
                            act.wait_ge(S("m_yo"), cn - 2)
                        gate(n - 2, OT)
                    if 1 <= n <= NT:
                        cm = cn - 1
                        act.wait_ge(S("m_hs"), cm + 1)
                        if cm >= 1:
                            act.wait_ge(S("m_sq"), cm)
                        if cm >= 2:
                            act.wait_ge(S("m_rs"), cm - 1)
                        act.activation(JK, HM[cm % 2], ACT.Square, accum_out=MS[:, cm % 2, 0:1]).then_inc(S("m_sq"), 1)
                    if h == NH - 1 and n >= 3:
                        wo_hi(n - 3)
                split_hi(act, jo["i"] + 2)
            def w1_hi(c, sl):
                act.wait_ge(S("g_in1"), 16 * c + 16)
                act.activation(w1p[sl][:, :, 0, :], w1s, ACT.Copy, scale=WS).then_inc(S("g_hi"), 1)

            def w2_hi(c, sl):
                act.wait_ge(S("g_m5"), c + 1)
                act.activation(w2p[sl][:, :, 0, :], w2s, ACT.Copy, scale=WS).then_inc(S("g_hi"), 1)

            for t in range(NT + 2):
                if t < NT:
                    act.wait_ge(S("o_x1"), t + 1)
                    if t >= 1:
                        act.wait_ge(S("h_sq"), N5 + t)
                    act.activation(junk2, x1(t), ACT.Square, accum_out=ssq2[:, t:t + 1]).then_inc(S("h_sq"), 1)
                if t >= 2:
                    u = t - 2
                    act.wait_ge(S("h_tr"), N5 + u + 1)
                    if u >= 2:
                        act.wait_ge(S("h_lo"), N5 + u - 1)
                    for k in range(KT):
                        ins = act.activation(hf2[u % 2][:, k, :], pb[:, 4 + 2 * (u % 2) + k // 4, P * (k % 4):P * (k % 4) + P],
                                             ACT.Identity, scale=affA[:, 2, k:k + 1], bias=affB[:, 2, k:k + 1])
                    ins.then_inc(S("h_aff"), 1)
                    if t == NT:
                        act.wait_ge(S("o_mm"), NT)
                        w1_hi(0, 0)

            w2_hi(0, 0)
            act.wait_ge(S("h_lo"), N5 + NT)

            def act_units(it, last=False):
                for i in range(8):
                    c, tb = 2 * it + i // 4, i % 4
                    for f in range(FT):
                        n = (c * 4 + tb) * FT + f
                        act.wait_ge(S("g_mm1"), n + 1)
                        act.wait_ge(S("a_lo"), n + 1)
                        act.activation(act_r[:, f, :], pb[:, 2 * (tb % 2) + f, :], ACT.Relu, scale=math.sqrt(AS) / WS
                                       ).then_inc(S("a_r"), 1)
                        act.wait_ge(S("a_r"), n + 1)
                        act.activation(act_p[tb % 2][:, f, 0, :], act_r[:, f, :], ACT.Square).then_inc(S("a_hi"), 1)
                    if tb == 1 and not (last and i // 4 == 1):
                        w1_hi(c + 1, (i // 4 + 1) % 2)
                        w2_hi(c + 1, (i // 4 + 1) % 2)
                    if last and i >= 6:
                        final_sq(tb - 2)

            def final_sq(tb):
                act.wait_ge(S("acc"), 4 + 8 * (4 * (NFC - 1) + tb + 1))
                for t in range(4 * tb, 4 * tb + 4):
                    if t >= 1:
                        act.wait_ge(S("h_sq"), N7 + t)
                    act.activation(junk_f[t % 2], x1(t), ACT.Square, accum_out=ssq2[:, t:t + 1]).then_inc(S("h_sq"), 1)

            with act.Fori(0, (NFC - NPEEL) // 2) as it:
                act_units(it)
            act_units((NFC - NPEEL) // 2, last=True)
            final_sq(2)
            final_sq(3)

        @block.gpsimd
        def _(pool):
            pool.memset(view(80, [256 + 256]), 0.0).then_inc(S("w_zeroed"), 1)
            pool.memset(eps_c[:], EPS).then_inc(S("eps"), 1)
            for n2 in range(FFT2):
                pool.wait_ge(S("f_raw"), n2 + 1)
                pool.wait_ge(S("f_dec"), n2 + 1)
                pool.tensor_tensor(filt[:, :, n2], ftmp[n2 % 2], dec[n2 % 2], ALU.mult).then_inc(S("f_filt"), 1)
            pool.memset(mhalf[:], -0.5).then_inc(S("mhalf"), 1)
            pool.wait_ge(S("mhalf"), 1)
            for t in range(NTC):
                pool.wait_ge(S("h_ms"), t + 1)
                pool.tensor_tensor(rst[:, t:t + 1], ssq[:, t:t + 1], mhalf[:], ALU.pow).then_inc(S("h_rs"), 1)
            pool.wait_ge(S("hy_y"), 8)
            pool.memset(view(115, [4 * KB]), 0.0).then_inc(S("rgw_clear"), 1)
            for cn in range(NT * NH):
                pool.wait_ge(S("m_ms"), cn + 1)
                if cn >= 2:
                    pool.wait_ge(S("m_yo"), cn - 1)
                pool.tensor_tensor(MS[:, cn % 2, 2:3], MS[:, cn % 2, 1:2], mhalf[:], ALU.pow).then_inc(S("m_rs"), 1)
                i = cn - NT * (NH - 1)
                if i >= 0:
                    k, c = wo_half(i)
                    if i == 0:
                        pool.wait_ge(S("m2_in"), 16)
                    pool.wait_ge(S(f"wo_in{k % 4}"), 16 * (k // 4 + 1))
                    pool.tensor_tensor(wos[k % 4][:, c], wos[k % 4][:, c], m2bc[:, c], ALU.mult).then_inc(S("wo_m"), 1)
            for t in range(NT):
                pool.wait_ge(S("h_ms"), N5 + t + 1)
                pool.tensor_tensor(rst2[:, t:t + 1], ssq2[:, t:t + 1], mhalf[:], ALU.pow).then_inc(S("h_rs"), 1)

            def mlp_gate(c):
                pool.wait_ge(S("g_in2"), 16 * c + 16)
                for f in range(FT):
                    ins = pool.tensor_tensor(w2s[:, f, :], w2s[:, f, :], m5bc, ALU.mult)
                ins.then_inc(S("g_m5"), 1)

            pool.wait_ge(S("m5_in"), 16)
            mlp_gate(0)

            def pool_units(it, last=False):
                for i in range(8):
                    c, tb = 2 * it + i // 4, i % 4
                    for f in range(FT):
                        n = (c * 4 + tb) * FT + f
                        pool.wait_ge(S("a_r"), n + 1)
                        pool.tensor_tensor(act_a[:, f, :], act_r[:, f, :], act_r[:, f, :], ALU.mult).then_inc(S("a_sq"), 1)
                    if tb == 0 and not (last and i // 4 == 1):
                        mlp_gate(c + 1)
                    if last and i >= 6:
                        final_rs(tb - 2)

            def final_rs(tb):
                pool.wait_ge(S("h_ms"), N7 + tb + 1)
                pool.tensor_tensor(rst2[:, 4 * tb:4 * tb + 4], ssq2[:, 4 * tb:4 * tb + 4],
                                   mhalf[:].broadcast_to([P, 4]), ALU.pow).then_inc(S("h_rs"), 1)

            with pool.Fori(0, (NFC - NPEEL) // 2) as it:
                pool_units(it)
            pool_units((NFC - NPEEL) // 2, last=True)
            for tb in range(2, NB):
                final_rs(tb)

        @block.vector
        def _(dve):
            ch = Chain(dve, "dve_chain")
            dve.wait_ge(S("params_in"), 80)
            ch(dve.tensor_copy(identb[:], ident[:]))
            ch(dve.tensor_copy(maskneg[:], mask_in))
            dve.wait_ge(S("ada_th"), 1)
            ch(dve.scalar_tensor_tensor(scs, sct, 1.0, col("cc", 0, 16), ALU.add, ALU.mult))
            dve.tensor_scalar(scs, scs, 0.5, None, ALU.mult).then_inc(S("ada_c"), 1)
            for lay in range(2):
                for b in range(NB):
                    dve.wait_ge(S("f_mm"), NB * lay + b + 1)
                    arg, kk = red[0], red[1]
                    if NB * lay + b >= 1:
                        dve.wait_ge(S("f_red"), NB * lay + b)
                    ch(dve.tensor_scalar(arg, pb[:, 4 + b % 2, :], col("ffn", 2 * lay), col("ffn", 2 * lay + 1),
                                         ALU.add, ALU.mult))
                    ch(dve.tensor_scalar(kk, arg, 1.0 / (2 * math.pi), MAGIC, ALU.mult, ALU.add))
                    ch(dve.tensor_scalar(kk, kk, MAGIC, None, ALU.subtract))
                    for part in (6.28125, 0.0019350051879882812, 3.0199159819567e-07):
                        ch(dve.scalar_tensor_tensor(arg, kk, -part, arg, ALU.mult, ALU.add))
                    if NB * lay + b >= 1:
                        dve.wait_ge(S("f_sin"), NB * lay + b)
                    dve.tensor_scalar(red[2], arg, 3.1415925, -3.1415925, ALU.min, ALU.max).then_inc(S("f_red"), 1)
            for n2 in range(FFT2):
                dve.wait_ge(S("f_h3"), n2 + 1)
                if n2 >= 2:
                    dve.wait_ge(S("f_filt"), n2 - 1)
                dve.tensor_tensor(ftmp[n2 % 2], pb[:, 6 + n2 % 2, 0:HYW], b3bc, ALU.add).then_inc(S("f_raw"), 1)
            dve.wait_ge(S("adab_in"), 16)
            dve.wait_ge(S("ada_ev"), 12)
            for i, r in enumerate((2, 5)):
                a = arow[0:1, r * D:(r + 1) * D]
                dve.tensor_tensor(a, a, adab_row[0:1, i, :], ALU.add).then_inc(S("ada_row"), 1)
            for q in range(16):
                dve.wait_ge(S("f_s2"), q + 1)
                dve.tensor_copy(Fsp[:, q % 2, 8 * (q // 2):8 * (q // 2) + 8, :],
                                pb[:, 2 + q % 2, :].rearrange("p (g k) -> p g k", g=8)).then_inc(S("f_spec"), 1)
            dve.wait_ge(S("ada_tr"), 1)
            ch(dve.tensor_copy(modT[:], pb[:, 7, 0:64].rearrange("p (a b) -> p a b", b=2)))
            mb = cols[:, COLS["adab"][0]:COLS["adab"][0] + 32].rearrange("p (a b) -> p a b", b=1)
            dve.tensor_tensor(modT[:], modT[:], mb.broadcast_to([P, 32, 2]), ALU.add).then_inc(S("adaT"), 1)
            dve.wait_ge(S("adaT"), 1)
            for w, (g, sc, sh, r) in enumerate((("n1g", 8, 0, 0), ("n1g", 8, 0, 1), ("n2g", 24, 16, 0))):
                ch(dve.scalar_tensor_tensor(affA[:, w, :], modT[:, sc:sc + KT, r], 1.0, col(g, 0, KT), ALU.add, ALU.mult))
                ch(dve.tensor_copy(affB[:, w, :], modT[:, sh:sh + KT, r]))
            dve.memset(rst[:], 0.0).then_inc(S("aff"), 1)
            dve.wait_ge(S("mod25_st"), 32)
            for t in range(NTC + 3):
                if t < NTC:
                    dve.wait_ge(S("h_sq"), t + 1)
                    dve.tensor_scalar(ssq[:, t:t + 1], ssq[:, t:t + 1], 1.0 / D, EPS, ALU.mult, ALU.add).then_inc(S("h_ms"), 1)
                if 1 <= t <= NTC:
                    u = t - 1
                    dve.wait_ge(S("h_rs"), u + 1)
                    if u >= 2:
                        dve.wait_ge(S("h_tr"), u - 1)
                    dve.tensor_scalar(xnrm[u % 2], xring[u % 4], rst[:, u:u + 1], None, ALU.mult).then_inc(S("h_xn"), 1)
                if 2 <= t < NTC + 2:
                    u = t - 2
                    dve.wait_ge(S("h_tr"), u + 1)
                    if u >= 2:
                        dve.wait_ge(S("h_lo"), u - 1)
                    w = 0 if u < NT else 1
                    for k in range(KT // 2, KT):
                        ins = dve.tensor_scalar(hf[u % 2][:, k, :], pb[:, 3 + 2 * (u % 2), P * (k - 4):P * (k - 4) + P],
                                                affA[:, w, k:k + 1], affB[:, w, k:k + 1], ALU.mult, ALU.add)
                    ins.then_inc(S("h_aff_hi"), 1)
                if t >= 3:
                    u = t - 3
                    dve.wait_ge(S("h_aff_hi"), u + 1)
                    dve.wait_ge(S("h_aff"), u + 1)
                    c = slice(P * u, P * u + P)
                    ch(dve.tensor_copy(hT[:, :, 0, c], hf[u % 2]))
                    dve.tensor_tensor(hT[:, :, 1, c], hf[u % 2], hT[:, :, 0, c], ALU.subtract).then_inc(S("h_lo"), 1)
                if t in (5, 9):
                    split_lo(dve, t // 4 - 1)
            split_lo(dve, 2)

            def conv(dst, taps, wc, zz, n=L):
                ch(dve.memset(zz[:, 0:1], 0.0))
                ch(dve.memset(zz[:, 1 + n:3 + n], 0.0))
                ch(dve.tensor_scalar(dst, zz[:, 0:n], wc[:, 0:1], None, ALU.mult))
                for k in range(1, taps):
                    ins = dve.scalar_tensor_tensor(dst, zz[:, k:k + n], wc[:, k:k + 1], dst, ALU.mult, ALU.add)
                    if k < taps - 1:
                        ch(ins)
                return ins

            for j in range(2):
                for i, (dst, wt) in enumerate(((U, 2 + j), (X0, 4 + j))):
                    jb = JOBS[3 * j + i]
                    if j == 1:
                        split_lo(dve, jb["i"] + 2)
                    dve.wait_ge(S("p_ev"), units_to_end(jb))
                    conv(dst, 3, col("hyc", 3 * wt, 3), ZP[j][i]).then_inc(S("cv"), 1)
                    dve.wait_ge(S("cv"), 3 * j + i + 1)
                dve.tensor_tensor(U, U, X0, ALU.mult).then_inc(S("u_ready"), 1)
                if j == 0:
                    split_lo(dve, 3)
                for q in range(8):
                    dve.wait_ge(S("hy_s2m"), 8 * j + q + 1)
                    dve.tensor_copy(US[:, q % 2, 8 * (q // 2):8 * (q // 2) + 8, :],
                                    pb[:, 4 + q % 2, :].rearrange("p (g k) -> p g k", g=8)).then_inc(S("hy_s2e"), 1)
                dve.wait_ge(S("hy_s2e"), 8 * j + 8)
                v3 = lambda a: a.rearrange("p (g k) -> p g k", g=8)
                for gb in range(4):
                    g, gf = slice(8 * gb, 8 * gb + 8), slice(32 * j + 8 * gb, 32 * j + 8 * gb + 8)
                    ur, ui, fr, fi = US[:, 0, g, :], US[:, 1, g, :], Fsp[:, 0, gf, :], Fsp[:, 1, gf, :]
                    if gb:
                        dve.wait_ge(S("hy_y"), 4 * j + gb)
                    else:
                        dve.wait_ge(S("hy_s1m"), 8 * j + 8)
                    ch(dve.tensor_tensor(v3(tP), ur, fr, ALU.mult))
                    ch(dve.tensor_tensor(v3(tQ), ui, fi, ALU.mult))
                    ch(dve.tensor_tensor(Y3[:, g, 1, :], v3(tP), v3(tQ), ALU.subtract))
                    ch(dve.tensor_tensor(v3(tP), ur, fi, ALU.mult))
                    ch(dve.tensor_tensor(v3(tQ), ui, fr, ALU.mult))
                    ch(dve.tensor_tensor(Y3[:, g, 2, :], v3(tP), v3(tQ), ALU.add))
                    dve.scalar_tensor_tensor(Y3[:, g, 0, :], v3(tP), -1.0, v3(tQ), ALU.mult, ALU.subtract
                                             ).then_inc(S("hy_y"), 1)
                split_lo(dve, 3 * j + 4)
                dve.wait_ge(S("p_ev"), units_to_end(JOBS[3 * j + 2]))
                dve.wait_ge(S("u_ready"), j + 1)
                wc = col("hyc", 3 * j, 3)
                ch(dve.tensor_scalar(X0, ZX, wc[:, 1:2], None, ALU.mult))
                ch(dve.scalar_tensor_tensor(X0[:, 1:L], ZX[:, 0:L - 1], wc[:, 0:1], X0[:, 1:L], ALU.mult, ALU.add))
                dve.scalar_tensor_tensor(X0[:, 0:L - 1], ZX[:, 1:L], wc[:, 2:3], X0[:, 0:L - 1], ALU.mult, ALU.add
                                         ).then_inc(S("cv"), 1)
                dve.wait_ge(S("cv"), 3 * j + 3)
                for q in range(4):
                    dve.wait_ge(S("hy_trb"), 4 * j + q + 1)
                    pv = lambda a: a.rearrange("p (a b) -> p b a", b=FFT2)[:, 8 * q:8 * q + 8, :]
                    dve.scalar_tensor_tensor(pv(CV), pv(U), col("hyb", j), pb[:, 2 + q % 2, :].rearrange("p (n a) -> p n a", n=8),
                                             ALU.mult, ALU.add).then_inc(S("hy_cv"), 1)
                dve.wait_ge(S("hy_cv"), 4 * j + 4)
                dve.tensor_tensor(CV, CV, X0, ALU.mult).then_inc(S("hy_yc"), 1)
                dve.wait_ge(S("hy_yc"), j + 1)
                norm_dve(dve, ch, CV, RS, YF, j, j).then_inc(S("hy_done"), 1)
                dve.wait_ge(S("hy_done"), j + 1)
            dve.wait_ge(S("sp_a"), 2)
            e, z, z2, pp = sp_t[:, 4:8], sp_t[:, 8:12], sp_t[:, 12:16], sp_t[:, 0:4]
            ch(dve.tensor_scalar(z, e, 2.0, None, ALU.add))
            ch(dve.reciprocal(z, z))
            ch(dve.tensor_tensor(z, z, e, ALU.mult))
            ch(dve.tensor_tensor(z2, z, z, ALU.mult))
            ch(dve.tensor_scalar(pp, z2, 1.0 / 17, None, ALU.mult))
            for k in (15, 13, 11, 9, 7, 5, 3):
                ch(dve.scalar_tensor_tensor(pp, pp, 1.0 / k, z2, ALU.add, ALU.mult))
            ch(dve.scalar_tensor_tensor(pp, pp, 1.0, z, ALU.add, ALU.mult))
            ch(dve.tensor_scalar(z, col("rgl", 0, 4), -1.0, 0.0, ALU.mult, ALU.max))
            ch(dve.scalar_tensor_tensor(z, pp, 2.0, z, ALU.mult, ALU.add))
            ch(dve.tensor_scalar(spl[:], z, -4.0, None, ALU.mult))
            ch(dve.tensor_scalar(nspl[:], z, 4.0, None, ALU.mult))
            dve.tensor_scalar(rbh[:], col("rgb", 0, 8), 0.5, None, ALU.mult).then_inc(S("rg_spl"), 1)
            for j in range(2):
                jx, jg = J[f"rgx{j}"], J[f"rgg{j}"]
                dve.wait_ge(S("p_ev"), jx["p0"] + jx["n"])
                wc = col("rgc", 4 * j, 4)
                conv(XR[:, 0:L], 4, wc, ZR).then_inc(S("rg_cv"), 1)
                conv(XR[:, L:LT], 4, wc, ZC, n=TC).then_inc(S("rg_cv"), 1)
                split_lo(dve, jg["i"] + 2)
                split_lo(dve, jx["i"] + 2)
                g2 = HS[1][:, 0:L]
                dve.wait_ge(S("rg_g1"), j + 1)
                ch(dve.tensor_scalar(g2, g2, 0.044715, 1.0, ALU.mult, ALU.add))
                dve.tensor_tensor(g2, g2, GG[j], ALU.mult).then_inc(S("rg_g2"), 1)
                dve.wait_ge(S("rg_g3"), j + 1)
                ch(dve.scalar_tensor_tensor(GG[j], g2, 1.0, GG[j], ALU.add, ALU.mult))
                for d in range(2):
                    for x in range(NB + 1):
                        v, b = 10 * j + 5 * d + x, RORD[d][x]
                        n, c = (BLK if b < NB else TC), rcols(b)
                        dve.wait_ge(S("rg_a"), v + 1)
                        ch(dve.tensor_tensor(A2[:, 0:n], RA[:, c], RA[:, c], ALU.mult))
                        dve.wait_ge(S("rg_th"), v + 1)
                        dve.scalar_tensor_tensor(OM[:, c], A2[:, 0:n], 1.0, TH[:, v % 2, 0:n], ALU.add, ALU.mult
                                                 ).then_inc(S("rg_om"), 1)
                        dve.wait_ge(S("rg_om"), v + 1)
                        ch(dve.scalar_tensor_tensor(TI[:, c], TI[:, c], 1.0, XR[:, c], ALU.add, ALU.mult))
                    dve.wait_ge(S("rg_sq"), 2 * j + d + 1)
                    ch(dve.scalar_tensor_tensor(OM, OM, 0.5, TI, ALU.mult, ALU.mult))
                    hs, rv = HS[d], (lambda a: a) if d == 0 else (lambda a: a[:, ::-1])
                    ch(dve.tensor_tensor_scan(rv(hs[:, L:LT]), rv(RA[:, L:LT]), rv(OM[:, L:LT]), 0.0, ALU.mult, ALU.add))
                    at = LT - 1 if d == 0 else L
                    dve.tensor_tensor_scan(rv(hs[:, 0:L]), rv(RA[:, 0:L]), rv(OM[:, 0:L]), hs[:, at:at + 1],
                                           ALU.mult, ALU.add).then_inc(S("rg_scan"), 1)
                    dve.wait_ge(S("rg_scan"), 2 * j + d + 1)
                h0 = HS[0][:, 0:L]
                ch(dve.tensor_tensor(h0, h0, HS[1][:, 0:L], ALU.add))
                dve.scalar_tensor_tensor(h0, h0, 0.5, GG[j], ALU.mult, ALU.mult).then_inc(S("rg_y"), 1)
                dve.wait_ge(S("rg_y"), j + 1)
                norm_dve(dve, ch, h0, OM[:, 0:L], TI[:, 0:L], 2 + j, 2 + j).then_inc(S("rg_done"), 1)
                dve.wait_ge(S("rg_done"), j + 1)
            split_lo(dve, J["gates"]["i"] + 2)
            ch(dve.memset(RR[0:64], 1.0))
            ch(dve.memset(RR[0:32, 0:LT:P], 0.0))
            ch(dve.memset(RR[32:64, P - 1:LT:P], 0.0))
            dve.wait_ge(S("r_ln"), 1)
            ch(dve.scalar_tensor_tensor(LF[0:64], GT[64:128], 0.0, LN[64:128], ALU.min, ALU.subtract))
            for d in range(2):
                r = slice(32 * d, 32 * d + 32)
                rv = (lambda a: a) if d == 0 else (lambda a: a[:, ::-1])
                ch(dve.tensor_tensor_scan(rv(MM[r, L:LT]), rv(LF[r, L:LT]), rv(GT[r, L:LT]), 0.0, ALU.add, ALU.max))
                at = LT - 1 if d == 0 else L
                ch(dve.tensor_tensor_scan(rv(MM[r, 0:L]), rv(LF[r, 0:L]), rv(GT[r, 0:L]), MM[r, at:at + 1],
                                          ALU.add, ALU.max))
                ch(dve.tensor_tensor_scan(rv(BB[r]), rv(RR[r]), rv(LF[r]), 0.0, ALU.mult, ALU.add))
            ch(dve.tensor_tensor(CW[0:64], GT[0:64], BB[0:64], ALU.subtract))
            ch(dve.tensor_tensor(R1[0:64], BB[0:64], MM[0:64], ALU.subtract))
            f, b = slice(0, 32), slice(32, 64)
            ch(dve.memset(M0[0:64, :], 0.0))
            ch(dve.tensor_copy(M0[f, 1:NT], MM[f, P - 1:P * (NT - 1):P]))
            ch(dve.tensor_copy(M0[f, 0:1], MM[f, LT - 1:LT]))
            ch(dve.tensor_copy(M0[f, 17:18], MM[f, L + P - 1:L + P]))
            ch(dve.tensor_copy(M0[b, 0:NT - 1], MM[b, P:L:P]))
            ch(dve.tensor_copy(M0[b, NT - 1:NT], MM[b, L:L + 1]))
            ch(dve.tensor_copy(M0[b, 16:17], MM[b, L + P:L + P + 1]))
            ch(dve.tensor_copy(NL[f, :], R1[f, P - 1:LT:P]))
            ch(dve.tensor_copy(NL[b, :], R1[b, 0:LT:P]))
            ch(dve.tensor_tensor(AR[0:64, :], M0[0:64, :], NL[0:64, :], ALU.add))
            v = lambda a: a.rearrange("p (n t) -> p n t", t=P)
            bc = lambda a: a[0:64, :].rearrange("p (n t) -> p n t", t=1).broadcast_to([64, NTC, P])
            ch(dve.tensor_tensor(v(LN[0:64]), v(R1[0:64]), bc(M0), ALU.add))
            dve.tensor_tensor(v(RR[0:64]), v(CW[0:64]), bc(NL), ALU.add).then_inc(S("r_m"), 1)
            dve.wait_ge(S("r_bc"), 1)
            dve.tensor_copy(AB[:].rearrange("p d h n -> p (d h n)"), pb[:, 6, 0:2 * NH * NTC]).then_inc(S("r_ab"), 1)
            for n in range(NTC):
                dve.wait_ge(S("r_tr"), n + 1)
                dve.tensor_copy(CC[:, n, :].rearrange("p (g h) -> p g h", g=4),
                                pb[:, 2 + n % 2, 0:P].rearrange("p (g h) -> p g h", g=4)[:, :, 0:NH])
                dve.tensor_copy(EM[:, n, :].rearrange("p (g h) -> p g h", g=2),
                                pb[:, 2 + n % 2, P:P + 64].rearrange("p (g h) -> p g h", g=2)[:, :, 0:NH]
                                ).then_inc(S("r_cc"), 1)
            dve.memset(V1[:, :, DH:DH + 1], 1.0).then_inc(S("m_one"), 1)
            def wo_lo(i):
                k, c = wo_half(i)
                dve.wait_ge(S("wo_hi"), i + 1)
                dve.scalar_tensor_tensor(wop[:, k, 1, c], wos[k % 4][:, c], WS, wop[:, k, 0, c], ALU.mult, ALU.subtract
                                         ).then_inc(S("wo_lo"), 1)

            for h in range(NH):
                jq, jk, jv, jo = (J[f"{nm}{h}"] for nm in "qkvo")
                dve.wait_ge(S("p_ev"), units_to_end(jk))
                if h:
                    dve.wait_ge(S("m_ylo"), NT * h)
                wc = col("mlc", 4 * (NH + h), 4)
                conv(KX[:, 0:L], 4, wc, ZM).then_inc(S("m_cv"), 1)
                conv(KX[:, L:LT], 4, wc, ZMC, n=TC).then_inc(S("m_cv"), 1)
                split_lo(dve, jk["i"] + 2)
                dve.wait_ge(S("m_th"), 2 * h + 1)
                dve.scalar_tensor_tensor(KX, TK, 1.0, KX, ALU.add, ALU.mult).then_inc(S("m_silu"), 1)
                dve.wait_ge(S("m_silu"), 2 * h + 1)
                dve.memset(V1[:, :, DH:DH + 1], 1.0).then_inc(S("m_ones"), 1)
                dve.wait_ge(S("p_ev"), units_to_end(jq))
                conv(QT, 4, col("mlc", 4 * h, 4), ZM).then_inc(S("m_cv"), 1)
                split_lo(dve, jq["i"] + 2)
                dve.wait_ge(S("m_th"), 2 * h + 2)
                dve.scalar_tensor_tensor(QT, ZM[:, 0:L], 1.0, QT, ALU.add, ALU.mult).then_inc(S("m_silu"), 1)
                dve.wait_ge(S("m_silu"), 2 * h + 2)

                def cl(it):
                    dve.wait_ge(S("m_cl"), it + 1)
                    if it >= 1:
                        dve.wait_ge(S("m_st"), it)
                    return pb[:, kbank(it), P:P + DH + 1]

                def state(it, dst, src, d, n):
                    part = cl(it)
                    if src is None:
                        dve.tensor_copy(dst, part).then_inc(S("m_st"), 1)
                    else:
                        dve.scalar_tensor_tensor(dst, src, AB[:, d, h, n:n + 1], part, ALU.mult, ALU.add
                                                 ).then_inc(S("m_st"), 1)

                i0 = ITS * h
                for x in range(17):
                    if x == 0 and h:
                        dve.wait_ge(S("m_out"), NT * h)
                    n = BWD[x]
                    state(i0 + x, CF[0] if x == 0 else CB[:, 15 if x == 1 else n - 1, :],
                          None if x == 0 else CF[0] if x == 1 else CB[:, n, :], 1, n)
                    if x == 10:
                        split_lo(dve, jv["i"] + 2)

                def weights(n):
                    cn = NT * h + n
                    c = slice(P * n, P * n + P)
                    dve.wait_ge(S("m_E"), cn + 1)
                    if cn >= 2:
                        dve.wait_ge(S("m_out"), cn - 1)
                    for d in range(2):
                        dve.scalar_tensor_tensor(S2[cn % 2][d], pb[:, 3, 0:P], QF, E2[d], ALU.mult, ALU.mult)
                    for d in range(2):
                        ins = dve.scalar_tensor_tensor(QW[cn % 2][d], pb[:, 6 + cn % 2, P * (2 + d):P * (3 + d)], QF,
                                                       QT[:, c], ALU.mult, ALU.mult)
                    ins.then_inc(S("m_S"), 1)

                weights(0)
                for y in range(2):
                    state(i0 + 17 + y, CF[y], None if y == 0 else CF[0], 0, FWD[y])
                for n in range(NT + 3):
                    cn = NT * h + n
                    if 1 <= n < NT:
                        weights(n)
                    if 1 <= n <= NT:
                        m, cm = n - 1, cn - 1
                        bk, hm = 4 + cm % 2, HM[cm % 2]
                        dve.wait_ge(S("m_out"), cm + 1)
                        if cm >= 2:
                            dve.wait_ge(S("m_sq"), cm - 1)
                            dve.wait_ge(S("m_yo"), cm - 1)
                        den = pb[:, bk, 256:389:132]
                        ch(dve.tensor_tensor(DN[:, 0:2], den, EM[:, m, h:8:4], ALU.max))
                        ch(dve.scalar_tensor_tensor(DN[:, 0:2], den, -1.0, DN[:, 0:2], ALU.mult, ALU.max))
                        ch(dve.reciprocal(DN[:, 2:4], DN[:, 0:2]))
                        ch(dve.tensor_scalar(hm, pb[:, bk, P:2 * P], DN[:, 2:3], None, ALU.mult))
                        dve.scalar_tensor_tensor(hm, pb[:, bk, 260:260 + P], DN[:, 3:4], hm, ALU.mult, ALU.add
                                                 ).then_inc(S("m_hs"), 1)
                    if 2 <= n < NT + 2:
                        cm = cn - 2
                        ms = MS[:, cm % 2, :]
                        dve.wait_ge(S("m_sq"), cm + 1)
                        if cm >= 2:
                            dve.wait_ge(S("m_rs"), cm - 1)
                        dve.tensor_scalar(ms[:, 1:2], ms[:, 0:1], 4.0 / DH, 4.0 * EPS, ALU.mult, ALU.add).then_inc(S("m_ms"), 1)
                    if n >= 3:
                        m, cm = n - 3, cn - 3
                        dve.wait_ge(S("m_yhi"), cm + 1)
                        cs = slice(P * m, P * m + P)
                        dve.tensor_tensor(yT[:, 2 + h, 1, cs], pb[:, 0, 0:P], yT[:, 2 + h, 0, cs],
                                          ALU.subtract).then_inc(S("m_ylo"), 1)
                    if h == NH - 1 and n >= 4:
                        wo_lo(n - 4)
                    if n < NT - 1:
                        if n >= 1:
                            dve.wait_ge(S("m_out"), cn)
                        state(i0 + 19 + n, CF[n % 2], CF[(n + 1) % 2], 0, n)
                    if 2 <= n < NT + 2:
                        m, cm = n - 2, cn - 2
                        dve.wait_ge(S("p_ev"), jo["p0"] + m + 1)
                        if m == 0:
                            dve.wait_ge(S("gb_in"), 16 * (h + 1))
                        ch(dve.scalar_tensor_tensor(OT, OT if h < NH - 1 else OS[:, m, :], 1.0, GB, ALU.add, ALU.mult))
                        dve.wait_ge(S("m_rs"), cm + 1)
                        if cm >= 1:
                            dve.wait_ge(S("m_yt"), cm)
                        dve.scalar_tensor_tensor(YO, HM[cm % 2], MS[:, cm % 2, 2:3], OT, ALU.mult, ALU.mult
                                                 ).then_inc(S("m_yo"), 1)
                split_lo(dve, jo["i"] + 2)
            wo_lo(NT - 1)
            def w1_lo(c, sl):
                dve.wait_ge(S("g_hi"), 2 * c + 1)
                dve.scalar_tensor_tensor(w1p[sl][:, :, 1, :], w1s, WS, w1p[sl][:, :, 0, :], ALU.mult, ALU.subtract
                                         ).then_inc(S("g_lo"), 1)

            def w2_lo(c, sl):
                dve.wait_ge(S("g_hi"), 2 * c + 2)
                dve.scalar_tensor_tensor(w2p[sl][:, :, 1, :], w2s, WS, w2p[sl][:, :, 0, :], ALU.mult, ALU.subtract
                                         ).then_inc(S("g_lo"), 1)

            dve.wait_ge(S("x1_in"), 16 * EARLY)
            for t in range(NT + 3):
                if t < NT:
                    dve.wait_ge(S("o_mm"), t + 1)
                    if t == EARLY:
                        dve.wait_ge(S("x1_rest_in"), 16 * (NT - EARLY))
                    xt = x1(t)
                    dve.scalar_tensor_tensor(xt, pb[:, 2 * (t % 2):2 * (t % 2) + 2, :].rearrange("p a b -> p (a b)"), 1 / WS,
                                             xt, ALU.mult, ALU.add).then_inc(S("o_x1"), 1)
                if 1 <= t <= NT:
                    u = t - 1
                    dve.wait_ge(S("h_sq"), N5 + u + 1)
                    dve.tensor_scalar(ssq2[:, u:u + 1], ssq2[:, u:u + 1], 1.0 / D, EPS, ALU.mult, ALU.add).then_inc(S("h_ms"), 1)
                    dve.wait_ge(S("h_rs"), N5 + u + 1)
                    if u >= 2:
                        dve.wait_ge(S("h_tr"), N5 + u - 1)
                    dve.tensor_scalar(xn2[u % 2], x1(u), rst2[:, u:u + 1], None, ALU.mult).then_inc(S("h_xn"), 1)
                if t == NT + 1:
                    w1_lo(0, 0)
                if t >= 3:
                    u = t - 3
                    dve.wait_ge(S("h_aff"), N5 + u + 1)
                    c = slice(P * u, P * u + P)
                    ch(dve.tensor_copy(hT2[:, :, 0, c], hf2[u % 2]))
                    dve.tensor_tensor(hT2[:, :, 1, c], hf2[u % 2], hT2[:, :, 0, c], ALU.subtract).then_inc(S("h_lo"), 1)
            for i in range(4):
                dve.memset(tiny[:], 0.0).then_inc(S("acc"), 1)
                dve.wait_ge(S("acc"), i + 1)
            for i in range(FT):
                dve.memset(tiny[:], 0.0).then_inc(S("a_lo"), 1)
                dve.wait_ge(S("a_lo"), i + 1)

            w2_lo(0, 0)

            def add_out(c, tb):
                dve.wait_ge(S("acc"), (c * 4 + tb) * 8 + 4)
                for o in range(8):
                    dve.wait_ge(S("g_mm2"), (c * 4 + tb) * 8 + o + 1)
                    xs = x1(4 * tb + o // 2)[:, BLK * (o % 2):BLK * (o % 2) + BLK]
                    dve.scalar_tensor_tensor(xs, pb[:, 4 + o % 4, :], 1.0 / (WS * AS), xs, ALU.mult, ALU.add
                                             ).then_inc(S("acc"), 1)

            def final_ms(tb):
                dve.wait_ge(S("h_sq"), N7 + 4 * tb + 4)
                c = slice(4 * tb, 4 * tb + 4)
                dve.tensor_scalar(ssq2[:, c], ssq2[:, c], 1.0 / D, EPS, ALU.mult, ALU.add).then_inc(S("h_ms"), 1)

            def final_out(tb):
                dve.wait_ge(S("h_rs"), N7 + tb + 1)
                if tb == 0:
                    dve.wait_ge(S("fg_in"), 16)
                for t in range(4 * tb, 4 * tb + 4):
                    if t >= 4:
                        dve.wait_ge(S(f"out_st{t % 4}"), 16 * (t // 4))
                    dve.scalar_tensor_tensor(outb[t % 4], x1(t), rst2[:, t:t + 1], fgbc, ALU.mult, ALU.mult
                                             ).then_inc(S("z_out"), 1)

            def dve_units(it, last=False):
                for i in range(8):
                    c, tb = 2 * it + i // 4, i % 4
                    for f in range(FT):
                        n = (c * 4 + tb) * FT + f
                        dve.wait_ge(S("a_sq"), n + 1)
                        dve.wait_ge(S("a_hi"), n + 1)
                        dve.tensor_tensor(act_p[tb % 2][:, f, 1, :], act_a[:, f, :], act_p[tb % 2][:, f, 0, :], ALU.subtract
                                          ).then_inc(S("a_lo"), 1)
                    if i >= 1:
                        add_out(2 * it + (i - 1) // 4, (i - 1) % 4)
                    if tb == 1 and not (last and i // 4 == 1):
                        w1_lo(c + 1, (i // 4 + 1) % 2)
                        w2_lo(c + 1, (i // 4 + 1) % 2)
                    if last and i >= 6:
                        final_ms(tb - 2)
                        final_out(tb - 2)
                add_out(2 * it + 1, 3)

            with dve.Fori(0, (NFC - NPEEL) // 2) as it:
                dve_units(it)
            dve_units((NFC - NPEEL) // 2, last=True)
            for tb in range(2, NB):
                final_ms(tb)
                final_out(tb)

        @block.tensor
        def _(pe):
            def ada_block(b):
                pe.wait_ge(S(f"ada_in{b % 2}"), 16 * (b // 2 + 1))
                if b >= 2:
                    pe.wait_ge(S("ada_ev"), b - 1)
                for k in range(KT):
                    mm = pe.matmul(pb[0:2, b % 2, :], scs.rearrange("p (k r) -> p k r", r=2)[:, k, :], ada_ring[b % 2][:, k, :],
                                   start=(k == 0), stop=(k == KT - 1))
                mm.then_inc(S("ada_mm"), 1)
            pe.wait_ge(S("filter_in"), 16 * 10)
            for lay in range(2):
                for b in range(NB):
                    u = NB * lay + b
                    if u >= 2:
                        pe.wait_ge(S("f_red"), u - 1)
                    if lay == 1:
                        pe.wait_ge(S("f_sin"), b + 1)
                    pe.matmul(pb[:, 4 + b % 2, :], (w1bd if lay == 0 else w2bd),
                              (featsT if lay == 0 else h1)[:, b * BLK:(b + 1) * BLK], start=True, stop=True
                              ).then_inc(S("f_mm"), 1)
                if lay == 0:
                    pe.wait_ge(S("ada_c"), 1)
                    ada_block(0)
                    ada_block(1)
            pe.wait_ge(S("f_sin"), 2 * NB)
            for n2 in range(FFT2):
                if n2 >= 2:
                    pe.wait_ge(S("f_raw"), n2 - 1)
                for q in range(2):
                    r = slice(64 * q, 64 * q + 64)
                    mm = pe.matmul(pb[r, 6 + n2 % 2, 0:HYW],
                                   h2[r, :].rearrange("p (a b) -> p b a", b=FFT2)[:, n2, :],
                                   w3s[r, :], start=True, stop=True)
                mm.then_inc(S("f_h3"), 1)
                if n2 % 2 == 1 and 1 + n2 // 2 < 12 and n2 >= 3:
                    ada_block(1 + n2 // 2)
            for n2 in range(FFT2):
                pe.wait_ge(S("f_filt"), n2 + 1)
                pe.wait_ge(S(f"F_in{(n2 // 4) % 2}"), 16 * (n2 // 8 + 1))
                if n2 >= 2:
                    pe.wait_ge(S("f_x1"), n2 - 1)
                pe.matmul(pb[:, 4 + n2 % 2, 0:HYW], Fring[(n2 // 4) % 2][:, n2 % 4, :], filt[:, :, n2],
                          start=True, stop=True).then_inc(S("f_s1"), 1)
            pe.wait_ge(S("f_x1"), FFT2)
            for q in range(16):
                if q >= 2:
                    pe.wait_ge(S("f_x1t"), q - 1)
                for i in range(4):
                    mm = pe.transpose(pb[:, 6 + q % 2, P * i:P * i + P],
                                      X1f[:, 4 * (4 * q + i):4 * (4 * q + i) + 4, :].rearrange("p c n -> p (c n)"), ident[:])
                mm.then_inc(S("f_tr"), 1)
            pe.wait_ge(S("f_x1t"), 16)
            for q in range(16):
                g8 = slice(8 * (q // 2), 8 * (q // 2) + 8)
                if q >= 2:
                    pe.wait_ge(S("f_spec"), q - 1)
                a, b = (0, 1) if q % 2 == 0 else (1, 0)
                pe.matmul(pb[:, 2 + q % 2, :], dft[:, 0, :], X1Tf[:, a, g8, :], start=True, stop=False)
                pe.matmul(pb[:, 2 + q % 2, :], dft[:, 1 + q % 2, :], X1Tf[:, b, g8, :], start=False, stop=True
                          ).then_inc(S("f_s2"), 1)
            pe.wait_ge(S("ada_ev"), 12)
            for i in range(32):
                row = [0, 1, 3, 4][i // 8]
                mm = pe.transpose(pb[:, 7, 2 * i:2 * i + 2], arow[0:2, row * D + P * (i % 8):row * D + P * (i % 8) + P],
                                  ident[0:2, 0:2])
            mm.then_inc(S("ada_tr"), 1)
            for t in range(NTC):
                pe.wait_ge(S("h_xn"), t + 1)
                if t >= 2:
                    pe.wait_ge(S("h_aff"), t - 1)
                    pe.wait_ge(S("h_aff_hi"), t - 1)
                for k in range(KT):
                    mm = pe.transpose(pb[:, 2 + 2 * (t % 2) + k // 4, P * (k % 4):P * (k % 4) + P],
                                      xnrm[t % 2][:, P * k:P * k + P], ident[:])
                mm.then_inc(S("h_tr"), 1)
                if t >= 8 and t % 2 == 0:
                    k = (t - 8) // 2
                    pe.wait_ge(S("h_lo"), 4 * (k // 2) + 4)
                    project(pe, JOBS[k % 2], [k // 2])
            pe.wait_ge(S("h_lo"), NTC)
            for k in range(5, 8):
                project(pe, JOBS[k % 2], [k // 2])
            for j in range(2):
                project(pe, JOBS[3 * j + 2], (0, 1))
                pe.wait_ge(S("u_ready"), j + 1)
                un = U.rearrange("p (a b) -> p b a", b=FFT2)
                for q in range(9):
                    if q < 8:
                        if q >= 2:
                            pe.wait_ge(S("hy_ut"), 8 * j + q - 1)
                        for i in range(4):
                            mm = pe.transpose(pb[0:64, 2 + q % 2, P * i:P * i + P], un[:, 4 * q + i, :], ident[:])
                        mm.then_inc(S("hy_utm"), 1)
                    if q >= 1:
                        v = q - 1
                        pe.wait_ge(S("hy_ut"), 8 * j + v + 1)
                        pe.wait_ge(S(f"Fh{v % 2}"), 16 * (4 * j + v // 2 + 1))
                        if v >= 2:
                            pe.wait_ge(S("hy_x1"), 8 * j + v - 1)
                        for i in range(4):
                            mm = pe.matmul(pb[:, 4 + v % 2, P * i:P * i + P], Fr2[v % 2][0:64, i, :], uT[0:64, 4 * v + i, :],
                                           start=True, stop=True)
                        mm.then_inc(S("hy_s1m"), 1)
                pe.wait_ge(S("hy_x1"), 8 * j + 8)
                for q in range(8):
                    if q >= 2:
                        pe.wait_ge(S("hy_tr"), 8 * j + q - 1)
                    for i in range(4):
                        g = 4 * q + i
                        mm = pe.transpose(pb[:, 2 + q % 2, P * i:P * i + P],
                                          X1[:, 4 * g:4 * g + 4, :].rearrange("p c n -> p (c n)"), ident[:])
                    mm.then_inc(S("hy_trm"), 1)
                pe.wait_ge(S("hy_tr"), 8 * j + 8)
                for q in range(8):
                    g8 = slice(8 * (q // 2), 8 * (q // 2) + 8)
                    if q >= 2:
                        pe.wait_ge(S("hy_s2e"), 8 * j + q - 1)
                    a, b = (0, 1) if q % 2 == 0 else (1, 0)
                    pe.matmul(pb[:, 4 + q % 2, :], dft[:, 0, :], X1T[:, a, g8, :], start=True, stop=False)
                    pe.matmul(pb[:, 4 + q % 2, :], dft[:, 1 + q % 2, :], X1T[:, b, g8, :], start=False, stop=True
                              ).then_inc(S("hy_s2m"), 1)
                project(pe, JOBS[3 * j + 2], (2, 3))
                for q in range(8):
                    pe.wait_ge(S("hy_y"), 4 * j + q // 2 + 1)
                    if q >= 2:
                        pe.wait_ge(S("hy_ze"), 8 * j + q - 1)
                    for i in range(4):
                        g = 4 * q + i
                        pe.matmul(pb[:, 2 + q % 2, P * i:P * i + P], Y3[:, g, 1:3, :].rearrange("p a k -> p (a k)"),
                                  dft[:, 0, :], start=True, stop=False)
                        mm = pe.matmul(pb[:, 2 + q % 2, P * i:P * i + P], Y3[:, g, 0:2, :].rearrange("p a k -> p (a k)"),
                                       dft[:, 1, :], start=False, stop=True)
                    mm.then_inc(S("hy_inva"), 1)
                pe.wait_ge(S("hy_ze"), 8 * j + 8)
                for q in range(8):
                    pe.wait_ge(S(f"Gh{q % 2}"), 16 * (4 * j + q // 2 + 1))
                    if q >= 2:
                        pe.wait_ge(S("hy_yt"), 8 * j + q - 1)
                    for i in range(4):
                        mm = pe.matmul(pb[0:64, 4 + q % 2, P * i:P * i + P], Gr[q % 2][:, i, :], Z[:, :, 4 * q + i],
                                       start=True, stop=True)
                    mm.then_inc(S("hy_invb"), 1)
                for q in range(4):
                    pe.wait_ge(S("hy_yt"), 8 * j + 2 * q + 2)
                    if q >= 2:
                        pe.wait_ge(S("hy_cv"), 4 * j + q - 1)
                    for i in range(8):
                        mm = pe.transpose(pb[:, 2 + q % 2, 64 * i:64 * i + 64], yt[0:64, 8 * q + i, :], ident[0:64, 0:64])
                    mm.then_inc(S("hy_trb"), 1)
                following = JOBS[3] if j == 0 else J["rgg0"]
                project(pe, following, (0, 1))
                norm_pe(pe, SQ, j)
                project(pe, following, (2, 3))
                if j == 0:
                    project(pe, JOBS[4])
            for j in range(2):
                if j == 0:
                    project(pe, J["rgx0"])
                project(pe, J["rgg1" if j == 0 else "gates"])
                pe.wait_ge(S("rgw_in"), 64)
                pe.wait_ge(S("rg_cv"), 2 * j + 2)
                for v in range(10 * j, 10 * j + 10):
                    d, x = (v // 5) % 2, v % 5
                    b = RORD[d][x]
                    n = BLK if b < NB else TC
                    if v >= 2:
                        pe.wait_ge(S("rg_ev"), v - 1)
                    for g in range(2):
                        mm = pe.matmul(pb[:, 2 + 2 * g + v % 2, 0:n], rgw[:, j, 2 * d + g, :], XR[:, rcols(b)],
                                       start=True, stop=True)
                    mm.then_inc(S("rg_mm"), 1)
                following = J["rgx1" if j == 0 else "k0"]
                project(pe, following, (0, 1))
                norm_pe(pe, GG[j], 2 + j)
                project(pe, following, range(2, NB + 1))
            pe.wait_ge(S("r_ar"), 1)
            for d in range(2):
                for h in range(NH):
                    mm = pe.matmul(pb[:, 6, NTC * (NH * d + h):NTC * (NH * d + h) + NTC],
                                   ident[0:64, 32 * d + h:32 * d + h + 1].broadcast_to([64, P]), AR[0:64, :],
                                   start=True, stop=True)
            mm.then_inc(S("r_bc"), 1)
            pe.wait_ge(S("r_rows"), 1)
            for n in range(NTC):
                if n >= 2:
                    pe.wait_ge(S("r_cc"), n - 1)
                pe.transpose(pb[:, 2 + n % 2, 0:P], CW[:, P * n:P * n + P], ident[:])
                pe.transpose(pb[:, 2 + n % 2, P:P + 64], LF[0:64, P * n:P * n + P], ident[0:64, 0:64]).then_inc(S("r_tr"), 1)
            for h in range(NH):
                jq, jk, jv, jo = (J[f"{nm}{h}"] for nm in "qkvo")
                if h:
                    project(pe, jk, range(1, NB + 1))
                project(pe, jq)
                project(pe, jv, (4, 3, 2))
                pe.wait_ge(S("m_silu"), 2 * h + 1)
                pe.wait_ge(S("r_cc"), NTC)
                i0 = ITS * h

                def ktr(it, n):
                    x = it - i0
                    if x == 0 and h:
                        pe.wait_ge(S("m_ylo"), NT * h)
                    if x >= 17 or (x == 0 and h):
                        pe.wait_ge(S("m_st"), it)
                    elif x >= 4:
                        pe.wait_ge(S("m_st"), it - 3)
                    pe.transpose(pb[:, kbank(it), 0:P], KX[:, P * n:P * n + P], ident[:]).then_inc(S("m_kt"), 1)

                def csum(it, n):
                    pe.wait_ge(S("m_kw"), it + 1)
                    pe.wait_ge(S("p_ev"), unit(jv, n // 4) + 1)
                    pe.matmul(pb[:, kbank(it), P:P + DH + 1], KW[it % 2], V1[:, n, :], start=True, stop=True).then_inc(S("m_cl"), 1)

                def heads(n):
                    cn = NT * h + n
                    c = slice(P * n, P * n + P)
                    if cn >= 1:
                        pe.wait_ge(S("m_S"), cn)
                    row = lambda r: ident[:, r:r + 1].broadcast_to([P, P])
                    for d in range(2):
                        pe.matmul(pb[:, 6 + cn % 2, P * d:P * d + P], row(32 * d + h), R1[:, c], start=True, stop=False)
                        pe.matmul(pb[:, 6 + cn % 2, P * d:P * d + P], identb[:], maskneg[:, d, :], start=False, stop=True)
                    for d in range(2):
                        pe.matmul(pb[:, 6 + cn % 2, P * (2 + d):P * (3 + d)], row(64 + 32 * d + h), R1[:, c],
                                  start=True, stop=True)
                    pe.matmul(pb[:, 3, 0:P], KX[:, c], QT[:, c], start=True, stop=True).then_inc(S("m_A"), 1)

                seq = BWD[0:17] + FWD[0:17]
                ktr(i0, seq[0])
                for x in range(19):
                    if x + 1 < 17:
                        ktr(i0 + x + 1, seq[x + 1])
                    csum(i0 + x, seq[x])
                    if x in (5, 9):
                        project(pe, jv, [1 if x == 5 else 0])
                    if h == NH - 1 and 10 <= x < 17:
                        project(pe, jo, range(2 * (x - 10), 2 * (x - 10) + 2 if x < 15 else NT if x == 15 else 0))
                    if x == 16:
                        pe.wait_ge(S("m_silu"), 2 * h + 2)
                        pe.wait_ge(S("m_st"), i0 + 14)
                        heads(0)
                    if x + 1 >= 17:
                        ktr(i0 + x + 1, seq[x + 1])

                def ytr(m):
                    cm = NT * h + m
                    pe.wait_ge(S("m_yo"), cm + 1)
                    if cm >= 1:
                        pe.wait_ge(S("m_ylo"), cm)
                    pe.transpose(pb[:, 0, 0:P], YO, ident[:]).then_inc(S("m_yt"), 1)

                for n in range(NT + 2):
                    cn = NT * h + n
                    if n < NT - 1:
                        heads(n + 1)
                        csum(i0 + 19 + n, n)
                    if n < NT:
                        pe.wait_ge(S("m_S"), cn + 1)
                        pe.wait_ge(S("m_st"), i0 + 19 + n)
                        if cn >= 2:
                            pe.wait_ge(S("m_hs"), cn - 1)
                        for d in range(2):
                            o = pb[:, 4 + cn % 2, P + 132 * d:P + 132 * d + DH + 1]
                            pe.matmul(o, S2[cn % 2][d], V1[:, n, :], start=True, stop=False)
                            mm = pe.matmul(o, QW[cn % 2][d], CF[(n + 1) % 2] if d == 0 else CB[:, n, :], start=False, stop=True)
                        mm.then_inc(S("m_out"), 1)
                    if 1 <= n <= NT and h < NH - 1:
                        project(pe, jo, [n - 1])
                    if n < NT - 2:
                        ktr(i0 + 20 + n, n + 1)
                    if n >= 2:
                        ytr(n - 2)
                    if n == NT and h < NH - 1:
                        project(pe, J[f"k{h + 1}"], [0])
            pe.wait_ge(S("wo_lo"), 2 * KT)
            pe.wait_ge(S("m_ylo"), NT * NH)
            for t in range(NT + 2):
                if t < NT:
                    if t >= 2:
                        pe.wait_ge(S("o_x1"), t - 1)
                    for dh in range(2):
                        for k in range(KT):
                            for m, (ys, ws) in enumerate(((0, 0), (0, 1), (1, 0))):
                                mm = pe.matmul(pb[:, 2 * (t % 2) + dh, :], yT[:, k, ys, P * t:P * t + P],
                                               wop[:, k, ws, BLK * dh:BLK * dh + BLK],
                                               start=(k == 0 and m == 0), stop=(k == KT - 1 and m == 2))
                    mm.then_inc(S("o_mm"), 1)
                if t >= 2:
                    u = t - 2
                    pe.wait_ge(S("h_xn"), N5 + u + 1)
                    if u >= 2:
                        pe.wait_ge(S("h_aff"), N5 + u - 1)
                    for k in range(KT):
                        mm = pe.transpose(pb[:, 4 + 2 * (u % 2) + k // 4, P * (k % 4):P * (k % 4) + P],
                                          xn2[u % 2][:, P * k:P * k + P], ident[:])
                    mm.then_inc(S("h_tr"), 1)

            def up(c, tb, sl):
                if tb == 0:
                    pe.wait_ge(S("g_lo"), 2 * c + 1)
                pe.wait_ge(S("h_lo"), N5 + 4 * tb + 4)
                for f in range(FT):
                    for k in range(KT):
                        for m, (ws, hs) in enumerate(((0, 0), (0, 1), (1, 0))):
                            mm = pe.matmul(pb[:, 2 * (tb % 2) + f, :], w1p[sl][:, k, ws, P * f:P * f + P],
                                           hT2[:, k, hs, BLK * tb:BLK * tb + BLK],
                                           start=(k == 0 and m == 0), stop=(k == KT - 1 and m == 2))
                    mm.then_inc(S("g_mm1"), 1)

            def down(c, tb, sl):
                pe.wait_ge(S("a_lo"), ((c * 4 + tb) + 1) * FT + FT)
                if tb == 0:
                    pe.wait_ge(S("g_lo"), 2 * c + 2)
                for o in range(8):
                    tt, dh = o // 2, o % 2
                    pe.wait_ge(S("acc"), (c * 4 + tb) * 8 + o + 1)
                    for f in range(FT):
                        for m, (hs, ws) in enumerate(((0, 0), (0, 1), (1, 0))):
                            mm = pe.matmul(pb[:, 4 + o % 4, :], act_p[tb % 2][:, f, hs, P * tt:P * tt + P],
                                           w2p[sl][:, f, ws, BLK * dh:BLK * dh + BLK],
                                           start=(f == 0 and m == 0), stop=(f == FT - 1 and m == 2))
                    mm.then_inc(S("g_mm2"), 1)

            def pe_units(it):
                for i in range(8):
                    up(2 * it + i // 4, i % 4, i // 4)
                    if i >= 1:
                        down(2 * it + (i - 1) // 4, (i - 1) % 4, (i - 1) // 4)
                down(2 * it + 1, 3, 1)

            with pe.Fori(0, (NFC - NPEEL) // 2) as it:
                pe_units(it)
            pe_units((NFC - NPEEL) // 2)


def host_data(inp):
    f = lambda a: np.ascontiguousarray(np.asarray(a))
    z = lambda *sh: np.zeros(sh, np.float32)
    pk = z(P, NCOL)

    def put(name, a):
        at, n = COLS[name]
        pk[:, at:at + n] = a

    byp = lambda a: f(a).reshape(-1, P).T
    put("cc", np.stack([byp(inp["c"][0]), byp(inp["c_ctx"])], axis=2).reshape(P, 16))
    put("n1g", byp(inp["norm1_g"][0]))
    put("n2g", byp(inp["norm2_g"][0]))
    ab = f(inp["ada_b"][0]).reshape(6, D)
    put("adab", byp(ab[[0, 1, 3, 4]].reshape(-1)))
    hc = f(inp["hy_conv"][0])
    put("hyc", hc.reshape(3, 6, P).transpose(2, 1, 0).reshape(P, 18))
    put("hyb", byp(inp["hy_bias"][0]))
    put("mlc", f(inp["ml_conv"][0]).reshape(4, 8, P).transpose(2, 1, 0).reshape(P, 32))
    put("rgc", f(inp["rg_conv"][0]).reshape(4, 2, P).transpose(2, 1, 0).reshape(P, 8))
    put("rgb", f(inp["rg_gate_b"][0]).reshape(4, 2, P).transpose(2, 1, 0).reshape(P, 8))
    put("rgl", f(inp["rg_lambda"][0]).reshape(2, 2, P).transpose(2, 1, 0).reshape(P, 4))
    mg = f(inp["mix_norm_g"][0])
    put("gcm", byp(np.concatenate([mg[:HYW], mg[HYW + MLW:]])))
    two = lambda a: np.concatenate([f(a), f(a)])
    put("ffn", np.stack([two(inp["hy_b1"][0]), two(inp["hy_freq"][0, 0]), two(inp["hy_b2"][0]),
                         two(inp["hy_freq"][0, 1])], axis=1))
    gb = f(inp["ml_gate_b"][0]).reshape(4, NH)
    g2 = z(P, 1)
    g2[0:4, 0], g2[32:36, 0], g2[64:68, 0], g2[96:100, 0] = gb[0], gb[2], gb[1], gb[3]
    put("gb", g2)
    n1, n2 = np.arange(64)[:, None], np.arange(FFT2)[None]
    tf = FFT2 * n1 + n2
    tb = L - FFT2 * n1 - n2
    put("negt", -(np.concatenate([tf, tb], axis=0) / (L - 1)).astype(np.float32))
    out = {"cols": pk, "ident": np.eye(P, dtype=np.float32)}
    bands = 16
    pos = np.arange(L, dtype=np.float32)
    t = (pos / np.float32(L - 1)).astype(np.float32)
    fr = np.linspace(1e-4, bands - 1, bands, dtype=np.float32)
    ang = (np.float32(2.0 * math.pi / L) * fr[None] * pos[:, None]).astype(np.float32)
    feats = np.concatenate([t[:, None], np.cos(ang), -np.sin(ang)], axis=-1).astype(np.float32)
    ft = z(P, L)
    ft[0:33] = feats.T
    ft[64:97, 1:] = feats[:0:-1].T
    out["feats"] = ft
    mx, mn = math.log(1e-2) / 0.3, math.log(1e-2) / 1.5
    out["absdelta"] = np.abs(np.linspace(mn, mx, HYW, dtype=np.float32))[None]
    n1 = np.arange(FFT1)[:, None, None]
    n2 = np.arange(FFT2)[None, :, None]
    k1 = np.arange(64)[None, None, :]
    th = 2 * np.pi * (k1 + 0.5) * (FFT2 * n1 + n2) / (FFT1 * FFT2)
    Fm = np.concatenate([np.cos(th), -np.sin(th)], axis=2)
    Fm[64:] *= -1
    Fm[64, 0] = 0
    out["Fm"] = Fm.astype(np.float32)
    thi = th[:64].transpose(2, 1, 0)
    sc = 2.0 / (FFT1 * FFT2)
    out["Gm"] = (np.concatenate([np.cos(thi), -np.sin(thi)], axis=0) * sc).astype(np.float32)
    a = np.arange(FFT2)
    w = 2 * np.pi * a[:, None] * a[None] / FFT2
    bd = lambda m: np.kron(np.eye(4), m)
    out["dft"] = np.stack([bd(np.cos(w)), bd(np.sin(w)), bd(-np.sin(w))], axis=1).astype(np.float32)
    out["gones"] = np.kron(np.eye(2), np.ones((64, 64))).astype(np.float32)
    si, ti = np.arange(P)[:, None], np.arange(P)[None]
    out["maskneg"] = np.stack([np.where(si <= ti, 0, NEG), np.where(si >= ti, 0, NEG)], axis=1).astype(np.float32)
    for name in ("hy_w1", "hy_w2", "hy_w3", "ada_w", "w_in", "w_out", "mlp_w1", "mlp_w2"):
        out[name] = f(inp[name][0])
    out["hy_b3"] = f(inp["hy_b3"])
    out["x"] = f(inp["x"][0])
    out["rgw"] = f(inp["rg_gate_w"][0]).reshape(4, 4, 64, 64)
    out["gml"] = mg[None, HYW:HYW + MLW].copy()
    out["final_g"] = f(inp["final_g"])[None]
    out["adab25"] = ab[[2, 5]][None].copy()
    out["ctx"] = f(inp["ctx"][0])
    return out


def kernel(**inputs):
    import concourse.bacc as _bacc
    from concourse.bass_utils import run_bass_kernel_spmd as _run

    nc = _bacc.Bacc("TRN2", target_bir_lowering=False, num_devices=1)
    arrays = host_data(inputs)
    dr = {k: nc.dram_tensor("in_" + k, a.shape, mybir.dt.from_np(a.dtype), kind="ExternalInput").ap()
          for k, a in arrays.items()}
    dr["out"] = nc.dram_tensor("out_0", (L, D), F32, kind="ExternalOutput").ap()
    dr["mod25"] = nc.dram_tensor("mod25", (2, D), F32, kind="Internal").ap()
    program(nc, dr)
    r = _run(nc, [{"in_" + k: a for k, a in arrays.items()}], core_ids=[0])
    return r.results[0]["out_0"].reshape(1, L, D)
```
